# Optimizing a Trainium2 kernel written in Bass

```python
import jax, jax.numpy as jnp
from jax import lax
import numpy as np
import math

D_MODEL = 1024
BATCH = 1
SEQ = 256
DEPTH = 2

N_A = DEPTH // 2
N_B = DEPTH - N_A
HEAD_DIM = 64
MIX_WIDTH = D_MODEL
MEM_LEN = 256
MEM_HEADS = 4
MEM_WIDTH = MEM_HEADS * HEAD_DIM
MAIN_WIDTH = MIX_WIDTH - MEM_WIDTH
POOL_WINDOWS = (2, 4, 8, 16)
POOL_GROUPS = len(POOL_WINDOWS)
POOL_GROUP_DIM = MAIN_WIDTH // POOL_GROUPS
SWA_Q_HEADS = MAIN_WIDTH // HEAD_DIM
SWA_KV_HEADS = 4
SWA_GROUP = SWA_Q_HEADS // SWA_KV_HEADS
KV_WIDTH = 2 * SWA_KV_HEADS * HEAD_DIM
MEM_KV_WIDTH = 2 * MEM_WIDTH
WINDOW = 128
BLOCK = 128
D_FF = 4 * D_MODEL
EPS = 1e-6


def rmsnorm(x, g):
    xf = x.astype(jnp.float32)
    y = xf * lax.rsqrt(jnp.mean(xf * xf, axis=-1, keepdims=True) + EPS)
    return (y * g.astype(jnp.float32)).astype(x.dtype)

def alibi_slopes(n):
    return jnp.exp2(-8.0 * jnp.arange(1, n + 1, dtype=jnp.float32) / n)

def pool_mixer(u, pool_w, pool_scale):
    B, S, _ = u.shape
    uf = u.astype(jnp.float32).reshape(B, S, POOL_GROUPS, POOL_GROUP_DIM)
    csum = jnp.concatenate([jnp.zeros((B, 1, POOL_GROUPS, POOL_GROUP_DIM), jnp.float32),
                            jnp.cumsum(uf, axis=1)], axis=1)
    win = jnp.array(POOL_WINDOWS, jnp.int32)
    t = jnp.arange(S, dtype=jnp.int32)[:, None]
    lo = jnp.maximum(t + 1 - win[None, :], 0)
    cnt = jnp.minimum(t + 1, win[None, :]).astype(jnp.float32)
    window_sum = csum[:, 1:] - csum[:, lo, jnp.arange(POOL_GROUPS)[None, :]]
    d = (window_sum / cnt[None, :, :, None] - uf).astype(u.dtype)
    mixed = jnp.einsum('bsgc,gcd->bsgd', d, pool_w)
    return mixed.reshape(B, S, MAIN_WIDTH) * pool_scale

def swa_sink_attention(q, k, v, sinks):
    B, S = q.shape[0], q.shape[1]
    nb = S // BLOCK
    qb = q.reshape(B, nb, BLOCK, SWA_KV_HEADS, SWA_GROUP, HEAD_DIM)

    def with_prev(a):
        ab = a.reshape(B, nb, BLOCK, SWA_KV_HEADS, HEAD_DIM)
        prev = jnp.pad(ab[:, :-1], ((0, 0), (1, 0), (0, 0), (0, 0), (0, 0)))
        return jnp.concatenate([prev, ab], axis=2)

    kb, vb = with_prev(k), with_prev(v)
    s = jnp.einsum('bnqkgd,bnpkd->bnkgqp', qb, kb).astype(jnp.float32) * (HEAD_DIM ** -0.5)
    blk = jnp.arange(nb, dtype=jnp.int32)[:, None] * BLOCK
    qpos = blk + jnp.arange(BLOCK, dtype=jnp.int32)[None, :]
    kpos = blk - BLOCK + jnp.arange(2 * BLOCK, dtype=jnp.int32)[None, :]
    dist = qpos[:, :, None] - kpos[:, None, :]
    valid = (dist >= 0) & (dist < WINDOW) & (kpos[:, None, :] >= 0)
    slopes = alibi_slopes(SWA_Q_HEADS).reshape(SWA_KV_HEADS, SWA_GROUP)
    s = s - slopes[None, None, :, :, None, None] * dist.astype(jnp.float32)[None, :, None, None]
    s = jnp.where(valid[None, :, None, None], s, jnp.finfo(jnp.float32).min)
    sink = sinks.astype(jnp.float32).reshape(SWA_KV_HEADS, SWA_GROUP)[None, None, :, :, None, None]
    m = jnp.maximum(jnp.max(s, axis=-1, keepdims=True), sink)
    e = jnp.exp(s - m)
    p = e / (jnp.sum(e, axis=-1, keepdims=True) + jnp.exp(sink - m))
    o = jnp.einsum('bnkgqp,bnpkd->bnqkgd', p.astype(vb.dtype), vb)
    return o.reshape(B, S, SWA_Q_HEADS * HEAD_DIM)

def memory_attention(q, mk, mv):
    s = jnp.einsum('bshd,bmhd->bhsm', q, mk).astype(jnp.float32) * (HEAD_DIM ** -0.5)
    p = jax.nn.softmax(s, axis=-1)
    o = jnp.einsum('bhsm,bmhd->bshd', p.astype(mv.dtype), mv)
    return o.reshape(q.shape[0], q.shape[1], MEM_WIDTH)

def sq_relu_mlp(x, w_up, w_down):
    h = jax.nn.relu(x @ w_up)
    return (h * h) @ w_down

def first_inputs(seed: int = 0) -> dict:
    key = jax.random.key(seed)
    ks = jax.random.split(key, 20)
    f32 = jnp.float32

    def nrm(k, shape, scale):
        return jax.random.normal(k, shape, f32) * scale

    def gain(k, shape):
        return 1.0 + 0.02 * jax.random.normal(k, shape, f32)

    return {
        "x": nrm(ks[0], (BATCH, SEQ, D_MODEL), 1.0),
        "mem": nrm(ks[1], (BATCH, MEM_LEN, D_MODEL), 1.0),
        "norm_mix": gain(ks[2], (DEPTH, D_MODEL)),
        "w_in": nrm(ks[3], (DEPTH, D_MODEL, MIX_WIDTH), D_MODEL ** -0.5),
        "pool_w": nrm(ks[4], (N_A, POOL_GROUPS, POOL_GROUP_DIM, POOL_GROUP_DIM), POOL_GROUP_DIM ** -0.5),
        "pool_scale": gain(ks[5], (N_A, MAIN_WIDTH)),
        "kv_norm": gain(ks[6], (D_MODEL,)),
        "w_kv": nrm(ks[7], (D_MODEL, KV_WIDTH), D_MODEL ** -0.5),
        "k_norm": gain(ks[8], (HEAD_DIM,)),
        "q_norm": gain(ks[9], (N_B, HEAD_DIM)),
        "sinks": nrm(ks[10], (N_B, SWA_Q_HEADS), 0.5),
        "mem_norm": gain(ks[11], (DEPTH, D_MODEL)),
        "w_mem_kv": nrm(ks[12], (DEPTH, D_MODEL, MEM_KV_WIDTH), D_MODEL ** -0.5),
        "mem_q_norm": gain(ks[13], (DEPTH, HEAD_DIM)),
        "mem_k_norm": gain(ks[14], (DEPTH, HEAD_DIM)),
        "w_out": nrm(ks[15], (DEPTH, MIX_WIDTH, D_MODEL), MIX_WIDTH ** -0.5),
        "norm_mlp": gain(ks[16], (DEPTH, D_MODEL)),
        "w_up": nrm(ks[17], (DEPTH, D_MODEL, D_FF), D_MODEL ** -0.5),
        "w_down": nrm(ks[18], (DEPTH, D_FF, D_MODEL), D_FF ** -0.5),
    }

def first_block(x, mem, norm_mix, w_in, pool_w, pool_scale, kv_norm, w_kv, k_norm, q_norm, sinks,
              mem_norm, w_mem_kv, mem_q_norm, mem_k_norm, w_out, norm_mlp, w_up, w_down):
    B, S, _ = x.shape
    h = x
    k_shared = None
    v_shared = None
    for l in range(DEPTH):
        if l == N_A:
            kv = rmsnorm(h, kv_norm) @ w_kv
            k_shared = rmsnorm(kv[..., :KV_WIDTH // 2].reshape(B, S, SWA_KV_HEADS, HEAD_DIM), k_norm)
            v_shared = kv[..., KV_WIDTH // 2:].reshape(B, S, SWA_KV_HEADS, HEAD_DIM)

        proj = rmsnorm(h, norm_mix[l]) @ w_in[l]
        main, mq = proj[..., :MAIN_WIDTH], proj[..., MAIN_WIDTH:]
        if l < N_A:
            main_out = pool_mixer(main, pool_w[l], pool_scale[l])
        else:
            j = l - N_A
            q = rmsnorm(main.reshape(B, S, SWA_Q_HEADS, HEAD_DIM), q_norm[j])
            main_out = swa_sink_attention(q, k_shared, v_shared, sinks[j])

        mkv = rmsnorm(mem, mem_norm[l]) @ w_mem_kv[l]
        mk = rmsnorm(mkv[..., :MEM_WIDTH].reshape(B, MEM_LEN, MEM_HEADS, HEAD_DIM), mem_k_norm[l])
        mv = mkv[..., MEM_WIDTH:].reshape(B, MEM_LEN, MEM_HEADS, HEAD_DIM)
        mqh = rmsnorm(mq.reshape(B, S, MEM_HEADS, HEAD_DIM), mem_q_norm[l])
        mem_out = memory_attention(mqh, mk, mv)

        h = h + jnp.concatenate([main_out, mem_out], axis=-1) @ w_out[l]
        h = h + sq_relu_mlp(rmsnorm(h, norm_mlp[l]), w_up[l], w_down[l])
    return h


DEPTH_2 = 1

HG_HEADS = 8
HG_DK = 128
HG_DV = 128
HG_WIDTH = HG_HEADS * HG_DK
HG_CHUNK = 64
AT_HEADS = 8
AT_DH = 128
AT_WIDTH = AT_HEADS * AT_DH
MOBA_BLOCK = 256
MOBA_TOPK = 3
Q_CHUNK = 16
REL_BUCKETS = 32
REL_MAX_DIST = 128
D_FF_2 = -(-8 * D_MODEL // (3 * 256)) * 256
N_BRANCH = 2
NORM_EPS = 1e-6
IN_SIZES = [HG_WIDTH, HG_WIDTH, HG_HEADS * HG_DV, HG_HEADS * HG_DV,
            AT_WIDTH, AT_WIDTH, AT_WIDTH, N_BRANCH * D_MODEL]
IN_COLS = sum(IN_SIZES)
IN_SPLITS = [int(s) for s in np.cumsum(IN_SIZES)[:-1]]


def rmsnorm_2(x, g):
    xf = x.astype(jnp.float32)
    y = xf * lax.rsqrt(jnp.mean(xf * xf, axis=-1, keepdims=True) + NORM_EPS)
    return (y * g.astype(jnp.float32)).astype(x.dtype)

def t5_bucket(dist):
    n = jnp.maximum(dist, 0)
    max_exact = REL_BUCKETS // 2
    nf = jnp.maximum(n, 1).astype(jnp.float32)
    large = max_exact + (jnp.log(nf / max_exact) / math.log(REL_MAX_DIST / max_exact)
                         * (REL_BUCKETS - max_exact)).astype(jnp.int32)
    large = jnp.minimum(large, REL_BUCKETS - 1)
    return jnp.where(n < max_exact, n, large)

def hgrn2_mix(q, f_logit, i, g, lb, out_gain):
    B, S, _ = q.shape
    f32 = jnp.float32
    C = HG_CHUNK
    N = S // C
    z = f_logit.astype(f32)
    f = lb + (1.0 - lb) * jax.nn.sigmoid(z)
    log_f = jnp.log(f)
    k = (1.0 - lb) * jax.nn.sigmoid(-z)
    qs = q.astype(f32) * HG_DK ** -0.5

    def to_chunks(t, d):
        return t.reshape(B, N, C, HG_HEADS, d).transpose(1, 0, 3, 2, 4)

    qc = to_chunks(qs, HG_DK)
    kc = to_chunks(k, HG_DK)
    lfc = to_chunks(log_f, HG_DK)
    vc = to_chunks(i.astype(f32), HG_DV)
    causal = jnp.tril(jnp.ones((C, C), dtype=bool))

    def step(state, inp):
        q_, k_, v_, lf_ = inp
        b = jnp.cumsum(lf_, axis=2)
        o_inter = jnp.einsum('bhtk,bhkv->bhtv', q_ * jnp.exp(b), state)
        diff = b[:, :, :, None, :] - b[:, :, None, :, :]
        decay = jnp.exp(jnp.where(causal[:, :, None], diff, -jnp.inf))
        attn = jnp.einsum('bhtk,bhsk,bhtsk->bhts', q_, k_, decay)
        o = o_inter + jnp.einsum('bhts,bhsv->bhtv', attn, v_)
        b_last = b[:, :, -1:, :]
        k_dec = k_ * jnp.exp(b_last - b)
        new_state = (jnp.exp(b_last[:, :, 0, :])[..., None] * state
                     + jnp.einsum('bhsk,bhsv->bhkv', k_dec, v_))
        return new_state, o

    s0 = jnp.zeros((B, HG_HEADS, HG_DK, HG_DV), f32)
    _, o = lax.scan(step, s0, (qc, kc, vc, lfc))
    o = o.transpose(1, 0, 3, 2, 4).reshape(B, S, HG_HEADS, HG_DV)
    o = rmsnorm_2(o, out_gain) * jax.nn.silu(g.astype(f32).reshape(B, S, HG_HEADS, HG_DV))
    return o.reshape(B, S, HG_HEADS * HG_DV).astype(q.dtype)

def moba_attention(q, k, v, rel_table):
    B, H, S, Dh = q.shape
    f32 = jnp.float32
    BLK = MOBA_BLOCK
    NB = -(-S // BLK)
    pad = NB * BLK - S
    kp = jnp.pad(k, ((0, 0), (0, 0), (0, pad), (0, 0)))
    vp = jnp.pad(v, ((0, 0), (0, 0), (0, pad), (0, 0)))
    kb = kp.reshape(B, H, NB, BLK, Dh)
    vb = vp.reshape(B, H, NB, BLK, Dh)
    kmean = jnp.mean(kb.astype(f32), axis=3)
    topk = min(MOBA_TOPK, NB)
    scale = Dh ** -0.5
    table_h = rel_table.astype(f32).T
    b_idx = jnp.arange(B)[:, None, None, None]
    h_idx = jnp.arange(H)[None, :, None, None]
    h_idx5 = jnp.arange(H)[None, :, None, None, None]
    n_chunks = S // Q_CHUNK

    def one_chunk(c):
        t0 = c * Q_CHUNK
        qc = lax.dynamic_slice_in_dim(q, t0, Q_CHUNK, axis=2)
        tpos = t0 + jnp.arange(Q_CHUNK)
        cur = t0 // BLK
        gate = jnp.einsum('bhqd,bhnd->bhqn', qc.astype(f32), kmean)
        gate = jnp.where(jnp.arange(NB) < cur, gate, -jnp.inf)
        _, sel = lax.top_k(gate, topk)
        sel_valid = sel < cur
        ks = kb[b_idx, h_idx, sel]
        vs = vb[b_idx, h_idx, sel]
        lp = jnp.einsum('bhqd,bhqjsd->bhqjs', qc, ks).astype(f32) * scale
        kpos = sel[..., None] * BLK + jnp.arange(BLK)
        bias_p = table_h[h_idx5, t5_bucket(tpos[:, None, None] - kpos)]
        lp = jnp.where(sel_valid[..., None], lp + bias_p, -jnp.inf)
        ko = lax.dynamic_slice_in_dim(kp, cur * BLK, BLK, axis=2)
        vo = lax.dynamic_slice_in_dim(vp, cur * BLK, BLK, axis=2)
        lo = jnp.einsum('bhqd,bhsd->bhqs', qc, ko).astype(f32) * scale
        dist_o = tpos[:, None] - (cur * BLK + jnp.arange(BLK))[None, :]
        lo = jnp.where(dist_o >= 0, lo + table_h[:, t5_bucket(dist_o)], -jnp.inf)
        logits = jnp.concatenate([lo, lp.reshape(B, H, Q_CHUNK, topk * BLK)], axis=-1)
        p = jax.nn.softmax(logits, axis=-1)
        p_own = p[..., :BLK].astype(v.dtype)
        p_past = p[..., BLK:].reshape(B, H, Q_CHUNK, topk, BLK).astype(v.dtype)
        return (jnp.einsum('bhqs,bhsd->bhqd', p_own, vo)
                + jnp.einsum('bhqjs,bhqjsd->bhqd', p_past, vs))

    out = lax.map(one_chunk, jnp.arange(n_chunks))
    return out.transpose(1, 2, 0, 3, 4).reshape(B, H, S, Dh)

def second_inputs(seed: int = 0) -> dict:
    key = jax.random.key(seed)
    ks = jax.random.split(key, 16)
    f32 = jnp.float32
    nrm = lambda k, shape, s: jax.random.normal(k, shape, f32) * s
    return {
        "x": jax.random.normal(ks[0], (BATCH, SEQ, D_MODEL), f32),
        "attn_norm_g": 1.0 + nrm(ks[1], (DEPTH_2, D_MODEL), 0.02),
        "w_in": nrm(ks[2], (DEPTH_2, D_MODEL, IN_COLS), D_MODEL ** -0.5),
        "hg_lb_gamma": nrm(ks[3], (DEPTH_2 + 1, HG_WIDTH), 0.5),
        "hg_out_norm_g": 1.0 + nrm(ks[4], (DEPTH_2, HG_DV), 0.02),
        "q_norm_g": 1.0 + nrm(ks[5], (DEPTH_2, AT_DH), 0.02),
        "k_norm_g": 1.0 + nrm(ks[6], (DEPTH_2, AT_DH), 0.02),
        "rel_bias_table": nrm(ks[7], (REL_BUCKETS, AT_HEADS), 0.2),
        "w_branch_hg": nrm(ks[8], (DEPTH_2, HG_HEADS * HG_DV, D_MODEL), (HG_HEADS * HG_DV) ** -0.5),
        "w_branch_attn": nrm(ks[9], (DEPTH_2, AT_WIDTH, D_MODEL), AT_WIDTH ** -0.5),
        "w_out": nrm(ks[10], (DEPTH_2, D_MODEL, D_MODEL), D_MODEL ** -0.5),
        "ffn_norm_g": 1.0 + nrm(ks[11], (DEPTH_2, D_MODEL), 0.02),
        "w_ffn_gate": nrm(ks[12], (DEPTH_2, D_MODEL, D_FF_2), D_MODEL ** -0.5),
        "w_ffn_up": nrm(ks[13], (DEPTH_2, D_MODEL, D_FF_2), D_MODEL ** -0.5),
        "w_ffn_down": nrm(ks[14], (DEPTH_2, D_FF_2, D_MODEL), D_FF_2 ** -0.5),
    }

def second_block(x, attn_norm_g, w_in, hg_lb_gamma, hg_out_norm_g, q_norm_g, k_norm_g,
              rel_bias_table, w_branch_hg, w_branch_attn, w_out, ffn_norm_g,
              w_ffn_gate, w_ffn_up, w_ffn_down):
    B, S, D = x.shape
    lb_all = jnp.cumsum(jax.nn.softmax(hg_lb_gamma.astype(jnp.float32), axis=0), axis=0)[:DEPTH_2]
    for l in range(DEPTH_2):
        h = rmsnorm_2(x, attn_norm_g[l])
        proj = h @ w_in[l]
        hq, hf, hi, hg, aq, ak, av, gl = jnp.split(proj, IN_SPLITS, axis=-1)
        y_hg = hgrn2_mix(hq, hf, hi, hg, lb_all[l], hg_out_norm_g[l]) @ w_branch_hg[l]
        qh = rmsnorm_2(aq.reshape(B, S, AT_HEADS, AT_DH), q_norm_g[l]).transpose(0, 2, 1, 3)
        kh = rmsnorm_2(ak.reshape(B, S, AT_HEADS, AT_DH), k_norm_g[l]).transpose(0, 2, 1, 3)
        vh = av.reshape(B, S, AT_HEADS, AT_DH).transpose(0, 2, 1, 3)
        att = moba_attention(qh, kh, vh, rel_bias_table)
        y_at = att.transpose(0, 2, 1, 3).reshape(B, S, AT_WIDTH) @ w_branch_attn[l]
        gates = jax.nn.sigmoid(gl.reshape(B, S, N_BRANCH, D))
        merged = gates[:, :, 0, :] * y_hg + gates[:, :, 1, :] * y_at
        x = x + merged @ w_out[l]
        h2 = rmsnorm_2(x, ffn_norm_g[l])
        x = x + (jax.nn.silu(h2 @ w_ffn_gate[l]) * (h2 @ w_ffn_up[l])) @ w_ffn_down[l]
    return x


def setup_inputs(seed=0):
    out = dict(first_inputs(seed))
    for name, value in second_inputs(seed + 1).items():
        if name != "x":
            out[name + "_2"] = value
    return out


def reference(
    x, mem, norm_mix, w_in, pool_w, pool_scale, kv_norm, w_kv, k_norm, q_norm, sinks, mem_norm,
    w_mem_kv, mem_q_norm, mem_k_norm, w_out, norm_mlp, w_up, w_down, attn_norm_g_2, w_in_2,
    hg_lb_gamma_2, hg_out_norm_g_2, q_norm_g_2, k_norm_g_2, rel_bias_table_2, w_branch_hg_2,
    w_branch_attn_2, w_out_2, ffn_norm_g_2, w_ffn_gate_2, w_ffn_up_2, w_ffn_down_2,
):
    x = first_block(
        x, mem, norm_mix, w_in, pool_w, pool_scale, kv_norm, w_kv, k_norm, q_norm, sinks,
        mem_norm, w_mem_kv, mem_q_norm, mem_k_norm, w_out, norm_mlp, w_up, w_down,
    )
    return second_block(
        x, attn_norm_g_2, w_in_2, hg_lb_gamma_2, hg_out_norm_g_2, q_norm_g_2, k_norm_g_2,
        rel_bias_table_2, w_branch_hg_2, w_branch_attn_2, w_out_2, ffn_norm_g_2, w_ffn_gate_2,
        w_ffn_up_2, w_ffn_down_2,
    )


_drawn_inputs = setup_inputs


def setup_inputs(seed=0):
    import zlib

    import numpy as np

    out = dict(_drawn_inputs(seed))
    spreads = {}
    factors = {'norm_mix': 3.695,
     'pool_scale': 3.872,
     'kv_norm': 8.0,
     'k_norm': 8.0,
     'q_norm': 8.0,
     'sinks': 5.165,
     'mem_norm': 8.0,
     'mem_q_norm': 8.0,
     'mem_k_norm': 8.0,
     'attn_norm_g_2': 7.454,
     'hg_out_norm_g_2': 8.0,
     'q_norm_g_2': 8.0,
     'k_norm_g_2': 8.0,
     'rel_bias_table_2': 8.0,
     'ffn_norm_g_2': 7.092}
    for name, (base, spread) in spreads.items():
        noise = np.random.default_rng([zlib.crc32(name.encode()), seed]).standard_normal(out[name].shape)
        drawn = base * np.exp(spread * noise) if base else spread * noise
        out[name] = __import__('jax').numpy.asarray(drawn.astype(out[name].dtype))
    for name, factor in factors.items():
        out[name] = (out[name] * factor).astype(out[name].dtype)
    return out
```

```python
from contextlib import ExitStack

import numpy as np

import concourse.bass as bass
from concourse import mybir

F32 = mybir.dt.float32
F32R = mybir.dt.float32r
BF16 = mybir.dt.bfloat16
I32 = mybir.dt.int32
ALU = mybir.AluOpType
ACT = mybir.ActivationFunctionType
AX_X = mybir.AxisListType.X

P = 128
SEQ = 256
TILES = SEQ // P
D = 1024
DCH = D // P
EPS = 1e-6
NEG = -1.0e30
UNIT_K = 4
NCOL = 512
UNIT = UNIT_K * NCOL
RAW_SLOTS, PART_SLOTS = 4, 3
AT_CHUNKS = 32
DH = 64
SWA_HEADS, KV_HEADS, MEM_HEADS = 12, 4, 4
WINDOWS = (2, 4, 8, 16)
PG = 192
D_FF, D_FF2 = 4096, 2816
H2 = 8
BUCKETS = 32
LEVELS = (1, 2, 4, 8, 16, 32, 64)

GAIN_ROWS = {}
_at = 0
for _name, _n in (("mix0", 8), ("mix1", 8), ("kv", 8), ("mem0", 8), ("mem1", 8), ("mlp0", 8), ("mlp1", 8),
                  ("attn2", 8), ("ffn2", 8), ("lb0", 8), ("lb1", 8), ("pool", 6), ("hg", 1), ("q2", 1), ("k2", 1),
                  ("k", 1), ("q", 1), ("mq0", 1), ("mq1", 1), ("mk0", 1), ("mk1", 1)):
    GAIN_ROWS[_name] = (_at, _n)
    _at += _n
N_GAINS = _at

GEMMS = {
    "mem0": (8, 512, 16, "nat"), "in0": (8, 1024, 0, "nat"), "mem1": (8, 512, 24, "nat"),
    "out0": (8, 1024, 8, "res"),
    "kv": (8, 512, 16, "nat"), "in1": (8, 1024, 0, "nat"), "out1": (8, 1024, 8, "res"),
    "w2": (8, 9216, 0, "w2"), "bhg": (8, 1024, 0, "gate"), "bat": (8, 1024, 8, "gate"),
    "out2": (8, 1024, 0, "res"),
    "ffg": (8, D_FF2, 0, "ffg"), "ffu": (8, D_FF2, 0, "ffu"), "down2": (22, 1024, 8, "res"),
}
for _l in (0, 1):
    for _h in (0, 1):
        GEMMS[f"up{_l}{_h}"] = (8, D_FF // 2, 0, "relu")
        GEMMS[f"down{_l}{_h}"] = (16, 1024, None, "res")


def h_slot(c):
    return 8 + c % (AT_CHUNKS - 8)


class Plan:

    def __init__(self):
        self.steps, self.units, self.groups, self.batches = [], [], [], []
        self.count = {}
        self.group_of = {}
        self.hs_last = {}
        self.prob_batch = {}

    def tick(self, name):
        self.count[name] = self.count.get(name, 0) + 1
        return self.count[name]

    def now(self, name):
        return self.count.get(name, 0)

    def add(self, kind, **st):
        st["kind"] = kind
        st["at"] = dict(self.count)
        self.steps.append(st)
        return st

    def mm(self, gemm, ng, kq, need=()):
        kch, cols, base, how = GEMMS[gemm]
        g = self.group_of.get((gemm, ng))
        if g is None:
            n0 = ng * NCOL
            g = dict(gemm=gemm, ng=ng, n0=n0, w=min(NCOL, cols - n0), kch=kch, how=how, index=len(self.groups),
                     engine="dve" if how in ("res", "gate", "ffg", "ffu") else "act")
            g["free"] = {e: sum(o["engine"] == e for o in self.groups[:-1]) for e in ("act", "dve")}
            self.groups.append(g)
            self.group_of[gemm, ng] = g
        first = kq * UNIT_K
        u = dict(index=len(self.units), gemm=gemm, k0=first, kn=min(UNIT_K, kch - first), n0=g["n0"], w=g["w"])
        self.units.append(u)
        g["last_unit"] = u["index"] + 1
        self.add("mm", unit=u, group=g, need=list(need))

    def evac(self, gemm, ng, **more):
        g = self.group_of[gemm, ng]
        self.add("evac", group=g, **more)
        g["done"] = self.tick("evac_" + g["engine"])
        return ("evac_" + g["engine"], g["done"])

    def batch(self, src, dst, how, need, gains=None, scale=None, head=None):
        b = dict(index=len(self.batches), src=src, dst=dst, how=how, need=need, gains=gains, scale=scale, head=head)
        b["act"] = self.tick("t_act")
        b["dve"] = self.tick("t_dve") if how == "split" else self.now("t_dve")
        if len(self.batches) >= 2:
            o = self.batches[-2]
            b["free"] = ("t_dve", o["dve"]) if o["how"] == "split" else ("t_act", o["act"])
        self.batches.append(b)
        self.tick("t_full")
        self.add("batch", batch=b)
        return b

    def split_ready(self):
        return ("t_dve", self.now("t_dve"))


def build_plan():
    pl = Plan()

    def col_of(gain, c=0):
        return GAIN_ROWS[gain][0] + c

    def turn(src, chunks, dst, need, gain=None, one_gain=False):
        for c in chunks:
            gains = None
            if gain:
                gains = (col_of(gain), ) * 2 if one_gain else (col_of(gain, c), col_of(gain, c + 1))
            pl.batch([(src, c), (src, c + 1)], dst + c, "split", need, gains=gains)
        return pl.split_ready()

    def plain(src, c, dst, need, gain=None, scale=None, how="plain"):
        pl.batch([(src, c), (src, c + 1)], dst, how, need, gains=(col_of(gain),) * 2 if gain else None, scale=scale)

    def stats(name, src, need):
        pl.tick("stats")
        pl.add("stats", n=pl.now("stats"), src=src, name=name, need=need)

    def headnorm(src, heads, need, off=0):
        i = pl.tick("headnorm")
        pl.add("headnorm", n=i, src=src, heads=heads, off=off, need=need)
        return ("head_normed", i)

    def scores(kind, h, **more):
        a = pl.tick("head")
        st = dict(a=a, type=kind, h=h, use6=pl.tick("use6"), full6=pl.tick("full6"), **more)
        pl.add("scores", **st)
        return st

    def head_tail(hd, close, chunk, use7):
        pl.add("normalise", head=hd)
        b = pl.batch(None, None, "probs", ("probs_ready", hd["a"]), head=hd)
        pl.prob_batch[hd["a"]] = b["index"] + 1
        hi7 = pl.tick("hi7") if close else 0
        pl.tick("values")
        pl.add("values", head=hd, batch=b, use7=use7, close=close, chunk=chunk, hi7=hi7)

    def heads(kind, hs, chunk_of, weave=(), **more):
        weave = list(weave)
        pending = use7 = None
        for n, h in enumerate(hs):
            hd = scores(kind, h, **more)
            if pending:
                head_tail(*pending)
            if n % 2 == 0:
                use7 = pl.tick("use7")
            pending = (hd, n % 2 == 1, chunk_of(h), use7)
            if weave:
                weave.pop(0)()
        head_tail(*pending)

    def pair_tail(gemm, x_first=None):
        last = GEMMS[gemm][0] // UNIT_K - 1 + (GEMMS[gemm][0] % UNIT_K > 0)
        pl.mm(gemm, 0, last)
        done0 = pl.evac(gemm, 0)
        pl.mm(gemm, 1, last - 1)
        first = x_first(done0) if x_first else None
        pl.mm(gemm, 1, last)
        return first, pl.evac(gemm, 1)

    pl.add("gains", use6=pl.tick("use6"))
    pl.tick("full6")
    gains = ("free6", 1)
    all8 = (0, 2, 4, 6)
    stats("mem", "mem", ("mem_in", 16))
    stats("x0", "x", ("x_in", 16))
    r = turn("mem", all8, 16, gains, "mem0")
    pl.mm("mem0", 0, 0, [r])
    r = turn("x", all8, 0, gains, "mix0")
    pl.mm("mem0", 0, 1)
    kv_done = pl.evac("mem0", 0)
    pl.mm("in0", 1, 0, [r])
    r = turn("mem", all8, 24, gains, "mem1")
    pl.mm("in0", 0, 0)
    pl.mm("in0", 1, 1)
    hi_done = pl.evac("in0", 1)
    pl.mm("in0", 0, 1)
    lo_done = pl.evac("in0", 0)

    nd = headnorm("mkv0", 4, kv_done)
    plain("mkv0", 0, ("mkt0", 0), nd, "mk0")
    nd = headnorm("nat", 4, hi_done, off=12)
    plain("nat", 6, ("qt", 6), nd, "mq0")
    pl.mm("mem1", 0, 0, [r])

    def pool_group(gi):
        pl.tick("full6")
        pl.add("pool_diff", gi=gi, use6=pl.tick("use6"), need=lo_done)
        pl.tick("full7")
        pl.tick("hi7")
        pl.add("pool_mix", gi=gi, use7=pl.tick("use7"), hi7=pl.now("hi7"), full7=pl.now("full7"))
    pool_group(0)
    pool_group(1)
    pl.mm("mem1", 0, 1)
    kv_done = pl.evac("mem1", 0)
    pool_group(2)
    pool_group(3)
    heads("mem", range(4), lambda h: 14 + h // 2, layer=0)
    mix = ("free7", pl.now("use7"))
    nd = headnorm("mkv1", 4, kv_done)
    plain("mkv1", 0, ("mkt1", 0), nd, "mk1")

    def out_gemm(name, need, x_first):
        pl.mm(name, 0, 0, [need])
        return pair_tail(name, x_first)

    def mlp(l, first, done1, gain, x_first):
        stats(gain, "x", done1)
        late = None
        for half in (0, 1):
            up, down = f"up{l}{half}", f"down{l}{half}"

            def finish(ng):
                n = pl.tick("squares")
                pl.evac(up, ng, hs=n)
                return ng, n

            def turn_h(ng, n):
                for pr in (0, 2):
                    b = pl.batch([(("hs", (n - 1) % 2), pr), (("hs", (n - 1) % 2), pr + 1)],
                                 h_slot(half * 16 + ng * 4 + pr), "split", ("squared", n))
                pl.hs_last[n] = b["index"] + 1
                return pl.split_ready()
            last = None
            for ng in range(4):
                if half == 0 and ng == 0:
                    pl.mm(up, 0, 0, [first])
                    r = turn("x", (4, 6), 0, done1, gain)
                    pl.mm(up, 1, 0)
                    pl.mm(up, 0, 1, [r])
                else:
                    if half or ng > 1:
                        pl.mm(up, ng, 0)
                    if last:
                        turn_h(*last)
                    pl.mm(up, ng, 1)
                last = finish(ng)
            ready = pl.split_ready()
            pl.mm(down, 0, 0, [ready])
            ready = turn_h(*last)
            pl.mm(down, 1, 0)
            pl.mm(down, 0, 1)
            pl.mm(down, 1, 1)
            pl.mm(down, 0, 2)
            pl.steps[-1]["need"].append(ready)
            first, done1 = pair_tail(down, x_first if half else None)
        return first, done1

    def x_first_of(*gains_dst):
        def go(done0):
            for gain, dst in gains_dst:
                r = turn("x", (0, 2), dst, done0, gain)
            return r
        return go

    first, done1 = out_gemm("out0", mix, x_first_of(("mlp0", 0)))
    first, done1 = mlp(0, first, done1, "mlp0", x_first_of(("kv", 16), ("mix1", 0)))

    stats("mix1", "x", done1)
    pl.mm("kv", 0, 0, [first])
    kv_late = turn("x", (4, 6), 16, done1, "kv")
    r = turn("x", (4, 6), 0, done1, "mix1")
    pl.mm("in1", 1, 0)
    pl.mm("kv", 0, 1, [kv_late])
    kv_done = pl.evac("kv", 0)
    pl.mm("in1", 1, 1, [r])
    hi_done = pl.evac("in1", 1)
    nd = headnorm("kvn", 4, kv_done)
    for pr in (0, 2):
        plain("kdup", pr, ("kt1", pr), nd, "k")
    pl.mm("in1", 0, 0)
    nd = headnorm("nat", 8, hi_done, off=8)
    plain("nat", 4, ("qt", 4), nd, "q")
    plain("nat", 6, ("qt", 6), nd, "mq1")

    def in1_second():
        pl.mm("in1", 0, 1)
        in1_second.done = pl.evac("in1", 0)
    heads("mem", range(4), lambda h: 14 + h // 2, layer=1, weave=(in1_second,))
    nd = headnorm("nat", 8, in1_second.done, off=0)
    plain("nat", 0, ("qt", 0), nd, "q")
    plain("nat", 2, ("qt", 2), nd, "q")
    heads("swa", list(range(8, 12)) + list(range(8)), lambda h: 8 + h // 2)
    first, done1 = out_gemm("out1", ("free7", pl.now("use7")), x_first_of(("mlp1", 0)))
    first, done1 = mlp(1, first, done1, "mlp1", x_first_of(("attn2", 0)))

    stats("attn2", "x", done1)
    pl.add("second_block")
    todo = []

    def run(n=1):
        for _ in range(n):
            if todo:
                todo.pop(0)()

    def level(l, j):
        k = 6 + (4 * l + j) % 2
        use = pl.tick(f"use{k}")
        full = pl.tick(f"full{k}")
        level.uses[l, j] = (k, use)
        pl.add("level", l=l, j=j, bank=k, use=use, full=full, scaled=level.uses.get((l - 1, j)))
    level.uses = {}

    def out_heads(q, t):
        k = 6 + t
        pl.tick(f"full{k}")
        pl.add("hg_out", q=q, t=t, bank=k, use=pl.tick(f"use{k}"), full=pl.now(f"full{k}"))

    def bias_rows():
        pl.tick("full6")
        pl.add("bias_rows", use6=pl.tick("use6"), full6=pl.now("full6"))

    def after_group(ng, need):
        nat2 = ("nat2", ng % 2)
        half, sec = ng % 2, ng // 2
        if sec == 0:
            todo.extend(lambda pr=pr: plain(nat2, pr, ("q2", 4 * half + pr), need, scale=P ** -0.5) for pr in (0, 2))
        elif sec == 1:
            todo.extend(lambda pr=pr: plain(nat2, pr, ("f2", 4 * half + pr), need, how="forget") for pr in (0, 2))
        elif sec == 2 and half:
            todo.append(bias_rows)
            for l in range(len(LEVELS) + 2):
                for j in range(4):
                    todo.append(lambda l=l, j=j: level(l, j))
            for q in (0, 1):
                for t in (0, 1):
                    todo.append(lambda q=q, t=t: out_heads(q, t))
            todo.append(lambda: pl.add("hg_norm", n=pl.tick("headnorm")))
        elif sec in (3, 4):
            def norm():
                n = pl.tick("headnorm")
                pl.add("headnorm2", n=n, slot=ng % 2, need=need)
                norm.done = ("head_normed", n)
            nm, g = ("aq", "q2") if sec == 3 else ("ak", "k2")
            todo[1:1] = [norm]
            todo[4:4] = [lambda pr=pr: plain(nat2, pr, (nm, 4 * half + pr), norm.done, g) for pr in (0, 2)]
        elif sec == 6:
            todo.append(lambda: pl.add("hg_gate", slot=ng % 2, half=half, n=pl.tick("hg_gate"), need=need))
        if ng == 13:
            todo.append(lambda: pl.add("bias_tiles"))
            state = dict(pending=None)

            def moba_step(h):
                hd = scores("moba", h)
                if state["pending"]:
                    head_tail(*state["pending"])
                state["pending"] = (hd, True, 8 + h, pl.tick("use7"))
            todo.extend(lambda h=h: moba_step(h) for h in range(H2))
            todo.append(lambda: head_tail(*state["pending"]))

    for ng in range(18):
        if ng == 0:
            pl.mm("w2", 0, 0, [first])
            r = turn("x", (4, 6), 0, done1, "attn2")
            pl.mm("w2", 1, 0)
            pl.mm("w2", 0, 1, [r])
        else:
            if ng > 1:
                pl.mm("w2", ng, 0)
                run(3 if 6 <= ng < 14 else 2 if ng < 14 else 1)
            pl.mm("w2", ng, 1)
            run(3 if 6 <= ng < 14 else 2 if ng < 14 else 1)
        while ng == 14 and len(todo) > H2 + 1:
            run()
        after_group(ng, pl.evac("w2", ng))
    while todo:
        run()
    hg_ready = turn("oh", all8, 0, ("hg_gated", pl.now("hg_gate")), "hg", one_gain=True)
    att_ready = ("free7", pl.now("use7"))
    pl.add("gates")
    pl.mm("bhg", 0, 0, [hg_ready])
    pair_tail("bhg")
    pl.mm("bat", 0, 0, [att_ready])
    m_first, done1 = pair_tail("bat", lambda done0: turn("gate", (0, 2), 0, done0))
    pl.mm("out2", 0, 0, [m_first])
    m_late = turn("gate", (4, 6), 0, done1)
    pl.mm("out2", 1, 0)
    pl.mm("out2", 0, 1, [m_late])
    done0 = pl.evac("out2", 0)
    first = None
    pl.mm("out2", 1, 1)
    done1 = pl.evac("out2", 1)
    first = turn("x", (0, 2), 0, done0, "ffn2")
    stats("ffn2", "x", done1)

    last = None

    def turn_g(ng, n, w, need):
        for pr in range(0, w // P, 2):
            b = pl.batch([(("hs2", (n - 1) % 2), pr), (("hs2", (n - 1) % 2), pr + 1)], 8 + 4 * ng + pr, "split", need)
        pl.hs_last["g", n] = b["index"] + 1
        return pl.split_ready()
    for ng in range(-(-D_FF2 // NCOL)):
        n = ng + 1
        if ng == 0:
            pl.mm("ffg", 0, 0, [first])
            r = turn("x", (4, 6), 0, done1, "ffn2")
            pl.mm("ffu", 0, 0)
            pl.mm("ffg", 0, 1, [r])
        else:
            pl.mm("ffg", ng, 0)
            turn_g(*last)
            pl.mm("ffg", ng, 1)
        pl.evac("ffg", ng, n=n)
        if ng:
            pl.mm("ffu", ng, 0)
        pl.mm("ffu", ng, 1)
        last = (ng, n, min(NCOL, D_FF2 - ng * NCOL), pl.evac("ffu", ng, n=n))
    pl.mm("down2", 0, 0, [pl.split_ready()])
    ready = turn_g(*last)
    pl.mm("down2", 1, 0)
    for kq in (1, 2, 3, 4):
        pl.mm("down2", 0, kq, [ready])
        if kq < 4:
            pl.mm("down2", 1, kq)
    pl.mm("down2", 0, 5)
    pl.add("store", half=0, need=pl.evac("down2", 0))
    pl.mm("down2", 1, 4)
    pl.mm("down2", 1, 5)
    pl.add("store", half=1, need=pl.evac("down2", 1))

    steps, seen = [], 0
    for st in pl.steps:
        if st["kind"] == "mm":
            ahead = min(len(pl.units), st["unit"]["index"] + PART_SLOTS)
            while seen < ahead:
                steps.append(dict(kind="split", unit=pl.units[seen]))
                seen += 1
        steps.append(st)
    pl.steps = steps
    return pl


def two_blocks_kernel(nc, a, out, scratch):
    pl = build_plan()
    steps = pl.steps
    with ExitStack() as ctx:
        base = (nc.sbuf_base + 63) // 64 * 64
        room = nc.sbuf_usable_end - base - 64
        ctx.enter_context(nc.sbuf_tensor("whole_map", [P, room // 4], F32))

        def at(name, off, shape, dt=F32):
            return nc.alloc_sbuf_tensor_at(name, [P, *shape], dt, offset=base + off)

        o = 0
        raw = at("raw", o, [RAW_SLOTS, UNIT]); o += RAW_SLOTS * UNIT * 4
        w_hi = at("w_hi", o, [PART_SLOTS, UNIT], F32R); o += PART_SLOTS * UNIT * 4
        w_lo = at("w_lo", o, [PART_SLOTS, UNIT], F32R); o += PART_SLOTS * UNIT * 4
        at_hi = at("at_hi", o, [AT_CHUNKS, SEQ], F32R); o += AT_CHUNKS * SEQ * 4
        upper_hi = o - 16 * SEQ * 4
        at_lo = at("at_lo", o, [AT_CHUNKS, SEQ], F32R); o += AT_CHUNKS * SEQ * 4
        upper_lo = o - 16 * SEQ * 4
        x = at("x_res", o, [TILES, D]); o += TILES * D * 4
        ident = at("ident_sb", o, [P]); o += P * 4
        gt = at("gt", o, [112]); o += 112 * 4
        stat = at("stat", o, [248]); o += 248 * 4
        sink = at("sink_sb", o, [SWA_HEADS]); o += 64
        lb = at("lb", o, [2, H2]); o += 64
        arena = o
        sc = at("sc", o, [3, 512]); o += 3 * 512 * 4
        pt = at("pt", o, [2, 512]); o += 2 * 512 * 4
        mkv = [at(f"mkv{l}", o + 4096 * l, [TILES, 512]) for l in (0, 1)]; o += 8192
        mkt = [at(f"mkt{l}", o + 2048 * l, [2, SEQ]) for l in (0, 1)]; o += 4096
        nat = at("nat", o, [TILES, D])
        mem = at("mem_sb", o, [TILES, D])
        hs = at("hs", o, [2, TILES, NCOL]); o += 8192
        qt = at("qt", o, [8, SEQ])
        square = at("square", o, [D // 2])
        grows = at("grows", o + 4096, [P])
        kdup = at("kdup", o + 4096, [TILES, KV_HEADS, 2, DH])
        dt = at("dt", o + 2048, [4, SEQ]); o += 8192
        junk = at("junk", o, [D], BF16); o += 2048
        poolp, pwa, pwb = at("poolp_sb", o, [4, 384]), at("pwa", o + 6144, [4, PG]), at("pwb", o + 9216, [4, PG])
        dist, kvn, kt1 = at("dist_sb", o, [384]), at("kvn", o + 1536, [TILES, 512]), at("kt1", o + 5632, [4, SEQ])
        o += 12288
        assert o <= room, (o, room)
        q2, k2 = at("q2", upper_hi, [H2, SEQ]), at("k2", upper_hi + 8192, [H2, SEQ])
        gate = at("gate", upper_hi, [2, TILES, D])
        f2, f2b = at("f2", upper_lo, [H2, SEQ]), at("f2b", upper_lo + 8192, [H2, SEQ // 2])
        attx = at("attx", upper_lo + 12288, [H2, P])
        oh, pt2 = at("oh", upper_lo, [TILES, D]), at("pt2", upper_lo + 8192, [2, 512])
        sgt = at("sgt", upper_lo + 12288, [TILES, 512])
        o = arena
        v2 = at("v2", o, [TILES, D]); ebias = at("ebias", o, [H2, SEQ]); sig2 = at("sig2", o, [TILES, NCOL]); o += 8192
        att = at("att", o, [H2, TILES, P]); sc2 = at("sc2", o, [3, 512]); o += 8192
        aq = at("aq", o, [H2, SEQ]); o += 8192
        ak = at("ak", o, [H2, SEQ])
        rrow, hot, tab = at("rrow", o, [384]), at("hot_sb", o + 1536, [384]), at("tab_sb", o + 3072, [H2]); o += 8192
        av = at("av", o, [TILES, D]); o += 8192
        nat2 = at("nat2", o, [2, TILES, NCOL]); hs2 = at("hs2", o, [2, TILES, NCOL]); o += 8192
        junk2 = at("junk2", o, [D], BF16); o += 2048
        lmask = at("lmask_sb", o, [len(LEVELS), P]); o += len(LEVELS) * P * 4
        assert o <= room, (o, room)

        bank = [ctx.enter_context(nc.psum_tensor(f"bank{i}", [P, 512], F32)) for i in range(8)]

        S = {n: ctx.enter_context(nc.semaphore(n)) for n in (
            "const_in", "x_in", "mem_in", "grow_in", "sink_in", "pool_in", "swa_in", "block2_in", "bias_in",
            "bias_out", "out_stored",
            "w_hi_ready", "w_lo_ready", "unit_used",
            "evac_act", "evac_dve",
            "t_full", "t_act", "t_dve",
            "full6", "full7", "free6", "free7", "hi7",
            "squares_summed", "rstd_ready", "head_squares", "head_rstd", "head_normed",
            "bias_neg", "probs_raw", "probs_ready", "values_done",
            "lb_ready", "forget_ready", "squared", "sigmoid_ready", "hg_sig", "hg_gated", "gates_ready",
            "dve_chain", "act_chain", "pool_chain")}
        raw_in = [ctx.enter_context(nc.semaphore(f"raw_in{i}")) for i in range(RAW_SLOTS)]

        def wait(eng, need):
            eng.wait_ge(S[need[0]], need[1])

        SSQ, VAR, RSTD = 0, 16, 32
        HSS, HVAR, HR, HALF = 48, 80, 112, 144
        AM, AN, AL, AR, AE = 176, 182, 188, 194, 200

        def col(c, n=1):
            return stat[:, c:c + n]

        norm_no = {st["name"]: st["n"] for st in steps if st["kind"] == "stats"}
        norm_of = {"mem0": "mem", "mem1": "mem", "in0": "x0", "kv": "mix1", "in1": "mix1", "w2": "attn2",
                   "ffg": "ffn2", "ffu": "ffn2", "up00": "mlp0", "up01": "mlp0", "up10": "mlp1", "up11": "mlp1"}

        def rstd_col(gemm):
            return RSTD + 2 * (norm_no[norm_of[gemm]] - 1)

        weights = {"mem0": a["w_mem_kv"][0], "mem1": a["w_mem_kv"][1], "in0": a["w_in"][0], "in1": a["w_in"][1],
                   "out0": a["w_out"][0], "out1": a["w_out"][1], "kv": a["w_kv"], "w2": a["w_in_2"][0],
                   "bhg": a["w_branch_hg_2"][0], "bat": a["w_branch_attn_2"][0], "out2": a["w_out_2"][0],
                   "ffg": a["w_ffn_gate_2"][0], "ffu": a["w_ffn_up_2"][0], "down2": a["w_ffn_down_2"][0]}
        for l in (0, 1):
            for half in (0, 1):
                n = D_FF // 2
                weights[f"up{l}{half}"] = a["w_up"][l][:, half * n:(half + 1) * n]
                weights[f"down{l}{half}"] = a["w_down"][l][half * n:(half + 1) * n, :]
        w2_order = [0, 1, 2, 3, 4, 5, 8, 9, 10, 11, 12, 13, 6, 7, 14, 15, 16, 17]

        def unit_ap(buf, slot, u):
            return buf[:, slot, 0:u["kn"] * u["w"]].rearrange("p (k n) -> p k n", k=u["kn"])

        def acc(g, t):
            return bank[2 * (g["index"] % 2) + t]

        def t_bank(b):
            return bank[4 + b["index"] % 2]

        natural = {"x": x, "mem": mem, "nat": nat, "oh": oh, "mkv0": mkv[0], "mkv1": mkv[1], "kvn": kvn}
        slotted = {"hs": hs, "nat2": nat2, "hs2": hs2}
        turned = {"qt": qt, "kt1": kt1, "mkt0": mkt[0], "mkt1": mkt[1], "q2": q2, "f2": f2, "aq": aq, "ak": ak}

        def chunk_of(src, t):
            name, c = src
            if name == "kdup":
                return kdup[:, t, c].rearrange("p two d -> p (two d)")
            if name == "gate":
                return gate[:, 0, t, c * P:(c + 1) * P]
            if isinstance(name, tuple):
                return slotted[name[0]][:, name[1], t, c * P:(c + 1) * P]
            return natural[name][:, t, c * P:(c + 1) * P]

        def segments(kind):
            return ((0, 0, 256), (1, 256, 256)) if kind == "mem" else ((0, 0, 128), (1, 128, 256))

        def prob_blocks(kind):
            if kind == "mem":
                return tuple((t * 256 + m * P, m, m * 256 + t * P, t) for m in (0, 1) for t in (0, 1))
            return ((0, 0, 0, 0), (128, 0, 128, 1), (256, 1, 256, 1))

        def scores_buf(hd):
            return (sc2 if hd["type"] == "moba" else sc)[:, (hd["a"] - 1) % 3]

        def pt_buf(hd):
            return (pt2 if hd["type"] == "moba" else pt)[:, (hd["a"] - 1) % 2]

        def pool_pieces(gi):
            cut = P if gi % 2 == 0 else P // 2
            for c0, c1 in ((0, cut), (cut, PG)):
                f = PG * gi + c0
                yield c0, c1, slice(f % P, f % P + c1 - c0), f // P

        def settle(eng, st):
            for name, count in (("t_full", "t_full"), ("full6", "full6"), ("full7", "full7"), ("values_done", "values"),
                                ("evac_dve", "evac_dve")):
                if st["at"].get(count):
                    eng.wait_ge(S[name], st["at"][count])

        g_row = {"mix0": a["norm_mix"][0], "mix1": a["norm_mix"][1], "kv": a["kv_norm"], "mem0": a["mem_norm"][0],
                 "mem1": a["mem_norm"][1], "mlp0": a["norm_mlp"][0], "mlp1": a["norm_mlp"][1],
                 "attn2": a["attn_norm_g_2"][0], "ffn2": a["ffn_norm_g_2"][0], "lb0": a["hg_lb_gamma_2"][0],
                 "lb1": a["hg_lb_gamma_2"][1], "pool": a["pool_scale"][0], "hg": a["hg_out_norm_g_2"][0],
                 "q2": a["q_norm_g_2"][0], "k2": a["k_norm_g_2"][0]}
        g_head = {"k": a["k_norm"], "q": a["q_norm"][0], "mq0": a["mem_q_norm"][0], "mq1": a["mem_q_norm"][1],
                  "mk0": a["mem_k_norm"][0], "mk1": a["mem_k_norm"][1]}
        gain_loads = len(g_row) + 2 * len(g_head)

        last_level = {st["bank"]: st["use"] for st in steps if st["kind"] == "level"}

        block = ctx.enter_context(nc.Block())

        @block.sync
        def _(sp):
            sp.dma_start(mem[:], a["mem"][0].rearrange("(t p) d -> p t d", p=P)).then_inc(S["mem_in"], 16)
            sp.dma_start(x[:], a["x"][0].rearrange("(t p) d -> p t d", p=P)).then_inc(S["x_in"], 16)
            for st in steps:
                if st["kind"] == "split":
                    u = st["unit"]
                    slot = u["index"] % RAW_SLOTS
                    if u["index"] >= RAW_SLOTS:
                        sp.wait_ge(S["w_lo_ready"], u["index"] - RAW_SLOTS + 1)
                    n0 = u["n0"] if u["gemm"] != "w2" else w2_order[u["n0"] // NCOL] * NCOL
                    src = weights[u["gemm"]][u["k0"] * P:(u["k0"] + u["kn"]) * P, n0:n0 + u["w"]]
                    sp.dma_start(unit_ap(raw, slot, u), src.rearrange("(k p) n -> p k n", p=P)).then_inc(raw_in[slot], 16)
                elif st["kind"] == "store":
                    wait(sp, st["need"])
                    h = slice(st["half"] * NCOL, (st["half"] + 1) * NCOL)
                    sp.dma_start(out[0].rearrange("(t p) d -> p t d", p=P)[:, :, h], x[:, :, h]).then_inc(S["out_stored"], 16)
            sp.wait_ge(S["out_stored"], 32)

        @block.gpsimd
        def _(pool):
            chain = [0]

            def link(ins):
                ins.then_inc(S["pool_chain"], 1)
                chain[0] += 1
                pool.wait_ge(S["pool_chain"], chain[0])

            link(pool.memset(stat[:, HALF:HALF + 32], -0.5))
            link(pool.memset(grows[:], 0.0))
            pool.dma_start(ident[:], a["ident"]).then_inc(S["const_in"], 16)
            for name, v in g_row.items():
                r, n = GAIN_ROWS[name]
                pool.dma_start(grows[r:r + n, :], v.rearrange("(n p) -> n p", n=n)).then_inc(S["grow_in"], 16)
            for name, v in g_head.items():
                r = GAIN_ROWS[name][0]
                for s in (0, DH):
                    pool.dma_start(grows[r:r + 1, s:s + DH], v.unsqueeze(0)).then_inc(S["grow_in"], 16)
            pool.dma_start(poolp[:], a["poolp"]).then_inc(S["pool_in"], 16)
            pw = a["pool_w"][0].rearrange("g c d -> c g d")
            pool.dma_start(pwa[:], pw[0:P]).then_inc(S["pool_in"], 16)
            pool.dma_start(pwb[0:PG - P], pw[P:PG]).then_inc(S["pool_in"], 16)
            pool.dma_start(sink[:], a["sinks"][0].partition_broadcast(P)).then_inc(S["sink_in"], 16)
            for st in steps:
                kind = st["kind"]
                if kind == "stats":
                    c = 2 * (st["n"] - 1)
                    pool.wait_ge(S["squares_summed"], st["n"])
                    link(pool.tensor_scalar(col(VAR + c, 2), col(SSQ + c, 2), 1.0 / D, EPS, ALU.mult, ALU.add))
                    pool.tensor_tensor(col(RSTD + c, 2), col(VAR + c, 2), col(HALF, 2), ALU.pow
                                       ).then_inc(S["rstd_ready"], 1)
                    if st["name"] == "mlp0":
                        settle(pool, st)
                        pool.dma_start(dist[:], a["dist"]).then_inc(S["swa_in"], 16)
                elif kind in ("headnorm", "headnorm2", "hg_norm"):
                    cols = {"headnorm": TILES * st.get("heads", 0), "headnorm2": TILES * 4, "hg_norm": TILES * H2}[kind]
                    pool.wait_ge(S["head_squares"], st["n"])
                    link(pool.tensor_scalar(col(HVAR, cols), col(HSS, cols), 1.0 / (DH if kind == "headnorm" else P), EPS,
                                            ALU.mult, ALU.add))
                    pool.tensor_tensor(col(HR, cols), col(HVAR, cols), col(HALF, cols), ALU.pow
                                       ).then_inc(S["head_rstd"], 1)
                elif kind == "evac" and st["group"]["how"] == "relu":
                    h = hs[:, (st["hs"] - 1) % 2]
                    pool.wait_ge(S["evac_act"], st["group"]["done"])
                    pool.tensor_tensor(h, h, h, ALU.mult).then_inc(S["squared"], 1)
                elif kind == "second_block":
                    settle(pool, st)
                    pool.wait_ge(S["rstd_ready"], st["at"]["stats"])
                    link(pool.memset(tab[BUCKETS:BUCKETS + 1], NEG))
                    pool.dma_start(tab[0:BUCKETS], a["rel_bias_table_2"]).then_inc(S["block2_in"], 16)
                    pool.dma_start(hot[0:BUCKETS + 1], a["hot"]).then_inc(S["block2_in"], 16)
                    pool.dma_start(lmask[:], a["lmask"]).then_inc(S["block2_in"], 16)
                elif kind == "bias_rows":
                    pool.wait_ge(S["free6"], st["use6"])
                    pool.dma_start(scratch, rrow[0:H2, :]).then_inc(S["bias_out"], 16)
                elif kind == "bias_tiles":
                    settle(pool, st)
                    pool.wait_ge(S["bias_out"], 16)
                    src = bass.AP(tensor=scratch.tensor, offset=0, ap=[[1, P], [384, H2], [1, SEQ]])
                    pool.dma_start(ebias[:], src).then_inc(S["bias_in"], 16)
            pool.wait_ge(S["bias_out"], 16)

        @block.scalar
        def _(act):
            chain = [0]

            def tick(ins):
                ins.then_inc(S["act_chain"], 1)
                chain[0] += 1

            for st in steps:
                kind = st["kind"]
                if kind == "split":
                    u = st["unit"]
                    i = u["index"]
                    n = u["kn"] * u["w"]
                    act.wait_ge(raw_in[i % RAW_SLOTS], 16 * (i // RAW_SLOTS + 1))
                    if i >= PART_SLOTS:
                        act.wait_ge(S["unit_used"], i - PART_SLOTS + 1)
                    act.activation(w_hi[:, i % PART_SLOTS, 0:n], raw[:, i % RAW_SLOTS, 0:n], ACT.Copy
                                   ).then_inc(S["w_hi_ready"], 1)
                elif kind == "gains":
                    act.wait_ge(S["lb_ready"], 1)
                    act.activation(lb[:, 0, :], lb[:, 1, :], ACT.Sigmoid).then_inc(S["lb_ready"], 1)
                elif kind == "stats":
                    wait(act, st["need"])
                    if st["n"] > 1:
                        act.wait_ge(S["squares_summed"], st["n"] - 1)
                    if st["name"] == "ffn2":
                        settle(act, st)
                    buf = natural[st["src"]]
                    tick(act.activation(junk[:], buf[:, 0, :], ACT.Square, accum_out=col(SSQ + 2 * (st["n"] - 1))))
                    act.wait_ge(S["act_chain"], chain[0])
                    act.activation(junk[:], buf[:, 1, :], ACT.Square, accum_out=col(SSQ + 2 * (st["n"] - 1) + 1)
                                   ).then_inc(S["squares_summed"], 1)
                elif kind == "evac" and st["group"]["how"] in ("nat", "relu", "w2", "ffg"):
                    g = st["group"]
                    how, ng, w = g["how"], g["ng"], g["w"]
                    act.wait_ge(S["unit_used"], g["last_unit"])
                    act.wait_ge(S["rstd_ready"], norm_no[norm_of[g["gemm"]]])
                    r = rstd_col(g["gemm"])
                    func, done = ACT.Copy, "evac_act"
                    if how == "nat":
                        settle(act, st)
                        dst = {"mem0": mkv[0], "mem1": mkv[1], "kv": kvn}.get(g["gemm"])
                        if dst is None:
                            dst = nat[:, :, g["n0"]:g["n0"] + w]
                    elif how == "relu":
                        func = ACT.Relu
                        dst = hs[:, (st["hs"] - 1) % 2]
                        if st["hs"] > 2:
                            act.wait_ge(S["t_full"], pl.hs_last[st["hs"] - 2])
                        else:
                            settle(act, st)
                    elif how == "ffg":
                        func, done = ACT.Sigmoid, "sigmoid_ready"
                        dst = sig2[:, :, 0:w]
                        act.wait_ge(S["evac_dve"], st["at"]["evac_dve"])
                    else:
                        half, sec = ng % 2, ng // 2
                        cols = slice(half * NCOL, (half + 1) * NCOL)
                        if sec == 2:
                            dst = v2[:, :, cols]
                        elif sec == 5:
                            dst = av[:, :, cols]
                        elif sec >= 7:
                            dst = gate[:, sec - 7, :, cols]
                            if ng == 14:
                                act.wait_ge(S["free6"], st["at"]["use6"] - 0)
                                act.wait_ge(S["free7"], st["at"]["use7"] - 0)
                        else:
                            dst = nat2[:, ng % 2]
                        if st["at"].get("t_full"):
                            act.wait_ge(S["t_full"], st["at"]["t_full"])
                        if sec == 6:
                            act.wait_ge(S["head_normed"], 9)
                    for t in range(TILES):
                        ins = act.activation(dst[:, t, :], acc(g, t)[:, 0:w], func, scale=col(r + t))
                    ins.then_inc(S[done], 1)
                elif kind == "batch":
                    b = st["batch"]
                    how, tb = b["how"], t_bank(b)
                    act.wait_ge(S["t_full"], b["index"] + 1)
                    if how == "split":
                        for i in (0, 1):
                            kw = dict(scale=gt[:, b["gains"][i]:b["gains"][i] + 1]) if b["gains"] else {}
                            ins = act.activation(at_hi[:, b["dst"] + i, :], tb[:, i * SEQ:(i + 1) * SEQ], ACT.Copy, **kw)
                    elif how == "plain":
                        nm, c = b["dst"]
                        if nm == "ak":
                            act.wait_ge(S["bias_out"], 16)
                        if nm == "qt":
                            act.wait_ge(S["free7"], st["at"].get("use7", 0)) if st["at"].get("use7") else None
                        kw = dict(scale=gt[:, b["gains"][0]:b["gains"][0] + 1]) if b["gains"] else \
                            dict(scale=b["scale"]) if b["scale"] else {}
                        ins = act.activation(turned[nm][:, c:c + 2, :], tb[:], ACT.Copy, **kw)
                    elif how == "forget":
                        c = b["dst"][1]
                        act.activation(f2[:, c:c + 2, :], tb[:], ACT.Sigmoid)
                        ins = act.activation(k2[:, c:c + 2, :], tb[:], ACT.Sigmoid, scale=-1.0)
                    else:
                        hd = b["head"]
                        if hd["a"] > 2:
                            act.wait_ge(S["values_done"], hd["a"] - 2)
                        n = 512 if hd["type"] == "mem" else 384
                        ins = act.activation(pt_buf(hd)[:, 0:n], tb[:, 0:n], ACT.Copy)
                    ins.then_inc(S["t_act"], 1)
                elif kind == "scores":
                    buf, s = scores_buf(st), (st["a"] - 1) % 3
                    act.wait_ge(S["bias_neg"], st["a"])
                    for i, (t, c0, n) in enumerate(segments(st["type"])):
                        ins = act.activation(buf[:, c0:c0 + n], buf[:, c0:c0 + n], ACT.Exp,
                                             scale=1.0 if st["type"] == "moba" else DH ** -0.5,
                                             bias=col(AN + 2 * s + i), accum_out=col(AL + 2 * s + i))
                    if st["type"] == "swa":
                        act.wait_ge(S["sink_in"], 16)
                        ins = act.activation(col(AE + 2 * s, 2), col(AN + 2 * s, 2), ACT.Exp,
                                             bias=sink[:, st["h"]:st["h"] + 1])
                    ins.then_inc(S["probs_raw"], 1)
                elif kind == "values" and st["close"]:
                    act.wait_ge(S["values_done"], st["head"]["a"])
                    act.activation(at_hi[:, st["chunk"], :], bank[7][:, 0:SEQ], ACT.Copy).then_inc(S["hi7"], 1)
                elif kind == "pool_mix":
                    act.wait_ge(S["full7"], st["full7"])
                    for i, (c0, c1, rows, ch) in enumerate(pool_pieces(st["gi"])):
                        gc = GAIN_ROWS["pool"][0] + ch
                        ins = act.activation(at_hi[rows, 8 + ch, :], bank[7][rows, i * SEQ:(i + 1) * SEQ], ACT.Copy,
                                             scale=gt[rows, gc:gc + 1])
                    ins.then_inc(S["hi7"], 1)
                elif kind in ("headnorm2", "hg_norm"):
                    act.wait_ge(S["head_rstd"], st["n"] - 1)
                    if kind == "hg_norm":
                        act.wait_ge(S["free6"], st["at"]["use6"])
                        act.wait_ge(S["free7"], st["at"]["use7"])
                    else:
                        wait(act, st["need"])
                    for half in range(2 if kind == "hg_norm" else 1):
                        for t in range(TILES):
                            for h in range(4):
                                j = t * 4 + h
                                if kind == "hg_norm":
                                    hh = 4 * half + h
                                    src, dst = oh[:, t, hh * P:(hh + 1) * P], HSS + t * H2 + hh
                                else:
                                    src, dst = nat2[:, st["slot"], t, h * P:(h + 1) * P], HSS + j
                                ins = act.activation(junk2[:, j * P:(j + 1) * P], src, ACT.Square, accum_out=col(dst))
                        if half == 0 and kind == "hg_norm":
                            tick(ins)
                            act.wait_ge(S["act_chain"], chain[0])
                    ins.then_inc(S["head_squares"], 1)
                    act.wait_ge(S["head_squares"], st["n"])
                elif kind == "hg_gate":
                    wait(act, st["need"])
                    if st["n"] > 1:
                        act.wait_ge(S["hg_gated"], st["n"] - 1)
                    act.activation(sgt[:], nat2[:, st["slot"]], ACT.Sigmoid).then_inc(S["hg_sig"], 1)
                elif kind == "gates":
                    act.wait_ge(S["evac_act"], pl.group_of["w2", 17]["done"])
                    act.activation(gate[:], gate[:], ACT.Sigmoid).then_inc(S["gates_ready"], 1)

        @block.tensor
        def _(pe):
            def take_bank(k, use):
                if use > 1:
                    pe.wait_ge(S[f"free{k}"], use - 1)

            for st in steps:
                kind = st["kind"]
                if kind == "gains":
                    pe.wait_ge(S["const_in"], 16)
                    pe.wait_ge(S["grow_in"], 16 * gain_loads)
                    pe.transpose(bank[6][:, 0:P], grows[:], ident[:]).then_inc(S["full6"], 1)
                elif kind == "mm":
                    u, g = st["unit"], st["group"]
                    for need in st["need"]:
                        wait(pe, need)
                    pe.wait_ge(S["w_lo_ready"], u["index"] + 1)
                    if u["k0"] == 0:
                        for e in ("act", "dve"):
                            if g["free"][e]:
                                pe.wait_ge(S["evac_" + e], g["free"][e])
                    slot = u["index"] % PART_SLOTS
                    wh, wl = unit_ap(w_hi, slot, u), unit_ap(w_lo, slot, u)
                    base_chunk = GEMMS[g["gemm"]][2]
                    for k in range(u["kn"]):
                        kc = u["k0"] + k
                        ch = h_slot(16 * int(g["gemm"][-1]) + kc) if base_chunk is None else base_chunk + kc
                        for t in range(TILES):
                            tok = slice(t * P, (t + 1) * P)
                            sums = acc(g, t)[:, 0:u["w"]]
                            pe.matmul(sums, at_hi[:, ch, tok], wh[:, k, :], start=kc == 0, stop=False)
                            pe.matmul(sums, at_hi[:, ch, tok], wl[:, k, :], start=False, stop=False)
                            ins = pe.matmul(sums, at_lo[:, ch, tok], wh[:, k, :], start=False, stop=kc == g["kch"] - 1)
                    ins.then_inc(S["unit_used"], 1)
                elif kind == "batch":
                    b = st["batch"]
                    wait(pe, b["need"])
                    if b["how"] != "probs" and b["src"][0][0] in ("x", "mem"):
                        wait(pe, (b["src"][0][0] + "_in", 16))
                    if "free" in b:
                        wait(pe, b["free"])
                    tb = t_bank(b)
                    if b["how"] == "probs":
                        for c, _, d, _ in prob_blocks(b["head"]["type"]):
                            ins = pe.transpose(tb[:, d:d + P], scores_buf(b["head"])[:, c:c + P], ident[:])
                    else:
                        for i in (0, 1):
                            for t in range(TILES):
                                c = i * SEQ + t * P
                                ins = pe.transpose(tb[:, c:c + P], chunk_of(b["src"][i], t), ident[:])
                    ins.then_inc(S["t_full"], 1)
                elif kind == "pool_diff":
                    pe.wait_ge(S["pool_in"], 48)
                    wait(pe, st["need"])
                    take_bank(6, st["use6"])
                    gi = st["gi"]
                    for i, (c0, c1) in enumerate(((0, P), (P, PG))):
                        ch = slice(PG * gi + c0, PG * gi + c1)
                        rows = slice(0, c1 - c0)
                        early, later = (bank[6][rows, i * SEQ + j * P:i * SEQ + (j + 1) * P] for j in (0, 1))
                        pe.matmul(early, nat[:, 0, ch], poolp[:, gi, 0:P], start=True, stop=True)
                        pe.matmul(later, nat[:, 0, ch], poolp[:, gi, P:SEQ], start=True, stop=False)
                        ins = pe.matmul(later, nat[:, 1, ch], poolp[:, gi, SEQ:SEQ + P], start=False, stop=True)
                    ins.then_inc(S["full6"], 1)
                elif kind == "pool_mix":
                    take_bank(7, st["use7"])
                    pe.wait_ge(S["free6"], st["at"]["use6"])
                    s, gi = 2 * (st["gi"] % 2), st["gi"]
                    for i, (c0, c1, rows, ch) in enumerate(pool_pieces(gi)):
                        mixed = bank[7][rows, i * SEQ:(i + 1) * SEQ]
                        pe.matmul(mixed, pwa[:, gi, c0:c1], dt[:, s, :], start=True, stop=False)
                        ins = pe.matmul(mixed, pwb[0:PG - P, gi, c0:c1], dt[0:PG - P, s + 1, :], start=False, stop=True)
                    ins.then_inc(S["full7"], 1)
                elif kind == "scores":
                    take_bank(6, st["use6"])
                    h = st["h"]
                    rows = slice(DH * (h % 2), DH * (h % 2) + DH)
                    if st["type"] == "mem":
                        q, k = qt[rows, 6 + h // 2, :], mkt[st["layer"]][rows, h // 2, :]
                    elif st["type"] == "swa":
                        q, k = qt[rows, h // 2, :], kt1[rows, h // (SWA_HEADS // KV_HEADS), :]
                    else:
                        q, k = aq[:, h, :], ak[:, h, :]
                    pe.wait_ge(S["t_act"], st["at"]["t_act"])
                    for t, c0, n in segments(st["type"]):
                        ins = pe.matmul(bank[6][:, c0:c0 + n], q[:, t * P:(t + 1) * P], k[:, 0:n], start=True, stop=True)
                    ins.then_inc(S["full6"], 1)
                elif kind == "values":
                    hd = st["head"]
                    h = hd["h"]
                    take_bank(7, st["use7"])
                    pe.wait_ge(S["t_act"], st["batch"]["act"])
                    rows = slice(DH * (h % 2), DH * (h % 2) + DH)
                    if hd["type"] == "mem":
                        buf, c0, n = mkv[hd["layer"]], MEM_HEADS * DH + DH * h, DH
                    elif hd["type"] == "swa":
                        buf, c0, n = kvn, KV_HEADS * DH + DH * (h // (SWA_HEADS // KV_HEADS)), DH
                    else:
                        buf, c0, n, rows = av, h * P, P, slice(0, P)
                    for t in range(TILES):
                        mine = [blk for blk in prob_blocks(hd["type"]) if blk[3] == t]
                        for i, (_, kt, d, _) in enumerate(mine):
                            ins = pe.matmul(bank[7][rows, t * P:(t + 1) * P], buf[:, kt, c0:c0 + n],
                                            pt_buf(hd)[:, d:d + P], start=i == 0, stop=i == len(mine) - 1)
                    ins.then_inc(S["values_done"], 1)
                elif kind == "bias_rows":
                    take_bank(6, st["use6"])
                    pe.wait_ge(S["block2_in"], 48)
                    pe.matmul(bank[6][0:H2, 0:384], tab[0:BUCKETS + 1, :], hot[0:BUCKETS + 1, :], start=True, stop=True
                              ).then_inc(S["full6"], 1)
                elif kind == "level":
                    l, j, bk = st["l"], st["j"], bank[st["bank"]]
                    take_bank(st["bank"], st["use"])
                    if l == 0:
                        pe.wait_ge(S["t_act"], st["at"]["t_act"])
                        pe.wait_ge(S["forget_ready"], j + 1)
                    else:
                        pe.wait_ge(S[f"free{st['scaled'][0]}"], st["scaled"][1])
                    if l <= len(LEVELS):
                        blocks = [(2 * j + i // 2, slice(i % 2 * P, (i % 2 + 1) * P), slice(i % 2 * P, (i % 2 + 1) * P))
                                  for i in range(4)]
                    else:
                        blocks = [(2 * j + i, slice(0, P), slice(P, SEQ)) for i in (0, 1)]
                    for i, (h, keys, queries) in enumerate(blocks):
                        ins = pe.matmul(bk[:, i * P:(i + 1) * P], k2[:, h, keys], q2[:, h, queries], start=True, stop=True)
                    ins.then_inc(S[f"full{st['bank']}"], 1)
                elif kind == "hg_out":
                    take_bank(st["bank"], st["use"])
                    pe.wait_ge(S["evac_act"], pl.group_of["w2", 5]["done"])
                    pe.wait_ge(S["free6"], last_level[6])
                    pe.wait_ge(S["free7"], last_level[7])
                    for i in range(4):
                        h = 4 * st["q"] + i
                        sums, vs = bank[st["bank"]][:, i * P:(i + 1) * P], slice(h * P, (h + 1) * P)
                        if st["t"] == 0:
                            ins = pe.matmul(sums, att[:, h, 0, :], v2[:, 0, vs], start=True, stop=True)
                        else:
                            pe.matmul(sums, attx[:, h, :], v2[:, 0, vs], start=True, stop=False)
                            ins = pe.matmul(sums, att[:, h, 1, :], v2[:, 1, vs], start=False, stop=True)
                    ins.then_inc(S[f"full{st['bank']}"], 1)

        @block.vector
        def _(dve):
            chain = [0]

            def tick(ins):
                ins.then_inc(S["dve_chain"], 1)
                chain[0] += 1

            def link(ins):
                tick(ins)
                dve.wait_ge(S["dve_chain"], chain[0])

            for st in steps:
                kind = st["kind"]
                if kind == "gains":
                    dve.wait_ge(S["full6"], 1)
                    dve.tensor_copy(gt[:, 0:N_GAINS], bank[6][:, 0:N_GAINS]).then_inc(S["free6"], 1)
                    dve.wait_ge(S["free6"], 1)
                    c0, c1 = GAIN_ROWS["lb0"][0], GAIN_ROWS["lb1"][0]
                    dve.tensor_tensor(lb[:, 1, :], gt[:, c0:c0 + H2], gt[:, c1:c1 + H2], ALU.subtract
                                      ).then_inc(S["lb_ready"], 1)
                    dve.wait_ge(S["lb_ready"], 2)
                    link(dve.tensor_scalar(lb[:, 1, :], lb[:, 0, :], -1.0, 1.0, ALU.mult, ALU.add))
                elif kind == "split":
                    u = st["unit"]
                    i = u["index"]
                    n = u["kn"] * u["w"]
                    dve.wait_ge(S["w_hi_ready"], i + 1)
                    dve.tensor_tensor(w_lo[:, i % PART_SLOTS, 0:n], raw[:, i % RAW_SLOTS, 0:n],
                                      w_hi[:, i % PART_SLOTS, 0:n].bitcast(F32), ALU.subtract
                                      ).then_inc(S["w_lo_ready"], 1)
                elif kind == "batch" and st["batch"]["how"] == "split":
                    b = st["batch"]
                    dve.wait_ge(S["t_act"], b["act"])
                    for i in (0, 1):
                        hi = at_hi[:, b["dst"] + i, :].bitcast(F32)
                        scale = gt[:, b["gains"][i]:b["gains"][i] + 1] if b["gains"] else 1.0
                        ins = dve.scalar_tensor_tensor(at_lo[:, b["dst"] + i, :], t_bank(b)[:, i * SEQ:(i + 1) * SEQ],
                                                       scale, hi, ALU.mult, ALU.subtract)
                    ins.then_inc(S["t_dve"], 1)
                elif kind == "batch" and st["batch"]["how"] == "forget":
                    b = st["batch"]
                    dve.wait_ge(S["t_act"], b["act"])
                    for h in (b["dst"][1], b["dst"][1] + 1):
                        dve.tensor_scalar(f2[:, h, :], f2[:, h, :], lb[:, 1, h:h + 1], lb[:, 0, h:h + 1], ALU.mult, ALU.add)
                        ins = dve.tensor_scalar(k2[:, h, :], k2[:, h, :], lb[:, 1, h:h + 1], None, ALU.mult)
                    ins.then_inc(S["forget_ready"], 1)
                elif kind == "evac" and st["group"]["how"] == "res":
                    g = st["group"]
                    dve.wait_ge(S["unit_used"], g["last_unit"])
                    dve.wait_ge(S["squares_summed"], st["at"]["stats"])
                    dve.wait_ge(S["t_full"], st["at"]["t_full"])
                    if st["at"].get("evac_dve"):
                        dve.wait_ge(S["evac_dve"], st["at"]["evac_dve"])
                    for t in range(TILES):
                        xs = x[:, t, g["n0"]:g["n0"] + NCOL]
                        ins = dve.tensor_tensor(xs, xs, acc(g, t)[:], ALU.add)
                    ins.then_inc(S["evac_dve"], 1)
                elif kind == "evac" and st["group"]["how"] == "gate":
                    g = st["group"]
                    branch = 0 if g["gemm"] == "bhg" else 1
                    cols = slice(g["n0"], g["n0"] + NCOL)
                    dve.wait_ge(S["unit_used"], g["last_unit"])
                    dve.wait_ge(S["gates_ready"], 1)
                    for t in range(TILES):
                        ins = dve.tensor_tensor(gate[:, branch, t, cols], gate[:, branch, t, cols], acc(g, t)[:], ALU.mult)
                    if branch:
                        link(ins)
                        ins = dve.tensor_tensor(gate[:, 0, :, cols], gate[:, 0, :, cols], gate[:, 1, :, cols], ALU.add)
                    ins.then_inc(S["evac_dve"], 1)
                elif kind == "evac" and st["group"]["how"] in ("ffg", "ffu"):
                    g = st["group"]
                    n, w, r = st["n"], g["w"], rstd_col("ffg")
                    buf = hs2[:, (n - 1) % 2]
                    if g["how"] == "ffg":
                        dve.wait_ge(S["sigmoid_ready"], n)
                        if n > 2:
                            dve.wait_ge(S["t_full"], pl.hs_last["g", n - 2])
                        else:
                            settle(dve, st)
                    else:
                        dve.wait_ge(S["unit_used"], g["last_unit"])
                        dve.wait_ge(S["evac_dve"], g["done"] - 1)
                    for t in range(TILES):
                        other = sig2[:, t, 0:w] if g["how"] == "ffg" else buf[:, t, 0:w]
                        ins = dve.scalar_tensor_tensor(buf[:, t, 0:w], acc(g, t)[:, 0:w], col(r + t), other,
                                                       ALU.mult, ALU.mult)
                    ins.then_inc(S["evac_dve"], 1)
                elif kind == "headnorm":
                    src, heads, n = natural[st["src"]], st["heads"], st["n"]
                    cols = slice(st["off"] * DH, (st["off"] + heads) * DH)
                    wait(dve, st["need"])
                    settle(dve, st)
                    if n > 1:
                        dve.wait_ge(S["head_rstd"], n - 1)
                    for t in range(TILES):
                        link(dve.tensor_tensor(square[:, 0:heads * DH], src[:, t, cols], src[:, t, cols], ALU.mult))
                        ins = dve.tensor_reduce(col(HSS + t * heads, heads),
                                                square[:, 0:heads * DH].rearrange("p (h d) -> p h d", d=DH), AX_X, ALU.add)
                        if t == 0:
                            link(ins)
                    ins.then_inc(S["head_squares"], 1)
                    dve.wait_ge(S["head_rstd"], n)
                    for t in range(TILES):
                        s_ = src[:, t, cols].rearrange("p (h d) -> p h d", d=DH)
                        r_ = col(HR + t * heads, heads).unsqueeze(2).to_broadcast([P, heads, DH])
                        if src is kvn:
                            both = [P, heads, 2, DH]
                            ins = dve.tensor_tensor(kdup[:, t], s_.unsqueeze(2).to_broadcast(both),
                                                    r_.unsqueeze(2).to_broadcast(both), ALU.mult)
                        else:
                            ins = dve.tensor_tensor(s_, s_, r_, ALU.mult)
                    ins.then_inc(S["head_normed"], 1)
                elif kind in ("headnorm2", "hg_norm"):
                    n_h = 4 if kind == "headnorm2" else H2
                    src = nat2[:, st["slot"]] if kind == "headnorm2" else oh
                    dve.wait_ge(S["head_rstd"], st["n"])
                    for t in range(TILES):
                        s_ = src[:, t, :].rearrange("p (h d) -> p h d", d=P)
                        r_ = col(HR + t * n_h, n_h).unsqueeze(2).to_broadcast([P, n_h, P])
                        ins = dve.tensor_tensor(s_, s_, r_, ALU.mult)
                    ins.then_inc(S["head_normed"], 1)
                elif kind == "hg_gate":
                    cols = slice(st["half"] * NCOL, (st["half"] + 1) * NCOL)
                    dve.wait_ge(S["hg_sig"], st["n"])
                    dve.wait_ge(S["head_normed"], st["at"]["headnorm"])
                    link(dve.tensor_tensor(oh[:, :, cols], oh[:, :, cols], nat2[:, st["slot"]], ALU.mult))
                    dve.tensor_tensor(oh[:, :, cols], oh[:, :, cols], sgt[:], ALU.mult).then_inc(S["hg_gated"], 1)
                elif kind == "pool_diff":
                    s = 2 * (st["gi"] % 2)
                    dve.wait_ge(S["full6"], st["at"]["full6"])
                    if st["gi"] > 1:
                        dve.wait_ge(S["full7"], st["gi"] - 1)
                    dve.tensor_copy(dt[:, s, :], bank[6][:, 0:SEQ])
                    dve.tensor_copy(dt[0:PG - P, s + 1, :], bank[6][0:PG - P, SEQ:2 * SEQ]).then_inc(S["free6"], 1)
                elif kind == "pool_mix":
                    dve.wait_ge(S["hi7"], st["hi7"])
                    for i, (c0, c1, rows, ch) in enumerate(pool_pieces(st["gi"])):
                        gc = GAIN_ROWS["pool"][0] + ch
                        ins = dve.scalar_tensor_tensor(at_lo[rows, 8 + ch, :], bank[7][rows, i * SEQ:(i + 1) * SEQ],
                                                       gt[rows, gc:gc + 1], at_hi[rows, 8 + ch, :].bitcast(F32),
                                                       ALU.mult, ALU.subtract)
                    ins.then_inc(S["free7"], 1)
                elif kind == "values" and st["close"]:
                    c = st["chunk"]
                    dve.wait_ge(S["hi7"], st["hi7"])
                    dve.scalar_tensor_tensor(at_lo[:, c, :], bank[7][:, 0:SEQ], 1.0, at_hi[:, c, :].bitcast(F32),
                                             ALU.mult, ALU.subtract).then_inc(S["free7"], 1)
                elif kind == "scores":
                    kd, buf, s = st["type"], scores_buf(st), (st["a"] - 1) % 3
                    dve.wait_ge(S["full6"], st["full6"])
                    if st["a"] > 3:
                        dve.wait_ge(S["t_full"], pl.prob_batch[st["a"] - 3])
                    if kd == "mem":
                        ins = dve.tensor_copy(buf[:, 0:512], bank[6][:, 0:512])
                    elif kd == "swa":
                        dve.wait_ge(S["swa_in"], 16)
                        slope = 2.0 ** (-8.0 * (st["h"] + 1) / SWA_HEADS)
                        ins = dve.scalar_tensor_tensor(buf[:, 0:384], dist[:], -slope * DH ** 0.5, bank[6][:, 0:384],
                                                       ALU.mult, ALU.add)
                    else:
                        dve.wait_ge(S["bias_in"], 16)
                        for t, c0, m in segments(kd):
                            ins = dve.scalar_tensor_tensor(buf[:, c0:c0 + m], bank[6][:, c0:c0 + m], P ** -0.5,
                                                           ebias[:, st["h"], m - 1::-1], ALU.mult, ALU.add)
                    ins.then_inc(S["free6"], 1)
                    dve.wait_ge(S["free6"], st["use6"])
                    for i, (t, c0, m) in enumerate(segments(kd)):
                        ins = dve.tensor_reduce(col(AM + 2 * s + i), buf[:, c0:c0 + m], AX_X, ALU.max)
                    link(ins)
                    scale = 1.0 if kd == "moba" else DH ** -0.5
                    if kd == "swa":
                        dve.wait_ge(S["sink_in"], 16)
                        link(dve.tensor_scalar(col(AM + 2 * s, 2), col(AM + 2 * s, 2), scale, sink[:, st["h"]:st["h"] + 1],
                                               ALU.mult, ALU.max))
                        scale = 1.0
                    dve.tensor_scalar(col(AN + 2 * s, 2), col(AM + 2 * s, 2), -scale, None, ALU.mult
                                      ).then_inc(S["bias_neg"], 1)
                elif kind == "normalise":
                    hd = st["head"]
                    buf, s = scores_buf(hd), (hd["a"] - 1) % 3
                    dve.wait_ge(S["probs_raw"], hd["a"])
                    if hd["type"] == "swa":
                        link(dve.tensor_tensor(col(AL + 2 * s, 2), col(AL + 2 * s, 2), col(AE + 2 * s, 2), ALU.add))
                    link(dve.reciprocal(col(AR + 2 * s, 2), col(AL + 2 * s, 2)))
                    for i, (t, c0, m) in enumerate(segments(hd["type"])):
                        ins = dve.tensor_scalar(buf[:, c0:c0 + m], buf[:, c0:c0 + m], col(AR + 2 * s + i), None, ALU.mult)
                    ins.then_inc(S["probs_ready"], 1)
                elif kind == "bias_rows":
                    dve.wait_ge(S["full6"], st["full6"])
                    dve.tensor_copy(rrow[0:H2, :], bank[6][0:H2, 0:384]).then_inc(S["free6"], 1)
                elif kind == "level":
                    l, pair = st["l"], slice(2 * st["j"], 2 * st["j"] + 2)
                    dve.wait_ge(S[f"full{st['bank']}"], st["full"])
                    attn = att[:, pair].rearrange("p h t n -> p (h t) n")
                    product = bank[st["bank"]][:].rearrange("p (b n) -> p b n", n=P)
                    if l == 0:
                        dve.wait_ge(S["block2_in"], 48)
                        link(dve.tensor_tensor(attn, product, ident[:].unsqueeze(1).to_broadcast([P, 4, P]), ALU.mult))
                        ins = dve.tensor_tensor(q2[:, pair], q2[:, pair], f2[:, pair], ALU.mult)
                    elif l <= len(LEVELS):
                        half = LEVELS[l - 1]
                        nb = SEQ // half
                        tick(dve.copy_predicated(attn, lmask[:, l - 1].bitcast(I32).unsqueeze(1).to_broadcast([P, 4, P]), product))
                        cur, nxt = (f2, f2b) if l % 2 else (f2b, f2)
                        f_ = cur[:, pair].rearrange("p h n -> p (h n)")[:, 0:2 * nb].rearrange("p (b two) -> p b two", two=2)
                        q_ = q2[:, pair].rearrange("p h (b two n) -> p (h b) two n", two=2, n=half)
                        k_ = k2[:, pair].rearrange("p h (b two n) -> p (h b) two n", two=2, n=half)
                        dve.wait_ge(S["dve_chain"], chain[0])
                        dve.tensor_tensor(q_[:, :, 1, :], q_[:, :, 1, :], f_[:, :, 0:1].to_broadcast([P, nb, half]), ALU.mult)
                        dve.tensor_tensor(k_[:, :, 0, :], k_[:, :, 0, :], f_[:, :, 1:2].to_broadcast([P, nb, half]), ALU.mult)
                        ins = dve.tensor_tensor(nxt[:, pair].rearrange("p h n -> p (h n)")[:, 0:nb], f_[:, :, 0], f_[:, :, 1],
                                                ALU.mult)
                    else:
                        ins = dve.tensor_copy(attx[:, pair].rearrange("p h n -> p (h n)"), bank[st["bank"]][:, 0:2 * P])
                    ins.then_inc(S[f"free{st['bank']}"], 1)
                    dve.wait_ge(S[f"free{st['bank']}"], st["use"])
                elif kind == "hg_out":
                    dve.wait_ge(S[f"full{st['bank']}"], st["full"])
                    dve.tensor_copy(oh[:, st["t"], st["q"] * NCOL:(st["q"] + 1) * NCOL], bank[st["bank"]][:]
                                    ).then_inc(S[f"free{st['bank']}"], 1)


def shape_constants():
    p, c = np.arange(P)[:, None], np.arange(384)[None, :]
    pool = np.zeros((P, len(WINDOWS), 384), np.float32)
    s, t = np.arange(SEQ)[:, None], np.arange(SEQ)[None, :]
    for i, w in enumerate(WINDOWS):
        m = ((t - s >= 0) & (t - s < w)) / np.minimum(t + 1, w) - (t == s)
        pool[:, i, 0:SEQ] = m[0:P]
        pool[:, i, SEQ:] = m[P:, P:]
    d = np.where(c < P, p - c, p + P - (c - P))
    dist = np.where((d >= 0) & (d < P), d, 1.0e30).astype(np.float32)
    n = np.arange(384) - (P - 1)
    nf = np.maximum(n, 1).astype(np.float32)
    large = 16 + (np.log(nf / 16).astype(np.float32) / np.float32(np.log(128 / 16)) * np.float32(16)).astype(np.int32)
    bucket = np.where(n < 16, n, np.minimum(large, BUCKETS - 1))
    hot = np.zeros((BUCKETS + 1, 384), np.float32)
    for j in range(384):
        hot[bucket[j] if n[j] >= 0 else BUCKETS, j] = 1.0
    levels = np.zeros((P, len(LEVELS), P), np.float32)
    q = np.arange(P)[None, :]
    for i, b in enumerate(LEVELS):
        levels[:, i, :] = (p // (2 * b) == q // (2 * b)) & (p % (2 * b) < b) & (q % (2 * b) >= b)
    return {"ident": np.eye(P, dtype=np.float32), "poolp": pool, "dist": dist, "hot": hot, "lmask": levels}


INPUTS = ["x", "mem", "norm_mix", "w_in", "pool_w", "pool_scale", "kv_norm", "w_kv", "k_norm", "q_norm", "sinks",
          "mem_norm", "w_mem_kv", "mem_q_norm", "mem_k_norm", "w_out", "norm_mlp", "w_up", "w_down", "attn_norm_g_2",
          "w_in_2", "hg_lb_gamma_2", "hg_out_norm_g_2", "q_norm_g_2", "k_norm_g_2", "rel_bias_table_2",
          "w_branch_hg_2", "w_branch_attn_2", "w_out_2", "ffn_norm_g_2", "w_ffn_gate_2", "w_ffn_up_2", "w_ffn_down_2"]


def kernel(**inputs):
    import concourse.bacc as bacc
    from concourse.bass_utils import run_bass_kernel_spmd

    nc = bacc.Bacc("TRN2", target_bir_lowering=False, num_devices=1)
    arrays, aps = {}, {}
    for name, v in [(n, inputs[n]) for n in INPUTS] + list(shape_constants().items()):
        v = np.ascontiguousarray(v)
        arrays[f"in_{name}"] = v
        aps[name] = nc.dram_tensor(f"in_{name}", v.shape, mybir.dt.from_np(v.dtype), kind="ExternalInput").ap()
    out = nc.dram_tensor("out_0", (1, SEQ, D), F32, kind="ExternalOutput").ap()
    scratch = nc.dram_tensor("bias_scratch", (H2, 384), F32, kind="Internal").ap()
    two_blocks_kernel(nc, aps, out, scratch)
    return run_bass_kernel_spmd(nc, [arrays], core_ids=[0]).results[0]["out_0"]
```

```python
from contextlib import ExitStack

import numpy as np

import concourse.bass as bass
from concourse import mybir

F32 = mybir.dt.float32
F32R = mybir.dt.float32r
BF16 = mybir.dt.bfloat16
I32 = mybir.dt.int32
ALU = mybir.AluOpType
ACT = mybir.ActivationFunctionType
AX_X = mybir.AxisListType.X

P = 128
SEQ = 256
TILES = SEQ // P
D = 1024
DCH = D // P
EPS = 1e-6
NEG = -1.0e30
UNIT_K = 4
NCOL = 512
UNIT = UNIT_K * NCOL
RAW_SLOTS, PART_SLOTS = 4, 3
AT_CHUNKS = 32
DH = 64
SWA_HEADS, KV_HEADS, MEM_HEADS = 12, 4, 4
WINDOWS = (2, 4, 8, 16)
PG = 192
D_FF, D_FF2 = 4096, 2816
H2 = 8
BUCKETS = 32
LEVELS = (1, 2, 4, 8, 16, 32, 64)

GAIN_ROWS = {}
_at = 0
for _name, _n in (("mix0", 8), ("mix1", 8), ("kv", 8), ("mem0", 8), ("mem1", 8), ("mlp0", 8), ("mlp1", 8),
                  ("attn2", 8), ("ffn2", 8), ("lb0", 8), ("lb1", 8), ("pool", 6), ("hg", 1), ("q2", 1), ("k2", 1),
                  ("k", 1), ("q", 1), ("mq0", 1), ("mq1", 1), ("mk0", 1), ("mk1", 1)):
    GAIN_ROWS[_name] = (_at, _n)
    _at += _n
N_GAINS = _at

GEMMS = {
    "mem0": (8, 512, 16, "nat"), "in0": (8, 1024, 0, "nat"), "mem1": (8, 512, 24, "nat"),
    "out0": (8, 1024, 8, "res"),
    "kv": (8, 512, 16, "nat"), "in1": (8, 1024, 0, "nat"), "out1": (8, 1024, 8, "res"),
    "w2": (8, 9216, 0, "w2"), "bhg": (8, 1024, 0, "gate"), "bat": (8, 1024, 8, "gate"),
    "out2": (8, 1024, 0, "res"),
    "ffg": (8, D_FF2, 0, "ffg"), "ffu": (8, D_FF2, 0, "ffu"), "down2": (22, 1024, 8, "res"),
}
for _l in (0, 1):
    for _h in (0, 1):
        GEMMS[f"up{_l}{_h}"] = (8, D_FF // 2, 0, "relu")
        GEMMS[f"down{_l}{_h}"] = (16, 1024, None, "res")


def h_slot(c):
    return 8 + c % (AT_CHUNKS - 8)


class Plan:

    def __init__(self):
        self.steps, self.units, self.groups, self.batches = [], [], [], []
        self.count = {}
        self.group_of = {}
        self.hs_last = {}
        self.prob_batch = {}

    def tick(self, name):
        self.count[name] = self.count.get(name, 0) + 1
        return self.count[name]

    def now(self, name):
        return self.count.get(name, 0)

    def add(self, kind, **st):
        st["kind"] = kind
        st["at"] = dict(self.count)
        self.steps.append(st)
        return st

    def mm(self, gemm, ng, kq, need=(), between=()):
        kch, cols, base, how = GEMMS[gemm]
        g = self.group_of.get((gemm, ng))
        if g is None:
            n0 = ng * NCOL
            g = dict(gemm=gemm, ng=ng, n0=n0, w=min(NCOL, cols - n0), kch=kch, how=how, index=len(self.groups),
                     engine="dve" if how in ("res", "gate", "ffg", "ffu") else "act", chunks=0)
            g["free"] = {e: sum(o["engine"] == e for o in self.groups[:-1]) for e in ("act", "dve")}
            self.groups.append(g)
            self.group_of[gemm, ng] = g
        first = kq * UNIT_K
        u = dict(index=len(self.units), gemm=gemm, k0=first, kn=min(UNIT_K, kch - first), n0=g["n0"], w=g["w"])
        self.units.append(u)
        g["last_unit"] = u["index"] + 1
        for k in range(u["kn"]):
            self.add("mm", unit=u, group=g, k=k, need=list(need) if k == 0 else [], start=g["chunks"] == 0,
                     stop=g["chunks"] == kch - 1)
            g["chunks"] += 1
            if k < len(between) and between[k]:
                between[k]()

    def evac(self, gemm, ng, **more):
        g = self.group_of[gemm, ng]
        self.add("evac", group=g, **more)
        g["done"] = self.tick("evac_" + g["engine"])
        return ("evac_" + g["engine"], g["done"])

    def batch(self, src, dst, how, need, gains=None, scale=None, head=None, more=()):
        b = dict(index=len(self.batches), src=src, dst=dst, how=how, need=need, gains=gains, scale=scale, head=head,
                 splits=[(dst, gains), *more])
        b["act"] = self.tick("t_act")
        b["dve"] = self.tick("t_dve") if how == "split" else self.now("t_dve")
        if len(self.batches) >= 2:
            o = self.batches[-2]
            b["free"] = ("t_dve", o["dve"]) if o["how"] == "split" else ("t_act", o["act"])
        self.batches.append(b)
        self.tick("t_full")
        self.add("batch", batch=b)
        return b

    def split_ready(self):
        return ("t_dve", self.now("t_dve"))


def build_plan():
    pl = Plan()

    def col_of(gain, c=0):
        return GAIN_ROWS[gain][0] + c

    def turn(src, c, dst, need, gain=None, one_gain=False, also=()):
        def cols(g):
            return None if g is None else (col_of(g),) * 2 if one_gain else (col_of(g, c), col_of(g, c + 1))
        return lambda: pl.batch([(src, c), (src, c + 1)], dst + c, "split", need, gains=cols(gain),
                                more=[(d + c, cols(g)) for d, g in also])

    def plain(src, c, dst, need, gain=None, scale=None, how="plain"):
        return lambda: pl.batch([(src, c), (src, c + 1)], dst, how, need, gains=(col_of(gain),) * 2 if gain else None,
                                scale=scale)

    def stats(name, src, need):
        pl.tick("stats")
        pl.add("stats", n=pl.now("stats"), src=src, name=name, need=need)

    def head_squares(src, heads, need, off=0):
        n = pl.tick("headnorm")
        st = dict(n=n, src=src, heads=heads, off=off, need=need)
        pl.add("head_squares", **st)
        return lambda: (pl.tick("head_scaled"), pl.add("head_scale", **st)), ("head_normed", n)

    def scores(kind, h, **more):
        hd = dict(a=pl.tick("head"), type=kind, h=h, use6=pl.tick("use6"), full6=pl.tick("full6"), **more)
        pl.add("scores", head=hd)
        return hd

    def turn_probs(hd):
        pl.add("normalise", head=hd)
        hd["batch"] = pl.batch(None, None, "probs", ("probs_ready", hd["a"]), head=hd)
        pl.prob_batch[hd["a"]] = hd["batch"]["index"] + 1

    def values(hd, close, chunk):
        if hd["type"] == "moba" or not close:
            values.use7 = pl.tick("use7")
        hi7 = pl.tick("hi7") if close else 0
        pl.tick("values")
        pl.add("values", head=hd, batch=hd["batch"], use7=values.use7, close=close, chunk=chunk, hi7=hi7)

    def head_steps(kind, hs, chunk_of, layer=0):
        live = []
        for i in range(len(hs) + 3):
            def ahead(i=i):
                if i < len(hs):
                    live.append(scores(kind, hs[i], layer=layer))
                if 2 <= i < len(hs) + 2:
                    turn_probs(live[i - 2])

            def behind(i=i):
                if i < len(hs):
                    pl.add("softmax", head=live[i])
                if i >= 3:
                    values(live[i - 3], kind == "moba" or i % 2 == 0, chunk_of(hs[i - 3]))
            yield ahead
            yield behind

    def woven_mm(order, steps):
        steps = list(steps)
        total = sum(min(UNIT_K, GEMMS[gm][0] - kq * UNIT_K) for gm, _, kq, _ in order)
        at = 0

        def upto(n):
            nonlocal at
            while at < n and at < len(steps):
                steps[at]()
                at += 1
        seen = 0
        for gm, ng, kq, need in order:
            kn = min(UNIT_K, GEMMS[gm][0] - kq * UNIT_K)
            pl.mm(gm, ng, kq, need() if callable(need) else need,
                  between=[lambda n=seen + k + 1: upto(n * len(steps) // total) for k in range(kn)])
            seen += kn
        upto(len(steps))

    def pair(gemm, need, late=(), first_x=None, skip=(), late_from=1):
        n = -(-GEMMS[gemm][0] // UNIT_K)
        ready = None
        for kq in range(n):
            if kq in skip:
                continue
            pl.mm(gemm, 0, kq, [r for r in (need if kq == 0 or kq - 1 in skip else None, ready) if r],
                  between=[None] * late_from + list(late) if kq == 0 else ())
            if kq == 0 and late:
                ready = pl.split_ready()
            if kq == n - 1:
                done0 = pl.evac(gemm, 0)
                turns = first_x(done0) if first_x else []
            else:
                turns = []
            pl.mm(gemm, 1, kq, between=[None] + turns)
        return pl.split_ready(), pl.evac(gemm, 1)

    evens = (0, 2, 4, 6)

    pl.add("gains", use6=pl.tick("use6"))
    pl.tick("full6")
    gains = ("free6", 1)
    for c in evens:
        turn("mem", c, 16, gains, "mem0", also=[(24, "mem1")])()
    stats("mem", "mem", ("mem_in", 16))
    r = pl.split_ready()
    pl.mm("mem0", 0, 0, [r], between=[turn("x", c, 0, gains, "mix0") for c in evens])
    r = pl.split_ready()
    stats("x0", "x", ("x_in", 16))
    pl.mm("mem0", 0, 1)
    kv_done = pl.evac("mem0", 0)
    scale_k, k_normed = head_squares("mkv0", 4, kv_done)
    pl.mm("in0", 1, 0, [r])
    scale_k()
    pl.mm("in0", 1, 1)
    hi_done = pl.evac("in0", 1)
    scale_q, q_normed = head_squares("nat", 4, hi_done, off=12)
    pl.mm("in0", 0, 0, between=[None, plain("mkv0", 0, ("mkt0", 0), k_normed, "mk0"), None, scale_q])
    pl.mm("in0", 0, 1, between=[None, None, plain("nat", 6, ("qt", 6), q_normed, "mq0")])
    lo_done = pl.evac("in0", 0)

    pool_use = {}

    def pool_group(gi):
        def diff():
            pl.tick("full6")
            pool_use[gi] = pl.tick("use6")
            pl.add("pool_diff", gi=gi, use6=pool_use[gi], need=lo_done, full6=pl.now("full6"))

        def mix():
            pl.tick("full7")
            pl.tick("hi7")
            pl.add("pool_mix", gi=gi, use7=pl.tick("use7"), hi7=pl.now("hi7"), full7=pl.now("full7"),
                   diff=pool_use[gi])
        return diff, mix
    woven_mm([("mem1", 0, 0, ()), ("mem1", 0, 1, ())], head_steps("mem", range(4), lambda h: 14 + h // 2, 0))
    kv_done = pl.evac("mem1", 0)
    scale_k, k_normed = head_squares("mkv1", 4, kv_done)
    pools = [pool_group(gi) for gi in range(4)]
    for gi in range(4):
        pools[gi][0]()
        if gi:
            pools[gi - 1][1]()
    woven_mm([("out0", 0, 0, [("free7", pl.now("use7"))])],
             [pools[3][1], scale_k, plain("mkv1", 0, ("mkt1", 0), k_normed, "mk1")])
    mix = ("free7", pl.now("use7"))

    def mlp(l, first, done1, gain, first_x):
        stats(gain, "x", done1)
        for half in (0, 1):
            up, down = f"up{l}{half}", f"down{l}{half}"

            def finish(ng):
                n = pl.tick("squares")
                pl.evac(up, ng, hs=n)
                return ng, n

            def turns(ng, n):
                def go(pr):
                    b = pl.batch([(("hs", (n - 1) % 2), pr), (("hs", (n - 1) % 2), pr + 1)],
                                 h_slot(half * 16 + ng * 4 + pr), "split", ("squared", n))
                    pl.hs_last[n] = b["index"] + 1
                return [lambda: go(0), None, lambda: go(2)]
            if half == 0:
                pl.mm(up, 0, 0, [first], between=[None, turn("x", 4, 0, done1, gain), turn("x", 6, 0, done1, gain)])
                r = pl.split_ready()
                pl.mm(up, 1, 0)
                pl.mm(up, 0, 1, [r])
                last = finish(0)
                pl.mm(up, 1, 1)
                now = finish(1)
                pl.mm(up, 2, 0, between=turns(*last))
                pl.mm(up, 2, 1, between=turns(*now))
                last = finish(2)
                rest = (3,)
            else:
                last, rest = None, (0, 1, 2, 3)
            for ng in rest:
                pl.mm(up, ng, 0)
                pl.mm(up, ng, 1, between=turns(*last) if last else ())
                last = finish(ng)
            pl.mm(down, 0, 0, [pl.split_ready()])
            pl.mm(down, 1, 0, between=turns(*last))
            ready = pl.split_ready()
            for kq in (1, 2):
                pl.mm(down, 0, kq)
                pl.mm(down, 1, kq)
            pl.mm(down, 0, 3, [ready])
            done0 = pl.evac(down, 0)
            pl.mm(down, 1, 3, between=[None] + first_x(done0) if half else ())
            first, done1 = pl.split_ready(), pl.evac(down, 1)
        return first, done1

    def first_half(gain, dst=0, also=()):
        return lambda done0: [turn("x", c, dst, done0, gain, also=also) for c in (0, 2)]

    pl.mm("out0", 1, 0)
    pl.mm("out0", 0, 1, [mix])
    done0 = pl.evac("out0", 0)
    pl.mm("out0", 1, 1, between=[None] + first_half("mlp0")(done0))
    first, done1 = pl.split_ready(), pl.evac("out0", 1)
    first, done1 = mlp(0, first, done1, "mlp0", first_half("kv", 16, [(0, "mix1")]))

    stats("mix1", "x", done1)
    pl.mm("kv", 0, 0, [first], between=[None] + [turn("x", c, 16, done1, "kv", also=[(0, "mix1")]) for c in (4, 6)])
    r = pl.split_ready()
    pl.mm("in1", 1, 0)
    pl.mm("kv", 0, 1, [r])
    kv_done = pl.evac("kv", 0)
    scale_k, k_normed = head_squares("kvn", 4, kv_done)
    pl.mm("in1", 1, 1, between=[None, None, scale_k])
    hi_done = pl.evac("in1", 1)
    scale_q, q_normed = head_squares("nat", 8, hi_done, off=8)
    dups = [plain("kdup", pr, ("kt1", pr), k_normed, "k") for pr in (0, 2)]
    pl.mm("in1", 0, 0, between=[dups[0], dups[1], None, scale_q])
    qs = [plain("nat", 6, ("qt", 6), q_normed, "mq1"), plain("nat", 4, ("qt", 4), q_normed, "q")]
    steps = list(head_steps("mem", range(4), lambda h: 14 + h // 2, 1))
    woven_mm([("in1", 0, 1, ())], [qs[0], qs[1]] + steps[:4])
    lo_done = pl.evac("in1", 0)
    for st in steps[4:6]:
        st()
    scale_q, q_normed = head_squares("nat", 8, lo_done, off=0)
    for st in steps[6:8]:
        st()
    scale_q()
    for st in steps[8:]:
        st()
    steps = list(head_steps("swa", range(8, 12), lambda h: 8 + h // 2))
    for st in steps[:2]:
        st()
    plain("nat", 0, ("qt", 0), q_normed, "q")()
    plain("nat", 2, ("qt", 2), q_normed, "q")()
    for st in steps[2:]:
        st()
    upper = ("free7", pl.now("use7"))
    woven_mm([("out1", 0, 1, [upper]), ("out1", 1, 1, ())], head_steps("swa", range(8), lambda h: 8 + h // 2))
    mix = ("free7", pl.now("use7"))
    pl.mm("out1", 0, 0, [mix])
    done0 = pl.evac("out1", 0)
    pl.mm("out1", 1, 0, between=[None] + first_half("mlp1")(done0))
    first, done1 = pl.split_ready(), pl.evac("out1", 1)
    first, done1 = mlp(1, first, done1, "mlp1", first_half("attn2"))

    stats("attn2", "x", done1)
    pl.add("second_block")
    todo = []

    def run(n=1):
        while n and todo:
            step = todo.pop(0)
            if step:
                step()
                n -= 1
    uses = {}

    def level(l, j):
        k = 6 + (4 * l + j) % 2
        use, full = pl.tick(f"use{k}"), pl.tick(f"full{k}")
        uses[l, j] = (k, use)
        pl.add("level", l=l, j=j, bank=k, use=use, full=full, scaled=uses.get((l - 1, j)))

    def out_heads(q, t):
        k = 6 + t
        pl.tick(f"full{k}")
        pl.add("hg_out", q=q, t=t, bank=k, use=pl.tick(f"use{k}"), full=pl.now(f"full{k}"))

    def bias_rows():
        pl.tick("full6")
        pl.add("bias_rows", use6=pl.tick("use6"), full6=pl.now("full6"))

    def hg_norm():
        pl.add("hg_norm", n=pl.tick("headnorm"))
        pl.tick("head_scaled")

    def after_group(ng, need):
        nat2 = ("nat2", ng % 2)
        half, sec = ng % 2, ng // 2
        if sec == 0:
            todo.extend(plain(nat2, pr, ("q2", 4 * half + pr), need, scale=P ** -0.5) for pr in (0, 2))
        elif sec == 1:
            todo.extend(plain(nat2, pr, ("f2", 4 * half + pr), need, how="forget") for pr in (0, 2))
        elif sec == 2 and half:
            todo.append(bias_rows)
            for l in range(len(LEVELS) + 2):
                for j in range(4):
                    todo.append(lambda l=l, j=j: level(l, j))
            for q in (0, 1):
                for t in (0, 1):
                    todo.append(lambda q=q, t=t: out_heads(q, t))
            todo.append(hg_norm)
        elif sec in (3, 4):
            norm = dict(n=0)

            def squares():
                norm["n"] = pl.tick("headnorm")
                pl.add("head_squares2", n=norm["n"], slot=ng % 2, need=need)

            def scale():
                pl.tick("head_scaled")
                pl.add("head_scale2", n=norm["n"], slot=ng % 2)
            nm, g = ("aq", "q2") if sec == 3 else ("ak", "k2")
            todo[1:1] = [squares]
            todo[4:4] = [scale]
            todo[5:5] = [lambda pr=pr: plain(nat2, pr, (nm, 4 * half + pr), ("head_normed", norm["n"]), g)()
                         for pr in (0, 2)]
        elif sec == 6:
            todo.append(lambda: pl.add("hg_gate", slot=ng % 2, half=half, n=pl.tick("hg_gate"), need=need))
        if ng == 13:
            todo.append(lambda: pl.add("bias_tiles"))
            todo.append(None)
            todo.extend(head_steps("moba", list(range(H2)), lambda h: 8 + h))

    pl.mm("w2", 0, 0, [first], between=[None] + [turn("x", c, 0, done1, "attn2") for c in (4, 6)])
    r = pl.split_ready()
    pl.mm("w2", 1, 0)
    for ng in range(18):
        for kq in (0, 1):
            if ng > 1 or kq:
                pl.mm("w2", ng, kq, [r], between=[run] * UNIT_K)
        while ng == 14 and None in todo:
            step = todo.pop(0)
            if step:
                step()
        after_group(ng, pl.evac("w2", ng))
    while todo:
        run()
    pl.add("gates")
    hg_done = ("hg_gated", pl.now("hg_gate"))
    for c in (0, 2):
        turn("oh", c, 0, hg_done, "hg", one_gain=True)()
    pair("bhg", pl.split_ready(), [turn("oh", c, 0, hg_done, "hg", one_gain=True) for c in (4, 6)], late_from=0)
    m_first, done1 = pair("bat", ("free7", pl.now("use7")),
                          first_x=lambda done0: [turn("gate", c, 0, done0) for c in (0, 2)])
    first, done1 = pair("out2", m_first, [turn("gate", c, 0, done1) for c in (4, 6)], first_x=first_half("ffn2"))
    stats("ffn2", "x", done1)

    def turns_g(ng, n, w, need):
        def go(pr):
            b = pl.batch([(("hs2", (n - 1) % 2), pr), (("hs2", (n - 1) % 2), pr + 1)], 8 + 4 * ng + pr, "split", need)
            pl.hs_last["g", n] = b["index"] + 1
        return [lambda: go(0), None, (lambda: go(2)) if w > 2 * P else None]
    last = None
    for ng in range(-(-D_FF2 // NCOL)):
        n = ng + 1
        if ng == 0:
            pl.mm("ffg", 0, 0, [first], between=[None] + [turn("x", c, 0, done1, "ffn2") for c in (4, 6)])
            r = pl.split_ready()
            pl.mm("ffu", 0, 0)
            pl.mm("ffg", 0, 1, [r])
        else:
            pl.mm("ffg", ng, 0)
            pl.mm("ffg", ng, 1, between=turns_g(*last))
        pl.evac("ffg", ng, n=n)
        if ng:
            pl.mm("ffu", ng, 0)
        pl.mm("ffu", ng, 1)
        last = (ng, n, min(NCOL, D_FF2 - ng * NCOL), pl.evac("ffu", ng, n=n))
    pl.mm("down2", 0, 0, [pl.split_ready()])
    pl.mm("down2", 1, 0, between=turns_g(*last))
    ready = pl.split_ready()
    for kq in (1, 2, 3, 4):
        pl.mm("down2", 0, kq, [ready])
        if kq < 4:
            pl.mm("down2", 1, kq)
    pl.mm("down2", 0, 5)
    pl.add("store", half=0, need=pl.evac("down2", 0))
    pl.mm("down2", 1, 4)
    pl.mm("down2", 1, 5)
    pl.add("store", half=1, need=pl.evac("down2", 1))

    steps, seen = [], 0
    for st in pl.steps:
        if st["kind"] == "mm":
            ahead = min(len(pl.units), st["unit"]["index"] + PART_SLOTS)
            while seen < ahead:
                steps.append(dict(kind="split", unit=pl.units[seen]))
                seen += 1
        steps.append(st)
    pl.steps = steps
    return pl


def two_blocks_kernel(nc, a, out, scratch):
    pl = build_plan()
    steps = pl.steps
    with ExitStack() as ctx:
        base = (nc.sbuf_base + 63) // 64 * 64
        room = nc.sbuf_usable_end - base - 64
        ctx.enter_context(nc.sbuf_tensor("whole_map", [P, room // 4], F32))

        def at(name, off, shape, dt=F32):
            return nc.alloc_sbuf_tensor_at(name, [P, *shape], dt, offset=base + off)

        o = 0
        raw = at("raw", o, [RAW_SLOTS, UNIT]); o += RAW_SLOTS * UNIT * 4
        w_hi = at("w_hi", o, [PART_SLOTS, UNIT], F32R); o += PART_SLOTS * UNIT * 4
        w_lo = at("w_lo", o, [PART_SLOTS, UNIT], F32R); o += PART_SLOTS * UNIT * 4
        at_hi = at("at_hi", o, [AT_CHUNKS, SEQ], F32R); o += AT_CHUNKS * SEQ * 4
        upper_hi = o - 16 * SEQ * 4
        at_lo = at("at_lo", o, [AT_CHUNKS, SEQ], F32R); o += AT_CHUNKS * SEQ * 4
        upper_lo = o - 16 * SEQ * 4
        x = at("x_res", o, [TILES, D]); o += TILES * D * 4
        ident = at("ident_sb", o, [P]); o += P * 4
        gt = at("gt", o, [112]); o += 112 * 4
        stat = at("stat", o, [248]); o += 248 * 4
        sink = at("sink_sb", o, [SWA_HEADS]); o += 64
        lb = at("lb", o, [2, H2]); o += 64
        arena = o
        sc = at("sc", o, [3, 512]); o += 3 * 512 * 4
        pt = at("pt", o, [2, 512]); o += 2 * 512 * 4
        mkv = [at(f"mkv{l}", o + 4096 * l, [TILES, 512]) for l in (0, 1)]; o += 8192
        mkt = [at(f"mkt{l}", o + 2048 * l, [2, SEQ]) for l in (0, 1)]; o += 4096
        nat = at("nat", o, [TILES, D])
        mem = at("mem_sb", o, [TILES, D])
        hs = at("hs", o, [2, TILES, NCOL]); o += 8192
        qt = at("qt", o, [8, SEQ])
        square = at("square", o, [D // 2])
        grows = at("grows", o + 4096, [P])
        kdup = at("kdup", o + 4096, [TILES, KV_HEADS, 2, DH])
        dt = at("dt", o + 2048, [4, SEQ]); o += 8192
        junk = at("junk", o, [D], BF16); o += 2048
        poolp, pwa, pwb = at("poolp_sb", o, [4, 384]), at("pwa", o + 6144, [4, PG]), at("pwb", o + 9216, [4, PG])
        dist, kvn, kt1 = at("dist_sb", o, [384]), at("kvn", o + 1536, [TILES, 512]), at("kt1", o + 5632, [4, SEQ])
        o += 12288
        assert o <= room, (o, room)
        q2, k2 = at("q2", upper_hi, [H2, SEQ]), at("k2", upper_hi + 8192, [H2, SEQ])
        gate = at("gate", upper_hi, [2, TILES, D])
        f2, f2b = at("f2", upper_lo, [H2, SEQ]), at("f2b", upper_lo + 8192, [H2, SEQ // 2])
        attx = at("attx", upper_lo + 12288, [H2, P])
        oh, pt2 = at("oh", upper_lo, [TILES, D]), at("pt2", upper_lo + 8192, [2, 512])
        sgt = at("sgt", upper_lo + 12288, [TILES, 512])
        o = arena
        v2 = at("v2", o, [TILES, D]); ebias = at("ebias", o, [H2, SEQ]); sig2 = at("sig2", o, [TILES, NCOL]); o += 8192
        att = at("att", o, [H2, TILES, P]); sc2 = at("sc2", o, [3, 512]); o += 8192
        aq = at("aq", o, [H2, SEQ]); o += 8192
        ak = at("ak", o, [H2, SEQ])
        rrow, hot, tab = at("rrow", o, [384]), at("hot_sb", o + 1536, [384]), at("tab_sb", o + 3072, [H2]); o += 8192
        av = at("av", o, [TILES, D]); o += 8192
        nat2 = at("nat2", o, [2, TILES, NCOL]); hs2 = at("hs2", o, [2, TILES, NCOL]); o += 8192
        junk2 = at("junk2", o, [D], BF16); o += 2048
        lmask = at("lmask_sb", o, [len(LEVELS), P]); o += len(LEVELS) * P * 4
        assert o <= room, (o, room)

        bank = [ctx.enter_context(nc.psum_tensor(f"bank{i}", [P, 512], F32)) for i in range(8)]

        S = {n: ctx.enter_context(nc.semaphore(n)) for n in (
            "const_in", "x_in", "mem_in", "grow_in", "sink_in", "pool_in", "swa_in", "block2_in", "bias_in",
            "bias_out", "out_stored",
            "w_hi_ready", "w_lo_ready", "unit_used",
            "evac_act", "evac_dve",
            "t_full", "t_act", "t_dve",
            "full6", "full7", "free6", "free7", "hi7",
            "squares_summed", "rstd_ready", "head_squares", "head_rstd", "head_normed",
            "bias_neg", "probs_raw", "probs_ready", "values_done",
            "lb_ready", "forget_ready", "squared", "sigmoid_ready", "hg_sig", "hg_gated", "gates_ready",
            "dve_chain", "act_chain", "pool_chain")}
        raw_in = [ctx.enter_context(nc.semaphore(f"raw_in{i}")) for i in range(RAW_SLOTS)]

        def wait(eng, need):
            eng.wait_ge(S[need[0]], need[1])

        SSQ, VAR, RSTD = 0, 16, 32
        HSS, HVAR, HR, HALF = 48, 80, 112, 144
        AM, AN, AL, AR, AE = 176, 182, 188, 194, 200

        def col(c, n=1):
            return stat[:, c:c + n]

        norm_no = {st["name"]: st["n"] for st in steps if st["kind"] == "stats"}
        norm_of = {"mem0": "mem", "mem1": "mem", "in0": "x0", "kv": "mix1", "in1": "mix1", "w2": "attn2",
                   "ffg": "ffn2", "ffu": "ffn2", "up00": "mlp0", "up01": "mlp0", "up10": "mlp1", "up11": "mlp1"}

        def rstd_col(gemm):
            return RSTD + 2 * (norm_no[norm_of[gemm]] - 1)

        weights = {"mem0": a["w_mem_kv"][0], "mem1": a["w_mem_kv"][1], "in0": a["w_in"][0], "in1": a["w_in"][1],
                   "out0": a["w_out"][0], "out1": a["w_out"][1], "kv": a["w_kv"], "w2": a["w_in_2"][0],
                   "bhg": a["w_branch_hg_2"][0], "bat": a["w_branch_attn_2"][0], "out2": a["w_out_2"][0],
                   "ffg": a["w_ffn_gate_2"][0], "ffu": a["w_ffn_up_2"][0], "down2": a["w_ffn_down_2"][0]}
        for l in (0, 1):
            for half in (0, 1):
                n = D_FF // 2
                weights[f"up{l}{half}"] = a["w_up"][l][:, half * n:(half + 1) * n]
                weights[f"down{l}{half}"] = a["w_down"][l][half * n:(half + 1) * n, :]
        w2_order = [0, 1, 2, 3, 4, 5, 8, 9, 10, 11, 12, 13, 6, 7, 14, 15, 16, 17]

        def unit_ap(buf, slot, u):
            return buf[:, slot, 0:u["kn"] * u["w"]].rearrange("p (k n) -> p k n", k=u["kn"])

        def acc(g, t):
            return bank[2 * (g["index"] % 2) + t]

        def t_bank(b):
            return bank[4 + b["index"] % 2]

        natural = {"x": x, "mem": mem, "nat": nat, "oh": oh, "mkv0": mkv[0], "mkv1": mkv[1], "kvn": kvn}
        slotted = {"hs": hs, "nat2": nat2, "hs2": hs2}
        turned = {"qt": qt, "kt1": kt1, "mkt0": mkt[0], "mkt1": mkt[1], "q2": q2, "f2": f2, "aq": aq, "ak": ak}

        def chunk_of(src, t):
            name, c = src
            if name == "kdup":
                return kdup[:, t, c].rearrange("p two d -> p (two d)")
            if name == "gate":
                return gate[:, 0, t, c * P:(c + 1) * P]
            if isinstance(name, tuple):
                return slotted[name[0]][:, name[1], t, c * P:(c + 1) * P]
            return natural[name][:, t, c * P:(c + 1) * P]

        def segments(kind):
            return ((0, 0, 256), (1, 256, 256)) if kind == "mem" else ((0, 0, 128), (1, 128, 256))

        def prob_blocks(kind):
            if kind == "mem":
                return tuple((t * 256 + m * P, m, m * 256 + t * P, t) for m in (0, 1) for t in (0, 1))
            return ((0, 0, 0, 0), (128, 0, 128, 1), (256, 1, 256, 1))

        def scores_buf(hd):
            return (sc2 if hd["type"] == "moba" else sc)[:, (hd["a"] - 1) % 3]

        def pt_buf(hd):
            return (pt2 if hd["type"] == "moba" else pt)[:, (hd["a"] - 1) % 2]

        def pool_pieces(gi):
            cut = P if gi % 2 == 0 else P // 2
            for c0, c1 in ((0, cut), (cut, PG)):
                f = PG * gi + c0
                yield c0, c1, slice(f % P, f % P + c1 - c0), f // P

        def settle(eng, st):
            for name, count in (("t_full", "t_full"), ("full6", "full6"), ("full7", "full7"), ("values_done", "values"),
                                ("evac_dve", "evac_dve")):
                if st["at"].get(count):
                    eng.wait_ge(S[name], st["at"][count])

        last_level = {st["bank"]: st["use"] for st in steps if st["kind"] == "level"}

        block = ctx.enter_context(nc.Block())

        @block.sync
        def _(sp):
            sp.dma_start(mem[:], a["mem"][0].rearrange("(t p) d -> p t d", p=P)).then_inc(S["mem_in"], 16)
            sp.dma_start(x[:], a["x"][0].rearrange("(t p) d -> p t d", p=P)).then_inc(S["x_in"], 16)
            for st in steps:
                if st["kind"] == "split":
                    u = st["unit"]
                    slot = u["index"] % RAW_SLOTS
                    if u["index"] >= RAW_SLOTS:
                        sp.wait_ge(S["w_lo_ready"], u["index"] - RAW_SLOTS + 1)
                    n0 = u["n0"] if u["gemm"] != "w2" else w2_order[u["n0"] // NCOL] * NCOL
                    src = weights[u["gemm"]][u["k0"] * P:(u["k0"] + u["kn"]) * P, n0:n0 + u["w"]]
                    sp.dma_start(unit_ap(raw, slot, u), src.rearrange("(k p) n -> p k n", p=P)).then_inc(raw_in[slot], 16)
                elif st["kind"] == "store":
                    wait(sp, st["need"])
                    h = slice(st["half"] * NCOL, (st["half"] + 1) * NCOL)
                    sp.dma_start(out[0].rearrange("(t p) d -> p t d", p=P)[:, :, h], x[:, :, h]).then_inc(S["out_stored"], 16)
            sp.wait_ge(S["out_stored"], 32)

        @block.gpsimd
        def _(pool):
            chain = [0]

            def link(ins):
                ins.then_inc(S["pool_chain"], 1)
                chain[0] += 1
                pool.wait_ge(S["pool_chain"], chain[0])

            link(pool.memset(stat[:, HALF:HALF + 32], -0.5))
            for st in steps:
                kind = st["kind"]
                if kind == "stats":
                    c = 2 * (st["n"] - 1)
                    pool.wait_ge(S["squares_summed"], st["n"])
                    link(pool.tensor_scalar(col(VAR + c, 2), col(SSQ + c, 2), 1.0 / D, EPS, ALU.mult, ALU.add))
                    pool.tensor_tensor(col(RSTD + c, 2), col(VAR + c, 2), col(HALF, 2), ALU.pow
                                       ).then_inc(S["rstd_ready"], 1)
                    if st["name"] == "mlp0":
                        settle(pool, st)
                        pool.dma_start(dist[:], a["dist"]).then_inc(S["swa_in"], 16)
                elif kind in ("head_squares", "head_squares2", "hg_norm"):
                    cols = {"head_squares": TILES * st.get("heads", 0), "head_squares2": TILES * 4, "hg_norm": TILES * H2}[kind]
                    pool.wait_ge(S["head_squares"], st["n"])
                    link(pool.tensor_scalar(col(HVAR, cols), col(HSS, cols), 1.0 / (DH if kind == "head_squares" else P), EPS,
                                            ALU.mult, ALU.add))
                    pool.tensor_tensor(col(HR, cols), col(HVAR, cols), col(HALF, cols), ALU.pow
                                       ).then_inc(S["head_rstd"], 1)
                elif kind == "evac" and st["group"]["how"] == "relu":
                    h = hs[:, (st["hs"] - 1) % 2]
                    pool.wait_ge(S["evac_act"], st["group"]["done"])
                    pool.tensor_tensor(h, h, h, ALU.mult).then_inc(S["squared"], 1)
                elif kind == "second_block":
                    settle(pool, st)
                    pool.wait_ge(S["rstd_ready"], st["at"]["stats"])
                    link(pool.memset(tab[BUCKETS:BUCKETS + 1], NEG))
                    pool.dma_start(tab[0:BUCKETS], a["rel_bias_table_2"]).then_inc(S["block2_in"], 16)
                    pool.dma_start(hot[0:BUCKETS + 1], a["hot"]).then_inc(S["block2_in"], 16)
                    pool.dma_start(lmask[:], a["lmask"]).then_inc(S["block2_in"], 16)
                elif kind == "bias_rows":
                    pool.wait_ge(S["free6"], st["use6"])
                    pool.dma_start(scratch, rrow[0:H2, :]).then_inc(S["bias_out"], 16)
                elif kind == "bias_tiles":
                    settle(pool, st)
                    pool.wait_ge(S["bias_out"], 16)
                    src = bass.AP(tensor=scratch.tensor, offset=0, ap=[[1, P], [384, H2], [1, SEQ]])
                    pool.dma_start(ebias[:], src).then_inc(S["bias_in"], 16)
            pool.wait_ge(S["bias_out"], 16)

        @block.scalar
        def _(act):
            chain = [0]

            def tick(ins):
                ins.then_inc(S["act_chain"], 1)
                chain[0] += 1

            act.dma_start(grows[0:N_GAINS], a["gains"]).then_inc(S["grow_in"], 16)
            act.dma_start(ident[:], a["ident"]).then_inc(S["const_in"], 16)
            act.dma_start(poolp[:], a["poolp"]).then_inc(S["pool_in"], 16)
            pw = a["pool_w"][0].rearrange("g c d -> c g d")
            act.dma_start(pwa[:], pw[0:P]).then_inc(S["pool_in"], 16)
            act.dma_start(pwb[0:PG - P], pw[P:PG]).then_inc(S["pool_in"], 16)
            act.dma_start(sink[:], a["sinks"][0].partition_broadcast(P)).then_inc(S["sink_in"], 16)
            for st in steps:
                kind = st["kind"]
                if kind == "split":
                    u = st["unit"]
                    i = u["index"]
                    n = u["kn"] * u["w"]
                    act.wait_ge(raw_in[i % RAW_SLOTS], 16 * (i // RAW_SLOTS + 1))
                    if i >= PART_SLOTS:
                        act.wait_ge(S["unit_used"], i - PART_SLOTS + 1)
                    act.activation(w_hi[:, i % PART_SLOTS, 0:n], raw[:, i % RAW_SLOTS, 0:n], ACT.Copy
                                   ).then_inc(S["w_hi_ready"], 1)
                elif kind == "gains":
                    act.wait_ge(S["lb_ready"], 1)
                    act.activation(lb[:, 0, :], lb[:, 1, :], ACT.Sigmoid).then_inc(S["lb_ready"], 1)
                elif kind == "stats":
                    wait(act, st["need"])
                    if st["n"] > 1:
                        act.wait_ge(S["squares_summed"], st["n"] - 1)
                    if st["name"] == "ffn2":
                        settle(act, st)
                    buf = natural[st["src"]]
                    tick(act.activation(junk[:], buf[:, 0, :], ACT.Square, accum_out=col(SSQ + 2 * (st["n"] - 1))))
                    act.wait_ge(S["act_chain"], chain[0])
                    act.activation(junk[:], buf[:, 1, :], ACT.Square, accum_out=col(SSQ + 2 * (st["n"] - 1) + 1)
                                   ).then_inc(S["squares_summed"], 1)
                elif kind == "evac" and st["group"]["how"] in ("nat", "relu", "w2", "ffg"):
                    g = st["group"]
                    how, ng, w = g["how"], g["ng"], g["w"]
                    act.wait_ge(S["unit_used"], g["last_unit"])
                    act.wait_ge(S["rstd_ready"], norm_no[norm_of[g["gemm"]]])
                    r = rstd_col(g["gemm"])
                    func, done = ACT.Copy, "evac_act"
                    if how == "nat":
                        settle(act, st)
                        dst = {"mem0": mkv[0], "mem1": mkv[1], "kv": kvn}.get(g["gemm"])
                        if dst is None:
                            dst = nat[:, :, g["n0"]:g["n0"] + w]
                    elif how == "relu":
                        func = ACT.Relu
                        dst = hs[:, (st["hs"] - 1) % 2]
                        if st["hs"] > 2:
                            act.wait_ge(S["t_full"], pl.hs_last[st["hs"] - 2])
                        else:
                            settle(act, st)
                    elif how == "ffg":
                        func, done = ACT.Sigmoid, "sigmoid_ready"
                        dst = sig2[:, :, 0:w]
                        act.wait_ge(S["evac_dve"], st["at"]["evac_dve"])
                    else:
                        half, sec = ng % 2, ng // 2
                        cols = slice(half * NCOL, (half + 1) * NCOL)
                        if sec == 2:
                            dst = v2[:, :, cols]
                        elif sec == 5:
                            dst = av[:, :, cols]
                        elif sec >= 7:
                            dst = gate[:, sec - 7, :, cols]
                            if ng == 14:
                                act.wait_ge(S["free6"], st["at"]["use6"] - 0)
                                act.wait_ge(S["free7"], st["at"]["use7"] - 0)
                        else:
                            dst = nat2[:, ng % 2]
                        if st["at"].get("t_full"):
                            act.wait_ge(S["t_full"], st["at"]["t_full"])
                        if sec == 6:
                            act.wait_ge(S["head_normed"], st["at"]["head_scaled"])
                    for t in range(TILES):
                        ins = act.activation(dst[:, t, :], acc(g, t)[:, 0:w], func, scale=col(r + t))
                    ins.then_inc(S[done], 1)
                elif kind == "batch":
                    b = st["batch"]
                    how, tb = b["how"], t_bank(b)
                    act.wait_ge(S["t_full"], b["index"] + 1)
                    if how == "split":
                        for dst, gains in b["splits"]:
                            if gains is None:
                                ins = act.activation(at_hi[:, dst:dst + 2, :], tb[:], ACT.Copy)
                                continue
                            for i in (0, 1):
                                ins = act.activation(at_hi[:, dst + i, :], tb[:, i * SEQ:(i + 1) * SEQ], ACT.Copy,
                                                     scale=gt[:, gains[i]:gains[i] + 1])
                    elif how == "plain":
                        nm, c = b["dst"]
                        if nm == "ak":
                            act.wait_ge(S["bias_out"], 16)
                        if nm == "qt":
                            act.wait_ge(S["free7"], st["at"].get("use7", 0)) if st["at"].get("use7") else None
                        kw = dict(scale=gt[:, b["gains"][0]:b["gains"][0] + 1]) if b["gains"] else \
                            dict(scale=b["scale"]) if b["scale"] else {}
                        ins = act.activation(turned[nm][:, c:c + 2, :], tb[:], ACT.Copy, **kw)
                    elif how == "forget":
                        c = b["dst"][1]
                        act.activation(f2[:, c:c + 2, :], tb[:], ACT.Sigmoid)
                        ins = act.activation(k2[:, c:c + 2, :], tb[:], ACT.Sigmoid, scale=-1.0)
                    else:
                        hd = b["head"]
                        if hd["a"] > 2:
                            act.wait_ge(S["values_done"], hd["a"] - 2)
                        n = 512 if hd["type"] == "mem" else 384
                        ins = act.activation(pt_buf(hd)[:, 0:n], tb[:, 0:n], ACT.Copy)
                    ins.then_inc(S["t_act"], 1)
                elif kind == "softmax":
                    st = st["head"]
                    buf, s = scores_buf(st), (st["a"] - 1) % 3
                    act.wait_ge(S["bias_neg"], st["a"])
                    for i, (t, c0, n) in enumerate(segments(st["type"])):
                        ins = act.activation(buf[:, c0:c0 + n], buf[:, c0:c0 + n], ACT.Exp,
                                             scale=1.0 if st["type"] == "moba" else DH ** -0.5,
                                             bias=col(AN + 2 * s + i), accum_out=col(AL + 2 * s + i))
                    if st["type"] == "swa":
                        act.wait_ge(S["sink_in"], 16)
                        ins = act.activation(col(AE + 2 * s, 2), col(AN + 2 * s, 2), ACT.Exp,
                                             bias=sink[:, st["h"]:st["h"] + 1])
                    ins.then_inc(S["probs_raw"], 1)
                elif kind == "values" and st["close"]:
                    act.wait_ge(S["values_done"], st["head"]["a"])
                    act.activation(at_hi[:, st["chunk"], :], bank[7][:, 0:SEQ], ACT.Copy).then_inc(S["hi7"], 1)
                elif kind == "pool_mix":
                    act.wait_ge(S["full7"], st["full7"])
                    for i, (c0, c1, rows, ch) in enumerate(pool_pieces(st["gi"])):
                        gc = GAIN_ROWS["pool"][0] + ch
                        ins = act.activation(at_hi[rows, 8 + ch, :], bank[7][rows, i * SEQ:(i + 1) * SEQ], ACT.Copy,
                                             scale=gt[rows, gc:gc + 1])
                    ins.then_inc(S["hi7"], 1)
                elif kind in ("head_squares2", "hg_norm"):
                    act.wait_ge(S["head_rstd"], st["n"] - 1)
                    act.wait_ge(S["head_normed"], st["at"]["head_scaled"])
                    if kind == "hg_norm":
                        act.wait_ge(S["free6"], st["at"]["use6"])
                        act.wait_ge(S["free7"], st["at"]["use7"])
                    else:
                        wait(act, st["need"])
                    for half in range(2 if kind == "hg_norm" else 1):
                        for t in range(TILES):
                            for h in range(4):
                                j = t * 4 + h
                                if kind == "hg_norm":
                                    hh = 4 * half + h
                                    src, dst = oh[:, t, hh * P:(hh + 1) * P], HSS + t * H2 + hh
                                else:
                                    src, dst = nat2[:, st["slot"], t, h * P:(h + 1) * P], HSS + j
                                ins = act.activation(junk2[:, j * P:(j + 1) * P], src, ACT.Square, accum_out=col(dst))
                        if half == 0 and kind == "hg_norm":
                            tick(ins)
                            act.wait_ge(S["act_chain"], chain[0])
                    ins.then_inc(S["head_squares"], 1)
                    act.wait_ge(S["head_squares"], st["n"])
                elif kind == "hg_gate":
                    wait(act, st["need"])
                    if st["n"] > 1:
                        act.wait_ge(S["hg_gated"], st["n"] - 1)
                    act.activation(sgt[:], nat2[:, st["slot"]], ACT.Sigmoid).then_inc(S["hg_sig"], 1)
                elif kind == "gates":
                    act.wait_ge(S["evac_act"], pl.group_of["w2", 17]["done"])
                    act.activation(gate[:], gate[:], ACT.Sigmoid).then_inc(S["gates_ready"], 1)

        @block.tensor
        def _(pe):
            def take_bank(k, use):
                if use > 1:
                    pe.wait_ge(S[f"free{k}"], use - 1)

            for st in steps:
                kind = st["kind"]
                if kind == "gains":
                    pe.wait_ge(S["const_in"], 16)
                    pe.wait_ge(S["grow_in"], 16)
                    pe.transpose(bank[6][:, 0:N_GAINS], grows[0:N_GAINS], ident[0:N_GAINS, 0:N_GAINS]).then_inc(S["full6"], 1)
                elif kind == "mm":
                    u, g = st["unit"], st["group"]
                    for need in st["need"]:
                        wait(pe, need)
                    if st["k"] == 0:
                        pe.wait_ge(S["w_lo_ready"], u["index"] + 1)
                    if st["start"]:
                        for e in ("act", "dve"):
                            if g["free"][e]:
                                pe.wait_ge(S["evac_" + e], g["free"][e])
                    slot, k = u["index"] % PART_SLOTS, st["k"]
                    wh, wl = unit_ap(w_hi, slot, u)[:, k, :], unit_ap(w_lo, slot, u)[:, k, :]
                    kc, first = u["k0"] + k, GEMMS[g["gemm"]][2]
                    ch = h_slot(16 * int(g["gemm"][-1]) + kc) if first is None else first + kc
                    for t in range(TILES):
                        tok = slice(t * P, (t + 1) * P)
                        sums = acc(g, t)[:, 0:u["w"]]
                        pe.matmul(sums, at_hi[:, ch, tok], wh, start=st["start"], stop=False)
                        pe.matmul(sums, at_hi[:, ch, tok], wl, start=False, stop=False)
                        ins = pe.matmul(sums, at_lo[:, ch, tok], wh, start=False, stop=st["stop"])
                    if k == u["kn"] - 1:
                        ins.then_inc(S["unit_used"], 1)
                elif kind == "batch":
                    b = st["batch"]
                    wait(pe, b["need"])
                    if b["how"] != "probs" and b["src"][0][0] in ("x", "mem"):
                        wait(pe, (b["src"][0][0] + "_in", 16))
                    if "free" in b:
                        wait(pe, b["free"])
                    tb = t_bank(b)
                    if b["how"] == "probs":
                        for c, _, d, _ in prob_blocks(b["head"]["type"]):
                            ins = pe.transpose(tb[:, d:d + P], scores_buf(b["head"])[:, c:c + P], ident[:])
                    else:
                        for i in (0, 1):
                            for t in range(TILES):
                                c = i * SEQ + t * P
                                ins = pe.transpose(tb[:, c:c + P], chunk_of(b["src"][i], t), ident[:])
                    ins.then_inc(S["t_full"], 1)
                elif kind == "pool_diff":
                    pe.wait_ge(S["pool_in"], 48)
                    wait(pe, st["need"])
                    take_bank(6, st["use6"])
                    gi = st["gi"]
                    for i, (c0, c1) in enumerate(((0, P), (P, PG))):
                        ch = slice(PG * gi + c0, PG * gi + c1)
                        rows = slice(0, c1 - c0)
                        early, later = (bank[6][rows, i * SEQ + j * P:i * SEQ + (j + 1) * P] for j in (0, 1))
                        pe.matmul(early, nat[:, 0, ch], poolp[:, gi, 0:P], start=True, stop=True)
                        pe.matmul(later, nat[:, 0, ch], poolp[:, gi, P:SEQ], start=True, stop=False)
                        ins = pe.matmul(later, nat[:, 1, ch], poolp[:, gi, SEQ:SEQ + P], start=False, stop=True)
                    ins.then_inc(S["full6"], 1)
                elif kind == "pool_mix":
                    take_bank(7, st["use7"])
                    pe.wait_ge(S["free6"], st["diff"])
                    s, gi = 2 * (st["gi"] % 2), st["gi"]
                    for i, (c0, c1, rows, ch) in enumerate(pool_pieces(gi)):
                        mixed = bank[7][rows, i * SEQ:(i + 1) * SEQ]
                        pe.matmul(mixed, pwa[:, gi, c0:c1], dt[:, s, :], start=True, stop=False)
                        ins = pe.matmul(mixed, pwb[0:PG - P, gi, c0:c1], dt[0:PG - P, s + 1, :], start=False, stop=True)
                    ins.then_inc(S["full7"], 1)
                elif kind == "scores":
                    t_act = st["at"]["t_act"]
                    st = st["head"]
                    take_bank(6, st["use6"])
                    h = st["h"]
                    rows = slice(DH * (h % 2), DH * (h % 2) + DH)
                    if st["type"] == "mem":
                        q, k = qt[rows, 6 + h // 2, :], mkt[st["layer"]][rows, h // 2, :]
                    elif st["type"] == "swa":
                        q, k = qt[rows, h // 2, :], kt1[rows, h // (SWA_HEADS // KV_HEADS), :]
                    else:
                        q, k = aq[:, h, :], ak[:, h, :]
                    pe.wait_ge(S["t_act"], t_act)
                    for t, c0, n in segments(st["type"]):
                        ins = pe.matmul(bank[6][:, c0:c0 + n], q[:, t * P:(t + 1) * P], k[:, 0:n], start=True, stop=True)
                    ins.then_inc(S["full6"], 1)
                elif kind == "values":
                    hd = st["head"]
                    h = hd["h"]
                    take_bank(7, st["use7"])
                    pe.wait_ge(S["t_act"], st["batch"]["act"])
                    rows = slice(DH * (h % 2), DH * (h % 2) + DH)
                    if hd["type"] == "mem":
                        buf, c0, n = mkv[hd["layer"]], MEM_HEADS * DH + DH * h, DH
                    elif hd["type"] == "swa":
                        buf, c0, n = kvn, KV_HEADS * DH + DH * (h // (SWA_HEADS // KV_HEADS)), DH
                    else:
                        buf, c0, n, rows = av, h * P, P, slice(0, P)
                    for t in range(TILES):
                        mine = [blk for blk in prob_blocks(hd["type"]) if blk[3] == t]
                        for i, (_, kt, d, _) in enumerate(mine):
                            ins = pe.matmul(bank[7][rows, t * P:(t + 1) * P], buf[:, kt, c0:c0 + n],
                                            pt_buf(hd)[:, d:d + P], start=i == 0, stop=i == len(mine) - 1)
                    ins.then_inc(S["values_done"], 1)
                elif kind == "bias_rows":
                    take_bank(6, st["use6"])
                    pe.wait_ge(S["block2_in"], 48)
                    pe.matmul(bank[6][0:H2, 0:384], tab[0:BUCKETS + 1, :], hot[0:BUCKETS + 1, :], start=True, stop=True
                              ).then_inc(S["full6"], 1)
                elif kind == "level":
                    l, j, bk = st["l"], st["j"], bank[st["bank"]]
                    take_bank(st["bank"], st["use"])
                    if l == 0:
                        pe.wait_ge(S["t_act"], st["at"]["t_act"])
                        pe.wait_ge(S["forget_ready"], j + 1)
                    else:
                        pe.wait_ge(S[f"free{st['scaled'][0]}"], st["scaled"][1])
                    if l <= len(LEVELS):
                        blocks = [(2 * j + i // 2, slice(i % 2 * P, (i % 2 + 1) * P), slice(i % 2 * P, (i % 2 + 1) * P))
                                  for i in range(4)]
                    else:
                        blocks = [(2 * j + i, slice(0, P), slice(P, SEQ)) for i in (0, 1)]
                    for i, (h, keys, queries) in enumerate(blocks):
                        ins = pe.matmul(bk[:, i * P:(i + 1) * P], k2[:, h, keys], q2[:, h, queries], start=True, stop=True)
                    ins.then_inc(S[f"full{st['bank']}"], 1)
                elif kind == "hg_out":
                    take_bank(st["bank"], st["use"])
                    pe.wait_ge(S["evac_act"], pl.group_of["w2", 5]["done"])
                    pe.wait_ge(S["free6"], last_level[6])
                    pe.wait_ge(S["free7"], last_level[7])
                    for i in range(4):
                        h = 4 * st["q"] + i
                        sums, vs = bank[st["bank"]][:, i * P:(i + 1) * P], slice(h * P, (h + 1) * P)
                        if st["t"] == 0:
                            ins = pe.matmul(sums, att[:, h, 0, :], v2[:, 0, vs], start=True, stop=True)
                        else:
                            pe.matmul(sums, attx[:, h, :], v2[:, 0, vs], start=True, stop=False)
                            ins = pe.matmul(sums, att[:, h, 1, :], v2[:, 1, vs], start=False, stop=True)
                    ins.then_inc(S[f"full{st['bank']}"], 1)

        @block.vector
        def _(dve):
            chain = [0]

            def tick(ins):
                ins.then_inc(S["dve_chain"], 1)
                chain[0] += 1

            def link(ins):
                tick(ins)
                dve.wait_ge(S["dve_chain"], chain[0])

            for st in steps:
                kind = st["kind"]
                if kind == "gains":
                    dve.wait_ge(S["full6"], 1)
                    dve.tensor_copy(gt[:, 0:N_GAINS], bank[6][:, 0:N_GAINS]).then_inc(S["free6"], 1)
                    dve.wait_ge(S["free6"], 1)
                    c0, c1 = GAIN_ROWS["lb0"][0], GAIN_ROWS["lb1"][0]
                    dve.tensor_tensor(lb[:, 1, :], gt[:, c0:c0 + H2], gt[:, c1:c1 + H2], ALU.subtract
                                      ).then_inc(S["lb_ready"], 1)
                    dve.wait_ge(S["lb_ready"], 2)
                    link(dve.tensor_scalar(lb[:, 1, :], lb[:, 0, :], -1.0, 1.0, ALU.mult, ALU.add))
                elif kind == "split":
                    u = st["unit"]
                    i = u["index"]
                    n = u["kn"] * u["w"]
                    dve.wait_ge(S["w_hi_ready"], i + 1)
                    dve.tensor_tensor(w_lo[:, i % PART_SLOTS, 0:n], raw[:, i % RAW_SLOTS, 0:n],
                                      w_hi[:, i % PART_SLOTS, 0:n].bitcast(F32), ALU.subtract
                                      ).then_inc(S["w_lo_ready"], 1)
                elif kind == "batch" and st["batch"]["how"] == "split":
                    b = st["batch"]
                    dve.wait_ge(S["t_act"], b["act"])
                    for dst, gains in b["splits"]:
                        if gains is None:
                            ins = dve.tensor_tensor(at_lo[:, dst:dst + 2, :].rearrange("p c n -> p (c n)"), t_bank(b)[:],
                                                    at_hi[:, dst:dst + 2, :].rearrange("p c n -> p (c n)").bitcast(F32),
                                                    ALU.subtract)
                            continue
                        for i in (0, 1):
                            hi = at_hi[:, dst + i, :].bitcast(F32)
                            ins = dve.scalar_tensor_tensor(at_lo[:, dst + i, :], t_bank(b)[:, i * SEQ:(i + 1) * SEQ],
                                                           gt[:, gains[i]:gains[i] + 1], hi, ALU.mult, ALU.subtract)
                    ins.then_inc(S["t_dve"], 1)
                elif kind == "batch" and st["batch"]["how"] == "forget":
                    b = st["batch"]
                    dve.wait_ge(S["t_act"], b["act"])
                    for h in (b["dst"][1], b["dst"][1] + 1):
                        dve.tensor_scalar(f2[:, h, :], f2[:, h, :], lb[:, 1, h:h + 1], lb[:, 0, h:h + 1], ALU.mult, ALU.add)
                        ins = dve.tensor_scalar(k2[:, h, :], k2[:, h, :], lb[:, 1, h:h + 1], None, ALU.mult)
                    ins.then_inc(S["forget_ready"], 1)
                elif kind == "evac" and st["group"]["how"] == "res":
                    g = st["group"]
                    dve.wait_ge(S["unit_used"], g["last_unit"])
                    dve.wait_ge(S["squares_summed"], st["at"]["stats"])
                    dve.wait_ge(S["t_full"], st["at"]["t_full"])
                    if st["at"].get("evac_dve"):
                        dve.wait_ge(S["evac_dve"], st["at"]["evac_dve"])
                    for t in range(TILES):
                        xs = x[:, t, g["n0"]:g["n0"] + NCOL]
                        ins = dve.tensor_tensor(xs, xs, acc(g, t)[:], ALU.add)
                    ins.then_inc(S["evac_dve"], 1)
                elif kind == "evac" and st["group"]["how"] == "gate":
                    g = st["group"]
                    branch = 0 if g["gemm"] == "bhg" else 1
                    cols = slice(g["n0"], g["n0"] + NCOL)
                    dve.wait_ge(S["unit_used"], g["last_unit"])
                    dve.wait_ge(S["gates_ready"], 1)
                    for t in range(TILES):
                        ins = dve.tensor_tensor(gate[:, branch, t, cols], gate[:, branch, t, cols], acc(g, t)[:], ALU.mult)
                    if branch:
                        link(ins)
                        ins = dve.tensor_tensor(gate[:, 0, :, cols], gate[:, 0, :, cols], gate[:, 1, :, cols], ALU.add)
                    ins.then_inc(S["evac_dve"], 1)
                elif kind == "evac" and st["group"]["how"] in ("ffg", "ffu"):
                    g = st["group"]
                    n, w, r = st["n"], g["w"], rstd_col("ffg")
                    buf = hs2[:, (n - 1) % 2]
                    if g["how"] == "ffg":
                        dve.wait_ge(S["sigmoid_ready"], n)
                        if n > 2:
                            dve.wait_ge(S["t_full"], pl.hs_last["g", n - 2])
                        else:
                            settle(dve, st)
                    else:
                        dve.wait_ge(S["unit_used"], g["last_unit"])
                        dve.wait_ge(S["evac_dve"], g["done"] - 1)
                    for t in range(TILES):
                        other = sig2[:, t, 0:w] if g["how"] == "ffg" else buf[:, t, 0:w]
                        ins = dve.scalar_tensor_tensor(buf[:, t, 0:w], acc(g, t)[:, 0:w], col(r + t), other,
                                                       ALU.mult, ALU.mult)
                    ins.then_inc(S["evac_dve"], 1)
                elif kind == "head_squares":
                    src, heads, n = natural[st["src"]], st["heads"], st["n"]
                    cols = slice(st["off"] * DH, (st["off"] + heads) * DH)
                    wait(dve, st["need"])
                    settle(dve, st)
                    if n > 1:
                        dve.wait_ge(S["head_rstd"], n - 1)
                    for t in range(TILES):
                        link(dve.tensor_tensor(square[:, 0:heads * DH], src[:, t, cols], src[:, t, cols], ALU.mult))
                        ins = dve.tensor_reduce(col(HSS + t * heads, heads),
                                                square[:, 0:heads * DH].rearrange("p (h d) -> p h d", d=DH), AX_X, ALU.add)
                        if t == 0:
                            link(ins)
                    ins.then_inc(S["head_squares"], 1)
                elif kind == "head_scale":
                    src, heads, n = natural[st["src"]], st["heads"], st["n"]
                    cols = slice(st["off"] * DH, (st["off"] + heads) * DH)
                    dve.wait_ge(S["head_rstd"], n)
                    for t in range(TILES):
                        s_ = src[:, t, cols].rearrange("p (h d) -> p h d", d=DH)
                        r_ = col(HR + t * heads, heads).unsqueeze(2).to_broadcast([P, heads, DH])
                        if src is kvn:
                            both = [P, heads, 2, DH]
                            ins = dve.tensor_tensor(kdup[:, t], s_.unsqueeze(2).to_broadcast(both),
                                                    r_.unsqueeze(2).to_broadcast(both), ALU.mult)
                        else:
                            ins = dve.tensor_tensor(s_, s_, r_, ALU.mult)
                    ins.then_inc(S["head_normed"], 1)
                elif kind in ("head_scale2", "hg_norm"):
                    n_h = 4 if kind == "head_scale2" else H2
                    src = nat2[:, st["slot"]] if kind == "head_scale2" else oh
                    dve.wait_ge(S["head_rstd"], st["n"])
                    for t in range(TILES):
                        s_ = src[:, t, :].rearrange("p (h d) -> p h d", d=P)
                        r_ = col(HR + t * n_h, n_h).unsqueeze(2).to_broadcast([P, n_h, P])
                        ins = dve.tensor_tensor(s_, s_, r_, ALU.mult)
                    ins.then_inc(S["head_normed"], 1)
                elif kind == "hg_gate":
                    cols = slice(st["half"] * NCOL, (st["half"] + 1) * NCOL)
                    dve.wait_ge(S["hg_sig"], st["n"])
                    dve.wait_ge(S["head_normed"], st["at"]["head_scaled"])
                    link(dve.tensor_tensor(oh[:, :, cols], oh[:, :, cols], nat2[:, st["slot"]], ALU.mult))
                    dve.tensor_tensor(oh[:, :, cols], oh[:, :, cols], sgt[:], ALU.mult).then_inc(S["hg_gated"], 1)
                elif kind == "pool_diff":
                    s = 2 * (st["gi"] % 2)
                    dve.wait_ge(S["full6"], st["full6"])
                    if st["gi"] > 1:
                        dve.wait_ge(S["full7"], st["gi"] - 1)
                    dve.tensor_copy(dt[:, s, :], bank[6][:, 0:SEQ])
                    dve.tensor_copy(dt[0:PG - P, s + 1, :], bank[6][0:PG - P, SEQ:2 * SEQ]).then_inc(S["free6"], 1)
                elif kind == "pool_mix":
                    dve.wait_ge(S["hi7"], st["hi7"])
                    for i, (c0, c1, rows, ch) in enumerate(pool_pieces(st["gi"])):
                        gc = GAIN_ROWS["pool"][0] + ch
                        ins = dve.scalar_tensor_tensor(at_lo[rows, 8 + ch, :], bank[7][rows, i * SEQ:(i + 1) * SEQ],
                                                       gt[rows, gc:gc + 1], at_hi[rows, 8 + ch, :].bitcast(F32),
                                                       ALU.mult, ALU.subtract)
                    ins.then_inc(S["free7"], 1)
                elif kind == "values" and st["close"]:
                    c = st["chunk"]
                    dve.wait_ge(S["hi7"], st["hi7"])
                    dve.scalar_tensor_tensor(at_lo[:, c, :], bank[7][:, 0:SEQ], 1.0, at_hi[:, c, :].bitcast(F32),
                                             ALU.mult, ALU.subtract).then_inc(S["free7"], 1)
                elif kind == "softmax":
                    st = st["head"]
                    kd, buf, s = st["type"], scores_buf(st), (st["a"] - 1) % 3
                    dve.wait_ge(S["full6"], st["full6"])
                    if st["a"] > 3:
                        dve.wait_ge(S["t_full"], pl.prob_batch[st["a"] - 3])
                    if kd == "mem":
                        ins = dve.tensor_copy(buf[:, 0:512], bank[6][:, 0:512])
                    elif kd == "swa":
                        dve.wait_ge(S["swa_in"], 16)
                        slope = 2.0 ** (-8.0 * (st["h"] + 1) / SWA_HEADS)
                        ins = dve.scalar_tensor_tensor(buf[:, 0:384], dist[:], -slope * DH ** 0.5, bank[6][:, 0:384],
                                                       ALU.mult, ALU.add)
                    else:
                        dve.wait_ge(S["bias_in"], 16)
                        for t, c0, m in segments(kd):
                            ins = dve.scalar_tensor_tensor(buf[:, c0:c0 + m], bank[6][:, c0:c0 + m], P ** -0.5,
                                                           ebias[:, st["h"], m - 1::-1], ALU.mult, ALU.add)
                    ins.then_inc(S["free6"], 1)
                    dve.wait_ge(S["free6"], st["use6"])
                    for i, (t, c0, m) in enumerate(segments(kd)):
                        ins = dve.tensor_reduce(col(AM + 2 * s + i), buf[:, c0:c0 + m], AX_X, ALU.max)
                    link(ins)
                    scale = 1.0 if kd == "moba" else DH ** -0.5
                    if kd == "swa":
                        dve.wait_ge(S["sink_in"], 16)
                        link(dve.tensor_scalar(col(AM + 2 * s, 2), col(AM + 2 * s, 2), scale, sink[:, st["h"]:st["h"] + 1],
                                               ALU.mult, ALU.max))
                        scale = 1.0
                    dve.tensor_scalar(col(AN + 2 * s, 2), col(AM + 2 * s, 2), -scale, None, ALU.mult
                                      ).then_inc(S["bias_neg"], 1)
                elif kind == "normalise":
                    hd = st["head"]
                    buf, s = scores_buf(hd), (hd["a"] - 1) % 3
                    dve.wait_ge(S["probs_raw"], hd["a"])
                    if hd["type"] == "swa":
                        link(dve.tensor_tensor(col(AL + 2 * s, 2), col(AL + 2 * s, 2), col(AE + 2 * s, 2), ALU.add))
                    link(dve.reciprocal(col(AR + 2 * s, 2), col(AL + 2 * s, 2)))
                    for i, (t, c0, m) in enumerate(segments(hd["type"])):
                        ins = dve.tensor_scalar(buf[:, c0:c0 + m], buf[:, c0:c0 + m], col(AR + 2 * s + i), None, ALU.mult)
                    ins.then_inc(S["probs_ready"], 1)
                elif kind == "bias_rows":
                    dve.wait_ge(S["full6"], st["full6"])
                    dve.tensor_copy(rrow[0:H2, :], bank[6][0:H2, 0:384]).then_inc(S["free6"], 1)
                elif kind == "level":
                    l, pair = st["l"], slice(2 * st["j"], 2 * st["j"] + 2)
                    dve.wait_ge(S[f"full{st['bank']}"], st["full"])
                    attn = att[:, pair].rearrange("p h t n -> p (h t) n")
                    product = bank[st["bank"]][:].rearrange("p (b n) -> p b n", n=P)
                    if l == 0:
                        dve.wait_ge(S["block2_in"], 48)
                        link(dve.tensor_tensor(attn, product, ident[:].unsqueeze(1).to_broadcast([P, 4, P]), ALU.mult))
                        ins = dve.tensor_tensor(q2[:, pair], q2[:, pair], f2[:, pair], ALU.mult)
                    elif l <= len(LEVELS):
                        half = LEVELS[l - 1]
                        nb = SEQ // half
                        tick(dve.copy_predicated(attn, lmask[:, l - 1].bitcast(I32).unsqueeze(1).to_broadcast([P, 4, P]), product))
                        cur, nxt = (f2, f2b) if l % 2 else (f2b, f2)
                        f_ = cur[:, pair].rearrange("p h n -> p (h n)")[:, 0:2 * nb].rearrange("p (b two) -> p b two", two=2)
                        q_ = q2[:, pair].rearrange("p h (b two n) -> p (h b) two n", two=2, n=half)
                        k_ = k2[:, pair].rearrange("p h (b two n) -> p (h b) two n", two=2, n=half)
                        dve.wait_ge(S["dve_chain"], chain[0])
                        dve.tensor_tensor(q_[:, :, 1, :], q_[:, :, 1, :], f_[:, :, 0:1].to_broadcast([P, nb, half]), ALU.mult)
                        dve.tensor_tensor(k_[:, :, 0, :], k_[:, :, 0, :], f_[:, :, 1:2].to_broadcast([P, nb, half]), ALU.mult)
                        ins = dve.tensor_tensor(nxt[:, pair].rearrange("p h n -> p (h n)")[:, 0:nb], f_[:, :, 0], f_[:, :, 1],
                                                ALU.mult)
                    else:
                        ins = dve.tensor_copy(attx[:, pair].rearrange("p h n -> p (h n)"), bank[st["bank"]][:, 0:2 * P])
                    ins.then_inc(S[f"free{st['bank']}"], 1)
                    dve.wait_ge(S[f"free{st['bank']}"], st["use"])
                elif kind == "hg_out":
                    dve.wait_ge(S[f"full{st['bank']}"], st["full"])
                    dve.tensor_copy(oh[:, st["t"], st["q"] * NCOL:(st["q"] + 1) * NCOL], bank[st["bank"]][:]
                                    ).then_inc(S[f"free{st['bank']}"], 1)


def shape_constants():
    p, c = np.arange(P)[:, None], np.arange(384)[None, :]
    pool = np.zeros((P, len(WINDOWS), 384), np.float32)
    s, t = np.arange(SEQ)[:, None], np.arange(SEQ)[None, :]
    for i, w in enumerate(WINDOWS):
        m = ((t - s >= 0) & (t - s < w)) / np.minimum(t + 1, w) - (t == s)
        pool[:, i, 0:SEQ] = m[0:P]
        pool[:, i, SEQ:] = m[P:, P:]
    d = np.where(c < P, p - c, p + P - (c - P))
    dist = np.where((d >= 0) & (d < P), d, 1.0e30).astype(np.float32)
    n = np.arange(384) - (P - 1)
    nf = np.maximum(n, 1).astype(np.float32)
    large = 16 + (np.log(nf / 16).astype(np.float32) / np.float32(np.log(128 / 16)) * np.float32(16)).astype(np.int32)
    bucket = np.where(n < 16, n, np.minimum(large, BUCKETS - 1))
    hot = np.zeros((BUCKETS + 1, 384), np.float32)
    for j in range(384):
        hot[bucket[j] if n[j] >= 0 else BUCKETS, j] = 1.0
    levels = np.zeros((P, len(LEVELS), P), np.float32)
    q = np.arange(P)[None, :]
    for i, b in enumerate(LEVELS):
        levels[:, i, :] = (p // (2 * b) == q // (2 * b)) & (p % (2 * b) < b) & (q % (2 * b) >= b)
    return {"ident": np.eye(P, dtype=np.float32), "poolp": pool, "dist": dist, "hot": hot, "lmask": levels}


def gain_rows(inputs):
    i = {k: np.asarray(v) for k, v in inputs.items()}
    rows = [i["norm_mix"], i["kv_norm"], i["mem_norm"], i["norm_mlp"], i["attn_norm_g_2"], i["ffn_norm_g_2"],
            i["hg_lb_gamma_2"], i["pool_scale"], i["hg_out_norm_g_2"], i["q_norm_g_2"], i["k_norm_g_2"]]
    for v in (i["k_norm"], i["q_norm"], i["mem_q_norm"][0], i["mem_q_norm"][1], i["mem_k_norm"][0], i["mem_k_norm"][1]):
        rows += [v, v]
    return np.concatenate([r.reshape(-1) for r in rows]).reshape(N_GAINS, P)


INPUTS = ["x", "mem", "w_in", "pool_w", "w_kv", "sinks", "w_mem_kv", "w_out", "w_up", "w_down", "w_in_2",
          "rel_bias_table_2", "w_branch_hg_2", "w_branch_attn_2", "w_out_2", "w_ffn_gate_2", "w_ffn_up_2",
          "w_ffn_down_2"]


def kernel(**inputs):
    import concourse.bacc as bacc
    from concourse.bass_utils import run_bass_kernel_spmd

    nc = bacc.Bacc("TRN2", target_bir_lowering=False, num_devices=1)
    arrays, aps = {}, {}
    for name, v in [*((n, inputs[n]) for n in INPUTS), ("gains", gain_rows(inputs)), *shape_constants().items()]:
        v = np.ascontiguousarray(v)
        arrays[f"in_{name}"] = v
        aps[name] = nc.dram_tensor(f"in_{name}", v.shape, mybir.dt.from_np(v.dtype), kind="ExternalInput").ap()
    out = nc.dram_tensor("out_0", (1, SEQ, D), F32, kind="ExternalOutput").ap()
    scratch = nc.dram_tensor("bias_scratch", (H2, 384), F32, kind="Internal").ap()
    two_blocks_kernel(nc, aps, out, scratch)
    return run_bass_kernel_spmd(nc, [arrays], core_ids=[0]).results[0]["out_0"]
```

```python
from contextlib import ExitStack

import numpy as np

import concourse.bass as bass
from concourse import mybir

F32 = mybir.dt.float32
F32R = mybir.dt.float32r
BF16 = mybir.dt.bfloat16
I32 = mybir.dt.int32
ALU = mybir.AluOpType
ACT = mybir.ActivationFunctionType
AX_X = mybir.AxisListType.X

P = 128
SEQ = 256
TILES = SEQ // P
D = 1024
DCH = D // P
EPS = 1e-6
NEG = -1.0e30
UNIT_K = 4
NCOL = 512
UNIT = UNIT_K * NCOL
RAW_SLOTS, PART_SLOTS = 4, 3
HI_AHEAD = (PART_SLOTS - 1) * UNIT_K
AT_CHUNKS = 32
DH = 64
SWA_HEADS, KV_HEADS, MEM_HEADS = 12, 4, 4
SCORE_SLOTS = 3
WINDOWS = (2, 4, 8, 16)
PG = 192
D_FF, D_FF2 = 4096, 2816
H2 = 8
BUCKETS = 32
LEVELS = (1, 2, 4, 8, 16, 32, 64)

GAIN_ROWS = {}
_at = 0
for _name, _n in (("mix0", 8), ("mix1", 8), ("kv", 8), ("mem0", 8), ("mem1", 8), ("mlp0", 8), ("mlp1", 8),
                  ("attn2", 8), ("ffn2", 8), ("lb0", 8), ("lb1", 8), ("pool", 6), ("hg", 1), ("q2", 1), ("k2", 1),
                  ("k", 1), ("q", 1), ("mq0", 1), ("mq1", 1), ("mk0", 1), ("mk1", 1)):
    GAIN_ROWS[_name] = (_at, _n)
    _at += _n
N_GAINS = _at

GEMMS = {
    "mem0": (8, 512, 16, "nat"), "in0": (8, 1024, 0, "nat"), "mem1": (8, 512, 24, "nat"),
    "out0": (8, 1024, 8, "res"),
    "kv": (8, 512, 16, "nat"), "in1": (8, 1024, 0, "nat"), "out1": (8, 1024, 8, "res"),
    "w2": (8, 9216, 0, "w2"), "bhg": (8, 1024, 0, "gate"), "bat": (8, 1024, 8, "gate"),
    "out2": (8, 1024, 0, "res"),
    "ffg": (8, D_FF2, 0, "ffg"), "ffu": (8, D_FF2, 0, "ffu"), "down2": (22, 1024, 8, "res"),
}
for _l in (0, 1):
    for _h in (0, 1):
        GEMMS[f"up{_l}{_h}"] = (8, D_FF // 2, 0, "relu")
        GEMMS[f"down{_l}{_h}"] = (16, 1024, None, "res")


def h_slot(c):
    return 8 + c % (AT_CHUNKS - 8)


class Plan:

    def __init__(self):
        self.steps, self.units, self.groups, self.batches = [], [], [], []
        self.count = {}
        self.group_of = {}
        self.hs_last = {}
        self.prob_batch = {}
        self.value_batch = {}
        self.closed = {}
        self.turned = {}
        self.pending = None

    def tick(self, name):
        self.count[name] = self.count.get(name, 0) + 1
        return self.count[name]

    def now(self, name):
        return self.count.get(name, 0)

    def add(self, kind, **st):
        st["kind"] = kind
        st["at"] = dict(self.count)
        self.steps.append(st)
        return st

    def mm(self, gemm, ng, kq, need=(), between=()):
        needs = need if callable(need) else (need if isinstance(need, dict) else {0: need}).get
        kch, cols, base, how = GEMMS[gemm]
        g = self.group_of.get((gemm, ng))
        if g is None:
            n0 = ng * NCOL
            g = dict(gemm=gemm, ng=ng, n0=n0, w=min(NCOL, cols - n0), kch=kch, how=how, index=len(self.groups),
                     engine="dve" if how in ("res", "gate", "ffg", "ffu") else "act", chunks=0)
            g["free"] = {e: sum(o["engine"] == e for o in self.groups[:-1]) for e in ("act", "dve")}
            self.groups.append(g)
            self.group_of[gemm, ng] = g
        first = kq * UNIT_K
        u = dict(index=len(self.units), gemm=gemm, k0=first, kn=min(UNIT_K, kch - first), n0=g["n0"], w=g["w"],
                 c0=self.now("chunk"))
        self.units.append(u)
        g["last_unit"] = u["index"] + 1
        for k in range(u["kn"]):
            self.tick("chunk")
            self.add("mm", unit=u, group=g, k=k, need=needs(k) or (), start=g["chunks"] == 0,
                     stop=g["chunks"] == kch - 1)
            g["chunks"] += 1
            if k < len(between) and between[k]:
                between[k]()

    def evac(self, gemm, ng, **more):
        g = self.group_of[gemm, ng]
        self.add("evac", group=g, **more)
        g["done"] = self.tick("evac_" + g["engine"])
        return ("evac_" + g["engine"], g["done"])

    def batch(self, src, dst, how, need, gains=None, scale=None, head=None, more=()):
        self.take()
        b = dict(index=len(self.batches), src=src, dst=dst, how=how, need=need, gains=gains, scale=scale, head=head,
                 splits=[(dst, gains), *more])
        b["act"] = self.tick("t_act")
        split = ("split", "values")
        b["dve"] = self.tick("t_dve") if how in split else self.now("t_dve")
        if len(self.batches) >= 2:
            o = self.batches[-2]
            b["free"] = ("t_dve", o["dve"]) if o["how"] in split else ("t_act", o["act"])
        self.batches.append(b)
        self.tick("t_full")
        if how == "values":
            self.add("batch", batch=b, part="product")
            self.pending = b
        else:
            self.add("batch", batch=b)
        return b

    def take(self):
        if self.pending:
            self.add("batch", batch=self.pending, part="take")
            self.pending = None

    def split_ready(self):
        return ("t_dve", self.now("t_dve"))


def build_plan():
    pl = Plan()

    def col_of(gain, c=0):
        return GAIN_ROWS[gain][0] + c

    def turn(src, c, dst, need, gain=None, one_gain=False, also=()):
        def cols(g):
            return None if g is None else (col_of(g),) * 2 if one_gain else (col_of(g, c), col_of(g, c + 1))
        return lambda: pl.batch([(src, c), (src, c + 1)], dst + c, "split", need, gains=cols(gain),
                                more=[(d + c, cols(g)) for d, g in also])

    def plain(src, c, dst, need, gain=None, scale=None, how="plain"):
        def go():
            b = pl.batch([(src, c), (src, c + 1)], dst, how, need, gains=(col_of(gain),) * 2 if gain else None,
                         scale=scale)
            pl.turned[dst[0], dst[1]] = pl.turned[dst[0], dst[1] + 1] = ("t_act", b["act"])
        return go

    def stats(name, src, need):
        pl.tick("stats")
        pl.add("stats", n=pl.now("stats"), src=src, name=name, need=need if isinstance(need, list) else [need])

    def head_squares(src, heads, need, off=0):
        first, second, scale, normed = head_norm(src, heads, need, off)
        first()
        second()
        return scale, normed

    def head_norm(src, heads, need, off=0):
        st = dict(src=src, heads=heads, off=off, need=need)
        st["n"] = n = pl.tick("headnorm")
        squares = [lambda t=t: pl.add("head_squares", t=t, **st) for t in range(TILES)]
        return *squares, lambda: (pl.tick("head_scaled"), pl.add("head_scale", **st)), ("head_normed", n)

    def scores(kind, h, **more):
        k = 6 + pl.tick("head") % 2
        hd = dict(a=pl.now("head"), type=kind, h=h, bank=k, use=pl.tick(f"use{k}"), full=pl.tick(f"full{k}"), **more)
        q, k = {"mem": (("qt", 6 + h // 2), (f"mkt{hd['layer']}", h // 2)), "moba": (("aq", h), ("ak", h)),
                "swa": (("qt", h // 2), ("kt1", h // (SWA_HEADS // KV_HEADS)))}[kind]
        pl.add("scores", head=hd, need=[pl.turned[q], pl.turned[k]])
        return hd

    def turn_probs(hd):
        pl.add("normalise", head=hd)
        hd["batch"] = pl.batch(None, None, "probs", ("probs_ready", hd["a"]), head=hd)
        pl.prob_batch[hd["a"]] = hd["batch"]["index"] + 1

    def values(pair, chunk):
        n = 2 if pair[0]["type"] == "moba" else 1
        b = pl.batch(pair, chunk, "values", ("t_act", pair[1]["batch"]["act"]))
        b["chunks"] = n
        for hd in pair:
            pl.value_batch[hd["a"]] = b["index"] + 1
        for c in range(n):
            pl.closed[chunk + c] = ("t_dve", b["dve"])

    def head_steps(heads):
        pairs = len(heads) // 2
        live = {}

        def score(i):
            live[i] = scores(heads[i][0], heads[i][1], layer=heads[i][3])

        def begin(j):
            pl.take()
            if j < pairs:
                score(2 * j)
            if j:
                turn_probs(live[2 * j - 2])

        def second(j):
            pl.add("softmax", head=live[2 * j])
            score(2 * j + 1)

        def third(j):
            if j:
                turn_probs(live[2 * j - 1])
            if j < pairs:
                pl.add("softmax", head=live[2 * j + 1])
        for j in range(pairs + 1):
            yield lambda j=j: begin(j)
            if j < pairs:
                yield lambda j=j: second(j)
            yield lambda j=j: third(j)
            yield (lambda j=j: values([live[2 * j - 2], live[2 * j - 1]], heads[2 * j - 2][2])) if j else lambda: None
        yield pl.take

    def woven_mm(order, steps):
        steps = list(steps)
        total = sum(min(UNIT_K, GEMMS[gm][0] - kq * UNIT_K) for gm, _, kq, *_ in order)
        at = 0

        def upto(n):
            nonlocal at
            while at < n and at < len(steps):
                steps[at]()
                at += 1
        seen = 0
        for gm, ng, kq, need, *after in order:
            kn = min(UNIT_K, GEMMS[gm][0] - kq * UNIT_K)
            pl.mm(gm, ng, kq, need,
                  between=[lambda n=seen + k + 1: upto(n * len(steps) // total) for k in range(kn)])
            seen += kn
            for step in after:
                step()
        upto(len(steps))

    def placed_mm(units, steps, places):
        run = 0

        def upto(n):
            nonlocal run
            while run < n:
                steps[run]()
                run += 1
        upto(places[0] + 1)
        seen = 0
        for gm, ng, kq, need in units:
            ends = [places[c] + 1 if c < len(places) else len(steps) for c in range(seen + 1, seen + UNIT_K + 1)]
            pl.mm(gm, ng, kq, need, between=[lambda n=n: upto(n) for n in ends])
            seen += UNIT_K

    def halves(ready):
        return {0: [(ready[0], ready[1] - 1)], 2: [ready]}

    def pair(gemm, need, late=(), first_x=None):
        n = -(-GEMMS[gemm][0] // UNIT_K)
        ready = None
        for kq in range(n):
            pl.mm(gemm, 0, kq, need if kq == 0 else [ready] if ready else [],
                  between=[None] + list(late) if kq == 0 else ())
            if kq == 0 and late:
                ready = pl.split_ready()
            if kq == n - 1:
                done0 = pl.evac(gemm, 0)
                turns = first_x(done0) if first_x else []
            else:
                turns = []
            pl.mm(gemm, 1, kq, between=[None] + turns)
        return pl.split_ready(), pl.evac(gemm, 1)

    evens = (0, 2, 4, 6)
    AHEAD_1 = 7
    OUT1_AT = (10, 13, 17, 20, 22, 24, 26, 28, 29, 31, 33, 35)

    pl.add("gains", use6=pl.tick("use6"))
    pl.tick("full6")
    gains = ("free6", 1)
    turn_mem = [turn("mem", c, 16, gains, "mem0") for c in evens]
    turn_x = [turn("x", c, 0, gains, "mix0") for c in evens]
    ready = [("t_dve", turn_mem[0]()["dve"]), ("t_dve", turn_mem[1]()["dve"])]
    pl.mm("mem0", 0, 0, {0: [ready[0]], 2: [ready[1]]}, between=[turn_mem[2], turn_mem[3], turn_x[0]])
    ready = pl.batches[2:4]
    pl.mm("mem0", 0, 1, {0: [("t_dve", ready[0]["dve"])], 2: [("t_dve", ready[1]["dve"])]},
          between=[turn_x[1], turn_x[2], turn_x[3]])
    r = pl.split_ready()
    stats("mem", "mem", [("mem_low_in", 16), ("mem_high_in", 16)])
    kv_done = pl.evac("mem0", 0)
    scale_k, k_normed = head_squares("mkv0", 4, kv_done)
    again = [turn("mem", c, 24, gains, "mem1") for c in evens]
    pl.mm("in0", 1, 0, [r], between=[again[0], again[1], scale_k])
    stats("x0", "x", ("x_in", 16))
    pl.mm("in0", 1, 1, between=[again[2], plain("mkv0", 0, ("mkt0", 0), k_normed, "mk0"), again[3]])
    hi_done = pl.evac("in0", 1)
    scale_q, q_normed = head_squares("nat", 4, hi_done, off=12)
    pl.mm("in0", 0, 0, between=[None, None, scale_q, plain("nat", 6, ("qt", 6), q_normed, "mq0")])

    pool_use = {}

    def pool_diff(gi):
        pl.tick("full6")
        pool_use[gi] = pl.tick("use6")
        pl.add("pool_diff", gi=gi, use6=pool_use[gi], need=("evac_act", pl.group_of["in0", 0]["done"]),
               full6=pl.now("full6"))

    def pool_mix(gi):
        pl.tick("full7")
        pl.tick("hi7")
        pl.add("pool_mix", gi=gi, use7=pl.tick("use7"), hi7=pl.now("hi7"), full7=pl.now("full7"), diff=pool_use[gi])
        return ("free7", pl.now("use7"))
    woven_mm([("in0", 0, 1, (), lambda: pl.evac("in0", 0)), ("mem1", 0, 0, ())],
             head_steps([("mem", h, 14 + h // 2, 0) for h in range(4)]))
    mixed = {}

    def pool_pair(gi):
        def go():
            pool_diff(gi)
            if gi:
                mixed[gi - 1] = pool_mix(gi - 1)
        return go
    pl.mm("mem1", 0, 1, between=[pool_pair(gi) for gi in range(4)])
    kv_done = pl.evac("mem1", 0)
    scale_k, k_normed = head_squares("mkv1", 4, kv_done)
    last_group = (1, 1, 2, 3)
    pl.mm("out0", 0, 0, lambda k: [mixed[last_group[k]]],
          between=[lambda: mixed.update({3: pool_mix(3)}), None, scale_k])
    mix = mixed[3]

    def mlp(l, first, done1, gain, first_x):
        stats(gain, "x", done1)
        for half in (0, 1):
            up, down = f"up{l}{half}", f"down{l}{half}"

            def finish(ng):
                n = pl.tick("squares")
                pl.evac(up, ng, hs=n)
                return ng, n

            def turns(ng, n):
                def go(pr):
                    b = pl.batch([(("hs", (n - 1) % 2), pr), (("hs", (n - 1) % 2), pr + 1)],
                                 h_slot(half * 16 + ng * 4 + pr), "split", ("squared", n))
                    pl.hs_last[n] = b["index"] + 1
                return [lambda: go(0), None, lambda: go(2)]
            if half == 0:
                pl.mm(up, 0, 0, halves(first), between=[None, turn("x", 4, 0, done1, gain), turn("x", 6, 0, done1, gain)])
                r = pl.split_ready()
                pl.mm(up, 1, 0)
                pl.mm(up, 0, 1, [r])
                last = finish(0)
                pl.mm(up, 1, 1)
                now = finish(1)
                pl.mm(up, 2, 0, between=turns(*last))
                pl.mm(up, 2, 1, between=turns(*now))
                last = finish(2)
                rest = (3,)
            else:
                last, rest = None, (0, 1, 2, 3)
            for ng in rest:
                pl.mm(up, ng, 0)
                pl.mm(up, ng, 1, between=turns(*last) if last else ())
                last = finish(ng)
            pl.mm(down, 0, 0, [pl.split_ready()])
            pl.mm(down, 1, 0, between=turns(*last))
            ready = pl.split_ready()
            for kq in (1, 2):
                pl.mm(down, 0, kq)
                pl.mm(down, 1, kq)
            pl.mm(down, 0, 3, [ready])
            done0 = pl.evac(down, 0)
            pl.mm(down, 1, 3, between=[None] + first_x(done0) if half else ())
            first, done1 = pl.split_ready(), pl.evac(down, 1)
        return first, done1

    def first_half(gain, dst=0, also=()):
        return lambda done0: [turn("x", c, dst, done0, gain, also=also) for c in (0, 2)]

    pl.mm("out0", 1, 0, between=[plain("mkv1", 0, ("mkt1", 0), k_normed, "mk1")])
    pl.mm("out0", 0, 1, [mix])
    done0 = pl.evac("out0", 0)
    pl.mm("out0", 1, 1, between=[None] + first_half("mlp0")(done0))
    first, done1 = pl.split_ready(), pl.evac("out0", 1)
    first, done1 = mlp(0, first, done1, "mlp0", first_half("kv", 16, [(0, "mix1")]))

    stats("mix1", "x", done1)
    pl.mm("kv", 0, 0, halves(first), between=[None] + [turn("x", c, 16, done1, "kv", also=[(0, "mix1")]) for c in (4, 6)])
    r = pl.split_ready()
    pl.mm("in1", 1, 0)
    pl.mm("kv", 0, 1, [r])
    kv_done = pl.evac("kv", 0)
    scale_k, k_normed = head_squares("kvn", 4, kv_done)
    dups = [plain("kdup", pr, ("kt1", pr), k_normed, "k") for pr in (0, 2)]
    pl.mm("in1", 1, 1, between=[None, None, scale_k])
    hi_done = pl.evac("in1", 1)
    scale_q, q_normed = head_squares("nat", 8, hi_done, off=8)
    pl.mm("in1", 0, 0, between=[dups[0], dups[1], None, scale_q])
    steps = list(head_steps([("swa", h, 8 + h // 2, 1) for h in range(8, 12)] +
                            [("mem", h, 14 + h // 2, 1) for h in range(4)] +
                            [("swa", h, 8 + h // 2, 1) for h in range(8)]))
    low = []

    def low_norm():
        low.extend(head_norm("nat", 8, pl.evac("in1", 0), off=0))
    qs = [plain("nat", 4, ("qt", 4), q_normed, "q"), plain("nat", 6, ("qt", 6), q_normed, "mq1")]
    woven_mm([("in1", 0, 1, (), low_norm)], [lambda: None] * 2 + qs + steps[:AHEAD_1])
    between = {AHEAD_1 + 1: lambda: low[0](), AHEAD_1 + 2: lambda: low[1](), AHEAD_1 + 5: lambda: low[2](),
               AHEAD_1 + 7: lambda: plain("nat", 0, ("qt", 0), low[3], "q")(),
               AHEAD_1 + 9: lambda: plain("nat", 2, ("qt", 2), low[3], "q")()}
    rest = []
    for i in range(AHEAD_1, len(steps)):
        rest.append((lambda i=i: (between[i](), steps[i]())) if i in between else steps[i])
    placed_mm([("out1", 0, 1, lambda k: [pl.closed[12 + k]]), ("out1", 1, 1, ()),
               ("out1", 0, 0, lambda k: [pl.closed[8 + k]])],
              rest, [n - AHEAD_1 for n in OUT1_AT])
    done0 = pl.evac("out1", 0)
    pl.mm("out1", 1, 0, between=[None] + first_half("mlp1")(done0))
    first, done1 = pl.split_ready(), pl.evac("out1", 1)
    first, done1 = mlp(1, first, done1, "mlp1", first_half("attn2"))

    stats("attn2", "x", done1)
    pl.add("second_block")
    todo = []

    def run(n=1):
        while n and todo:
            step = todo.pop(0)
            if step:
                step()
                n -= 1
    uses = {}

    def level(l, j):
        k = 6 + pl.tick("levels") % 2
        use, full = pl.tick(f"use{k}"), pl.tick(f"full{k}")
        uses[l, j] = (k, use)
        if l == 1:
            scaled = [uses[0, 2 * j], uses[0, 2 * j + 1]]
        else:
            scaled = [uses[l - 1, j if l <= len(LEVELS) else j // 2]] if l else []
        pl.add("level", l=l, j=j, bank=k, use=use, full=full, scaled=scaled)

    def out_heads(q, t):
        k = 6 + t
        pl.tick(f"full{k}")
        pl.add("hg_out", q=q, t=t, bank=k, use=pl.tick(f"use{k}"), full=pl.now(f"full{k}"))

    def bias_rows():
        pl.tick("full6")
        pl.add("bias_rows", use6=pl.tick("use6"), full6=pl.now("full6"))

    hg_normed = []

    def hg_norm():
        hg_normed.append(pl.tick("headnorm"))
        pl.add("hg_norm", n=hg_normed[0])

    def after_group(ng, need):
        nat2 = ("nat2", ng % 2)
        half, sec = ng % 2, ng // 2
        if sec == 0:
            todo.extend(plain(nat2, pr, ("q2", 4 * half + pr), need, scale=P ** -0.5) for pr in (0, 2))
        elif sec == 1:
            todo.extend(plain(nat2, pr, ("f2", 4 * half + pr), need, how="forget") for pr in (0, 2))
        elif sec == 2 and half:
            todo.append(bias_rows)
            for l in range(len(LEVELS) + 2):
                for j in range(2 if 1 <= l <= len(LEVELS) else 4):
                    todo.append(lambda l=l, j=j: level(l, j))
                    if 1 <= l <= len(LEVELS):
                        todo.append(lambda: None)
            todo.append(None)
            for q in (0, 1):
                for t in (0, 1):
                    todo.append(lambda q=q, t=t: out_heads(q, t))
            todo.append(hg_norm)
        elif sec in (3, 4):
            norm = dict(n=0)

            def squares():
                norm["n"] = pl.tick("headnorm")
                pl.add("head_squares2", n=norm["n"], slot=ng % 2, need=need)

            def scale():
                pl.tick("head_scaled")
                pl.add("head_scale2", n=norm["n"], slot=ng % 2)
            nm, g = ("aq", "q2") if sec == 3 else ("ak", "k2")
            todo[1:1] = [squares]
            todo[4:4] = [scale]
            todo[6:6] = [lambda pr=pr: plain(nat2, pr, (nm, 4 * half + pr), ("head_normed", norm["n"]), g)()
                         for pr in (0, 2)]
        elif sec == 6:
            n = pl.tick("hg_gate")
            todo.append(lambda: pl.add("hg_silu", slot=ng % 2, n=n, need=need))
            todo.append(lambda: None)
            todo.append(lambda: pl.add("hg_gate", slot=ng % 2, half=half, n=n, rstd=hg_normed[0]))
        if ng == 13:
            todo.append(lambda: pl.add("bias_tiles"))
            todo.append(lambda: None)
            for i, step in enumerate(head_steps([("moba", h, 8 + h, 2) for h in range(H2)])):
                todo.extend([step, lambda: None] if i % 2 and i < 19 else [step])

    pl.mm("w2", 0, 0, halves(first), between=[None] + [turn("x", c, 0, done1, "attn2") for c in (4, 6)])
    r = pl.split_ready()
    pl.mm("w2", 1, 0)
    whole = []

    def finish():
        while whole:
            ng = whole.pop()
            while ng == 14 and None in todo:
                step = todo.pop(0)
                if step:
                    step()
            after_group(ng, pl.evac("w2", ng))

    def finish_and_run():
        finish()
        run()
    for ng in range(18):
        for kq in (0, 1):
            if ng > 1 or kq:
                pl.mm("w2", ng, kq, [r], between=[finish_and_run] + [run] * (UNIT_K - 1))
        whole.append(ng)
    pl.mm("bat", 0, 0, lambda k: [pl.closed[8 + k]], between=[finish_and_run] + [run] * (UNIT_K - 1))
    while todo:
        run()
    hg_done = ("hg_gated", pl.now("hg_gate"))
    gates = [lambda g=g, h=h: pl.add("gates", branch=g, half=h, n=pl.tick("gates")) for g, h in ((1, 0), (1, 1), (0, 0), (0, 1))]
    turn_oh = [turn("oh", c, 0, hg_done, "hg", one_gain=True) for c in evens]
    gates[0]()
    pl.mm("bat", 0, 1, lambda k: [pl.closed[12 + k]], between=[turn_oh[0], gates[1], turn_oh[1], turn_oh[2]])
    pl.evac("bat", 0)
    pl.mm("bat", 1, 0, between=[turn_oh[3], gates[2], None, gates[3]])
    r = pl.split_ready()
    pl.mm("bat", 1, 1)
    pl.evac("bat", 1)
    m_first, done1 = pair("bhg", [r], first_x=lambda done0: [turn("gate", c, 0, done0) for c in (0, 2)])
    first, done1 = pair("out2", halves(m_first), [turn("gate", c, 0, done1) for c in (4, 6)], first_x=first_half("ffn2"))
    stats("ffn2", "x", done1)

    def turns_g(ng, n, w, need):
        def go(pr):
            b = pl.batch([(("hs2", (n - 1) % 2), pr), (("hs2", (n - 1) % 2), pr + 1)], 8 + 4 * ng + pr, "split", need)
            pl.hs_last["g", n] = b["index"] + 1
        return [lambda: go(0), None, (lambda: go(2)) if w > 2 * P else None]
    last = None
    for ng in range(-(-D_FF2 // NCOL)):
        n = ng + 1
        if ng == 0:
            pl.mm("ffg", 0, 0, halves(first), between=[None] + [turn("x", c, 0, done1, "ffn2") for c in (4, 6)])
            r = pl.split_ready()
            pl.mm("ffu", 0, 0)
            pl.mm("ffg", 0, 1, [r])
        else:
            pl.mm("ffg", ng, 0)
            pl.mm("ffg", ng, 1, between=turns_g(*last))
        pl.evac("ffg", ng, n=n)
        if ng:
            pl.mm("ffu", ng, 0)
        pl.mm("ffu", ng, 1)
        last = (ng, n, min(NCOL, D_FF2 - ng * NCOL), pl.evac("ffu", ng, n=n))
    pl.mm("down2", 0, 0, [pl.split_ready()])
    pl.mm("down2", 1, 0, between=turns_g(*last))
    ready = pl.split_ready()
    for kq in (1, 2, 3, 4):
        pl.mm("down2", 0, kq, [ready])
        if kq < 4:
            pl.mm("down2", 1, kq)
    pl.mm("down2", 0, 5)
    pl.add("store", half=0, need=pl.evac("down2", 0))
    pl.mm("down2", 1, 4)
    pl.mm("down2", 1, 5)
    pl.add("store", half=1, need=pl.evac("down2", 1))

    chunks = [(u, k) for u in pl.units for k in range(u["kn"])]
    steps, hi, lo, c = [], 0, 0, 0
    for st in pl.steps:
        if st["kind"] == "mm":
            c += 1
            for kind in ["split_hi"] * (min(len(chunks), c + min(HI_AHEAD, c + 1)) - hi):
                steps.append(dict(kind=kind, unit=chunks[hi][0], k=chunks[hi][1]))
                hi += 1
                while lo < hi - 1 or lo < hi == len(chunks):
                    steps.append(dict(kind="split_lo", unit=chunks[lo][0], k=chunks[lo][1]))
                    lo += 1
        steps.append(st)
    pl.steps = steps
    return pl


def two_blocks_kernel(nc, a, out, scratch):
    pl = build_plan()
    steps = pl.steps
    with ExitStack() as ctx:
        base = (nc.sbuf_base + 63) // 64 * 64
        room = nc.sbuf_usable_end - base - 32
        ctx.enter_context(nc.sbuf_tensor("whole_map", [P, room // 4], F32))

        def at(name, off, shape, dt=F32):
            return nc.alloc_sbuf_tensor_at(name, [P, *shape], dt, offset=base + off)

        o = 0
        raw = at("raw", o, [RAW_SLOTS, UNIT]); o += RAW_SLOTS * UNIT * 4
        w_hi = at("w_hi", o, [PART_SLOTS, UNIT], F32R); o += PART_SLOTS * UNIT * 4
        w_lo = at("w_lo", o, [PART_SLOTS, UNIT], F32R); o += PART_SLOTS * UNIT * 4
        at_hi = at("at_hi", o, [AT_CHUNKS, SEQ], F32R); o += AT_CHUNKS * SEQ * 4
        upper_hi = o - 16 * SEQ * 4
        at_lo = at("at_lo", o, [AT_CHUNKS, SEQ], F32R); o += AT_CHUNKS * SEQ * 4
        upper_lo = o - 16 * SEQ * 4
        x = at("x_res", o, [TILES, D]); o += TILES * D * 4
        ident = at("ident_sb", o, [P]); o += P * 4
        gt = at("gt", o, [104]); o += 104 * 4
        stat = at("stat", o, [184]); o += 184 * 4
        sink = at("sink_sb", o, [SWA_HEADS]); o += 64
        lb = at("lb", o, [2, H2]); o += 64
        arena = o
        sc = at("sc", o, [SCORE_SLOTS, 512]); o += SCORE_SLOTS * 512 * 4
        pt = at("pt", o, [2, 512]); o += 2 * 512 * 4
        mkv = [at(f"mkv{l}", o + 4096 * l, [TILES, 512]) for l in (0, 1)]; o += 8192
        mkt = [at(f"mkt{l}", o + 2048 * l, [2, SEQ]) for l in (0, 1)]; o += 4096
        nat = at("nat", o, [TILES, D])
        mem = at("mem_sb", o, [TILES, D])
        hs = at("hs", o, [2, TILES, NCOL]); o += 8192
        qt = at("qt", o, [8, SEQ])
        square = at("square", o, [D // 2])
        grows = at("grows", o + 4096, [P])
        kdup = at("kdup", o + 4096, [TILES, KV_HEADS, 2, DH])
        dt = at("dt", o + 2048, [4, SEQ]); o += 8192
        junk = at("junk", o, [D], BF16); o += 2048
        poolp, pwa, pwb = at("poolp_sb", o, [4, 384]), at("pwa", o + 6144, [4, PG]), at("pwb", o + 9216, [4, PG])
        dist, kvn, kt1 = at("dist_sb", o, [384]), at("kvn", o + 1536, [TILES, 512]), at("kt1", o + 5632, [4, SEQ])
        o += 12288
        assert o <= room, (o, room)
        q2, k2 = at("q2", upper_hi, [H2, SEQ]), at("k2", upper_hi + 8192, [H2, SEQ])
        gate = at("gate", upper_hi, [2, TILES, D])
        f2, f2b = at("f2", upper_lo, [H2, SEQ]), at("f2b", upper_lo + 8192, [H2, SEQ // 2])
        attx = at("attx", upper_lo + 12288, [H2, P])
        oh, pt2 = at("oh", upper_lo, [TILES, D]), at("pt2", upper_lo + 8192, [2, 512])
        sgt = at("sgt", upper_lo + 12288, [TILES, 512])
        o = arena
        v2 = at("v2", o, [TILES, D]); ebias = at("ebias", o, [H2, SEQ]); sig2 = at("sig2", o, [TILES, NCOL]); o += 8192
        att = at("att", o, [H2, TILES, P]); sc2 = at("sc2", o, [SCORE_SLOTS, 512]); o += 8192
        aq = at("aq", o, [H2, SEQ]); o += 8192
        ak = at("ak", o, [H2, SEQ])
        rrow, hot, tab = at("rrow", o, [384]), at("hot_sb", o + 1536, [384]), at("tab_sb", o + 3072, [H2]); o += 8192
        av = at("av", o, [TILES, D]); o += 8192
        nat2 = at("nat2", o, [2, TILES, NCOL]); hs2 = at("hs2", o, [2, TILES, NCOL]); o += 8192
        junk2 = at("junk2", o, [D], BF16); o += 2048
        lmask = at("lmask_sb", o, [len(LEVELS), P // 2]); o += len(LEVELS) * P * 2
        assert o <= room, (o, room)

        bank = [ctx.enter_context(nc.psum_tensor(f"bank{i}", [P, 512], F32)) for i in range(8)]

        S = {n: ctx.enter_context(nc.semaphore(n)) for n in (
            "const_in", "x_in", "mem_low_in", "mem_high_in", "grow_in", "sink_in", "pool_in", "swa_in", "block2_in", "bias_in",
            "bias_out", "out_stored",
            "w_hi_ready", "w_lo_ready", "unit_used",
            "evac_act", "evac_dve",
            "t_full", "t_act", "t_dve",
            "full6", "full7", "free6", "free7", "hi7",
            "squares_summed", "rstd_ready", "head_squares", "head_rstd", "head_normed",
            "bias_neg", "probs_raw", "probs_ready",
            "lb_ready", "forget_ready", "squared", "sigmoid_ready", "hg_sig", "hg_silu", "hg_gated", "gates_ready",
            "dve_chain", "act_chain", "pool_chain")}
        raw_in = [ctx.enter_context(nc.semaphore(f"raw_in{i}")) for i in range(RAW_SLOTS)]

        def wait(eng, need):
            eng.wait_ge(S[need[0]], need[1])

        SSQ, VAR, RSTD = 0, 16, 32
        HSS, HR, HALF = 48, 80, 112
        AM, AN, AL, AR, AE = (144 + 2 * SCORE_SLOTS * i for i in range(5))

        def col(c, n=1):
            return stat[:, c:c + n]

        norm_no = {st["name"]: st["n"] for st in steps if st["kind"] == "stats"}
        norm_of = {"mem0": "mem", "mem1": "mem", "in0": "x0", "kv": "mix1", "in1": "mix1", "w2": "attn2",
                   "ffg": "ffn2", "ffu": "ffn2", "up00": "mlp0", "up01": "mlp0", "up10": "mlp1", "up11": "mlp1"}

        def rstd_col(gemm):
            return RSTD + 2 * (norm_no[norm_of[gemm]] - 1)

        weights = {"mem0": a["w_mem_kv"][0], "mem1": a["w_mem_kv"][1], "in0": a["w_in"][0], "in1": a["w_in"][1],
                   "out0": a["w_out"][0], "out1": a["w_out"][1], "kv": a["w_kv"], "w2": a["w_in_2"][0],
                   "bhg": a["w_branch_hg_2"][0], "bat": a["w_branch_attn_2"][0], "out2": a["w_out_2"][0],
                   "ffg": a["w_ffn_gate_2"][0], "ffu": a["w_ffn_up_2"][0], "down2": a["w_ffn_down_2"][0]}
        for l in (0, 1):
            for half in (0, 1):
                n = D_FF // 2
                weights[f"up{l}{half}"] = a["w_up"][l][:, half * n:(half + 1) * n]
                weights[f"down{l}{half}"] = a["w_down"][l][half * n:(half + 1) * n, :]
        w2_order = [0, 1, 2, 3, 4, 5, 8, 9, 10, 11, 12, 13, 6, 7, 14, 15, 16, 17]

        def unit_ap(buf, slot, u):
            return buf[:, slot, 0:u["kn"] * u["w"]].rearrange("p (k n) -> p k n", k=u["kn"])

        def acc(g, t):
            return bank[2 * (g["index"] % 2) + t]

        def t_bank(b):
            return bank[4 + b["index"] % 2]

        natural = {"x": x, "mem": mem, "nat": nat, "oh": oh, "mkv0": mkv[0], "mkv1": mkv[1], "kvn": kvn}
        slotted = {"hs": hs, "nat2": nat2, "hs2": hs2}
        turned = {"qt": qt, "kt1": kt1, "mkt0": mkt[0], "mkt1": mkt[1], "q2": q2, "f2": f2, "aq": aq, "ak": ak}

        def chunk_of(src, t):
            name, c = src
            if name == "kdup":
                return kdup[:, t, c].rearrange("p two d -> p (two d)")
            if name == "gate":
                return gate[:, 0, t, c * P:(c + 1) * P]
            if isinstance(name, tuple):
                return slotted[name[0]][:, name[1], t, c * P:(c + 1) * P]
            return natural[name][:, t, c * P:(c + 1) * P]

        def segments(kind):
            return ((0, 0, 256), (1, 256, 256)) if kind == "mem" else ((0, 0, 128), (1, 128, 256))

        def prob_blocks(kind):
            if kind == "mem":
                return tuple((t * 256 + m * P, m, m * 256 + t * P, t) for m in (0, 1) for t in (0, 1))
            return ((0, 0, 0, 0), (128, 0, 128, 1), (256, 1, 256, 1))

        def scores_buf(hd):
            return (sc2 if hd["type"] == "moba" else sc)[:, (hd["a"] - 1) % SCORE_SLOTS]

        def pt_buf(hd):
            return (pt2 if hd["type"] == "moba" else pt)[:, (hd["a"] - 1) % 2]

        def pool_pieces(gi):
            cut = P if gi % 2 == 0 else P // 2
            for c0, c1 in ((0, cut), (cut, PG)):
                f = PG * gi + c0
                yield c0, c1, slice(f % P, f % P + c1 - c0), f // P

        def settle(eng, st):
            for name, count in (("t_full", "t_full"), ("full6", "full6"), ("full7", "full7"),
                                ("evac_dve", "evac_dve")):
                if st["at"].get(count):
                    eng.wait_ge(S[name], st["at"][count])

        last_level = {st["bank"]: st["use"] for st in steps if st["kind"] == "level"}

        block = ctx.enter_context(nc.Block())

        @block.sync
        def _(sp):
            sp.dma_start(ident[:], a["ident"]).then_inc(S["const_in"], 16)
            sp.dma_start(grows[0:N_GAINS], a["gains"]).then_inc(S["grow_in"], 16)
            for half, sem in ((slice(0, D // 2), "mem_low_in"), (slice(D // 2, D), "mem_high_in")):
                sp.dma_start(mem[:, :, half], a["mem"][0].rearrange("(t p) d -> p t d", p=P)[:, :, half]
                             ).then_inc(S[sem], 16)
            for st in steps:
                if st["kind"] == "split_hi" and st["k"] == 0:
                    u = st["unit"]
                    slot = u["index"] % RAW_SLOTS
                    if u["index"] >= RAW_SLOTS:
                        sp.wait_ge(S["w_lo_ready"], pl.units[u["index"] - RAW_SLOTS + 1]["c0"])
                    n0 = u["n0"] if u["gemm"] != "w2" else w2_order[u["n0"] // NCOL] * NCOL
                    src = weights[u["gemm"]][u["k0"] * P:(u["k0"] + u["kn"]) * P, n0:n0 + u["w"]]
                    sp.dma_start(unit_ap(raw, slot, u), src.rearrange("(k p) n -> p k n", p=P)).then_inc(raw_in[slot], 16)
                    if u["index"] == 0:
                        sp.dma_start(x[:], a["x"][0].rearrange("(t p) d -> p t d", p=P)).then_inc(S["x_in"], 16)
                elif st["kind"] == "store":
                    wait(sp, st["need"])
                    h = slice(st["half"] * NCOL, (st["half"] + 1) * NCOL)
                    sp.dma_start(out[0].rearrange("(t p) d -> p t d", p=P)[:, :, h], x[:, :, h]).then_inc(S["out_stored"], 16)
            sp.wait_ge(S["out_stored"], 32)

        @block.gpsimd
        def _(pool):
            chain = [0]

            def link(ins):
                ins.then_inc(S["pool_chain"], 1)
                chain[0] += 1
                pool.wait_ge(S["pool_chain"], chain[0])

            link(pool.memset(stat[:, HALF:HALF + 32], -0.5))
            for st in steps:
                kind = st["kind"]
                if kind == "stats":
                    c = 2 * (st["n"] - 1)
                    pool.wait_ge(S["squares_summed"], st["n"])
                    link(pool.tensor_scalar(col(VAR + c, 2), col(SSQ + c, 2), 1.0 / D, EPS, ALU.mult, ALU.add))
                    pool.tensor_tensor(col(RSTD + c, 2), col(VAR + c, 2), col(HALF, 2), ALU.pow
                                       ).then_inc(S["rstd_ready"], 1)
                    if st["name"] == "mlp0":
                        settle(pool, st)
                        pool.dma_start(dist[:], a["dist"]).then_inc(S["swa_in"], 16)
                elif kind in ("head_squares", "head_squares2", "hg_norm") and st.get("t") != 0:
                    cols = {"head_squares": TILES * st.get("heads", 0), "head_squares2": TILES * 4, "hg_norm": TILES * H2}[kind]
                    pool.wait_ge(S["head_squares"], st["n"])
                    link(pool.tensor_scalar(col(HSS, cols), col(HSS, cols), 1.0 / (DH if kind == "head_squares" else P), EPS,
                                            ALU.mult, ALU.add))
                    pool.tensor_tensor(col(HR, cols), col(HSS, cols), col(HALF, cols), ALU.pow
                                       ).then_inc(S["head_rstd"], 1)
                elif kind == "evac" and st["group"]["how"] == "relu":
                    h = hs[:, (st["hs"] - 1) % 2]
                    pool.wait_ge(S["evac_act"], st["group"]["done"])
                    pool.tensor_tensor(h, h, h, ALU.mult).then_inc(S["squared"], 1)
                elif kind == "hg_silu":
                    g_ = nat2[:, st["slot"]]
                    pool.wait_ge(S["hg_sig"], st["n"])
                    pool.tensor_tensor(g_, g_, sgt[:], ALU.mult).then_inc(S["hg_silu"], 1)
                elif kind == "second_block":
                    settle(pool, st)
                    pool.wait_ge(S["rstd_ready"], st["at"]["stats"])
                    link(pool.memset(tab[BUCKETS:BUCKETS + 1], NEG))
                    pool.dma_start(tab[0:BUCKETS], a["rel_bias_table_2"]).then_inc(S["block2_in"], 16)
                    pool.dma_start(hot[0:BUCKETS + 1], a["hot"]).then_inc(S["block2_in"], 16)
                    pool.dma_start(lmask[:], a["lmask"]).then_inc(S["block2_in"], 16)
                elif kind == "bias_rows":
                    pool.wait_ge(S["free6"], st["use6"])
                    pool.dma_start(scratch, rrow[0:H2, :]).then_inc(S["bias_out"], 16)
                elif kind == "bias_tiles":
                    settle(pool, st)
                    pool.wait_ge(S["bias_out"], 16)
                    src = bass.AP(tensor=scratch.tensor, offset=0, ap=[[1, P], [384, H2], [1, SEQ]])
                    pool.dma_start(ebias[:], src).then_inc(S["bias_in"], 16)
            pool.wait_ge(S["bias_out"], 16)

        @block.scalar
        def _(act):
            chain = [0]

            def tick(ins):
                ins.then_inc(S["act_chain"], 1)
                chain[0] += 1

            for st in steps:
                kind = st["kind"]
                if kind == "split_hi":
                    u = st["unit"]
                    i = u["index"]
                    n = slice(st["k"] * u["w"], (st["k"] + 1) * u["w"])
                    if st["k"] == 0:
                        act.wait_ge(raw_in[i % RAW_SLOTS], 16 * (i // RAW_SLOTS + 1))
                        if i >= PART_SLOTS:
                            act.wait_ge(S["unit_used"], i - PART_SLOTS + 1)
                    act.activation(w_hi[:, i % PART_SLOTS, n], raw[:, i % RAW_SLOTS, n], ACT.Copy
                                   ).then_inc(S["w_hi_ready"], 1)
                elif kind == "gains":
                    act.wait_ge(S["lb_ready"], 1)
                    act.activation(lb[:, 0, :], lb[:, 1, :], ACT.Sigmoid).then_inc(S["lb_ready"], 1)
                elif kind == "stats":
                    for need in st["need"]:
                        wait(act, need)
                    if st["n"] > 1:
                        act.wait_ge(S["squares_summed"], st["n"] - 1)
                    if st["name"] == "ffn2":
                        settle(act, st)
                    if st["name"] == "mem":
                        act.dma_start(poolp[:], a["poolp"]).then_inc(S["pool_in"], 16)
                        pw = a["pool_w"][0].rearrange("g c d -> c g d")
                        act.dma_start(pwa[:], pw[0:P]).then_inc(S["pool_in"], 16)
                        act.dma_start(pwb[0:PG - P], pw[P:PG]).then_inc(S["pool_in"], 16)
                        act.dma_start(sink[:], a["sinks"][0].partition_broadcast(P)).then_inc(S["sink_in"], 16)
                    buf = natural[st["src"]]
                    tick(act.activation(junk[:], buf[:, 0, :], ACT.Square, accum_out=col(SSQ + 2 * (st["n"] - 1))))
                    act.wait_ge(S["act_chain"], chain[0])
                    act.activation(junk[:], buf[:, 1, :], ACT.Square, accum_out=col(SSQ + 2 * (st["n"] - 1) + 1)
                                   ).then_inc(S["squares_summed"], 1)
                elif kind == "evac" and st["group"]["how"] in ("nat", "relu", "w2", "ffg"):
                    g = st["group"]
                    how, ng, w = g["how"], g["ng"], g["w"]
                    act.wait_ge(S["unit_used"], g["last_unit"])
                    act.wait_ge(S["rstd_ready"], norm_no[norm_of[g["gemm"]]])
                    r = rstd_col(g["gemm"])
                    func, done = ACT.Copy, "evac_act"
                    if how == "nat":
                        settle(act, st)
                        dst = {"mem0": mkv[0], "mem1": mkv[1], "kv": kvn}.get(g["gemm"])
                        if dst is None:
                            dst = nat[:, :, g["n0"]:g["n0"] + w]
                    elif how == "relu":
                        func = ACT.Relu
                        dst = hs[:, (st["hs"] - 1) % 2]
                        if st["hs"] > 2:
                            act.wait_ge(S["t_full"], pl.hs_last[st["hs"] - 2])
                        else:
                            settle(act, st)
                    elif how == "ffg":
                        func, done = ACT.Sigmoid, "sigmoid_ready"
                        dst = sig2[:, :, 0:w]
                        act.wait_ge(S["evac_dve"], st["at"]["evac_dve"])
                    else:
                        half, sec = ng % 2, ng // 2
                        cols = slice(half * NCOL, (half + 1) * NCOL)
                        if sec == 2:
                            dst = v2[:, :, cols]
                        elif sec == 5:
                            dst = av[:, :, cols]
                        elif sec >= 7:
                            dst = gate[:, sec - 7, :, cols]
                            if ng == 14:
                                act.wait_ge(S["free6"], st["at"]["use6"])
                                act.wait_ge(S["free7"], st["at"]["use7"])
                        else:
                            dst = nat2[:, ng % 2]
                        if st["at"].get("t_full"):
                            act.wait_ge(S["t_full"], st["at"]["t_full"])
                        if sec == 6:
                            act.wait_ge(S["head_normed"], st["at"]["head_scaled"])
                    for t in range(TILES):
                        ins = act.activation(dst[:, t, :], acc(g, t)[:, 0:w], func, scale=col(r + t))
                    ins.then_inc(S[done], 1)
                elif kind == "batch" and st.get("part") != "product":
                    b = st["batch"]
                    how, tb = b["how"], t_bank(b)
                    act.wait_ge(S["t_full"], b["index"] + 1)
                    if how == "split":
                        for dst, gains in b["splits"]:
                            if gains is None:
                                ins = act.activation(at_hi[:, dst:dst + 2, :], tb[:], ACT.Copy)
                                continue
                            for i in (0, 1):
                                ins = act.activation(at_hi[:, dst + i, :], tb[:, i * SEQ:(i + 1) * SEQ], ACT.Copy,
                                                     scale=gt[:, gains[i]:gains[i] + 1])
                    elif how == "plain":
                        nm, c = b["dst"]
                        if nm == "ak":
                            act.wait_ge(S["bias_out"], 16)
                        kw = dict(scale=gt[:, b["gains"][0]:b["gains"][0] + 1]) if b["gains"] else \
                            dict(scale=b["scale"]) if b["scale"] else {}
                        ins = act.activation(turned[nm][:, c:c + 2, :], tb[:], ACT.Copy, **kw)
                    elif how == "values":
                        n = b["chunks"]
                        ins = act.activation(at_hi[:, b["dst"]:b["dst"] + n, :], tb[:, 0:n * SEQ], ACT.Copy)
                    elif how == "forget":
                        c = b["dst"][1]
                        act.activation(f2[:, c:c + 2, :], tb[:], ACT.Sigmoid)
                        ins = act.activation(k2[:, c:c + 2, :], tb[:], ACT.Sigmoid, scale=-1.0)
                    else:
                        hd = b["head"]
                        if hd["a"] > 2:
                            act.wait_ge(S["t_full"], pl.value_batch[hd["a"] - 2])
                        n = 512 if hd["type"] == "mem" else 384
                        ins = act.activation(pt_buf(hd)[:, 0:n], tb[:, 0:n], ACT.Copy)
                    ins.then_inc(S["t_act"], 1)
                elif kind == "softmax":
                    st = st["head"]
                    buf, s = scores_buf(st), (st["a"] - 1) % SCORE_SLOTS
                    act.wait_ge(S["bias_neg"], st["a"])
                    for i, (t, c0, n) in enumerate(segments(st["type"])):
                        ins = act.activation(buf[:, c0:c0 + n], buf[:, c0:c0 + n], ACT.Exp,
                                             scale=1.0 if st["type"] == "moba" else DH ** -0.5,
                                             bias=col(AN + 2 * s + i), accum_out=col(AL + 2 * s + i))
                    if st["type"] == "swa":
                        act.wait_ge(S["sink_in"], 16)
                        ins = act.activation(col(AE + 2 * s, 2), col(AN + 2 * s, 2), ACT.Exp,
                                             bias=sink[:, st["h"]:st["h"] + 1])
                    ins.then_inc(S["probs_raw"], 1)
                elif kind == "pool_mix":
                    act.wait_ge(S["full7"], st["full7"])
                    for i, (c0, c1, rows, ch) in enumerate(pool_pieces(st["gi"])):
                        gc = GAIN_ROWS["pool"][0] + ch
                        ins = act.activation(at_hi[rows, 8 + ch, :], bank[7][rows, i * SEQ:(i + 1) * SEQ], ACT.Copy,
                                             scale=gt[rows, gc:gc + 1])
                    ins.then_inc(S["hi7"], 1)
                elif kind in ("head_squares2", "hg_norm"):
                    act.wait_ge(S["head_rstd"], st["n"] - 1)
                    act.wait_ge(S["head_normed"], st["at"]["head_scaled"])
                    if kind == "hg_norm":
                        act.wait_ge(S["free6"], st["at"]["use6"])
                        act.wait_ge(S["free7"], st["at"]["use7"])
                    else:
                        wait(act, st["need"])
                    for half in range(2 if kind == "hg_norm" else 1):
                        for t in range(TILES):
                            for h in range(4):
                                j = t * 4 + h
                                if kind == "hg_norm":
                                    hh = 4 * half + h
                                    src, dst = oh[:, t, hh * P:(hh + 1) * P], HSS + t * H2 + hh
                                else:
                                    src, dst = nat2[:, st["slot"], t, h * P:(h + 1) * P], HSS + j
                                ins = act.activation(junk2[:, j * P:(j + 1) * P], src, ACT.Square, accum_out=col(dst))
                        if half == 0 and kind == "hg_norm":
                            tick(ins)
                            act.wait_ge(S["act_chain"], chain[0])
                    ins.then_inc(S["head_squares"], 1)
                    act.wait_ge(S["head_squares"], st["n"])
                elif kind == "hg_silu":
                    wait(act, st["need"])
                    if st["n"] > 1:
                        act.wait_ge(S["hg_silu"], st["n"] - 1)
                    act.activation(sgt[:], nat2[:, st["slot"]], ACT.Sigmoid).then_inc(S["hg_sig"], 1)
                elif kind == "gates":
                    act.wait_ge(S["evac_act"], pl.group_of["w2", 17]["done"])
                    part = gate[:, st["branch"], :, st["half"] * NCOL:(st["half"] + 1) * NCOL]
                    act.activation(part, part, ACT.Sigmoid).then_inc(S["gates_ready"], 1)

        @block.tensor
        def _(pe):
            def take_bank(k, use):
                if use > 1:
                    pe.wait_ge(S[f"free{k}"], use - 1)

            for st in steps:
                kind = st["kind"]
                if kind == "gains":
                    pe.wait_ge(S["const_in"], 16)
                    pe.wait_ge(S["grow_in"], 16)
                    pe.transpose(bank[6][:, 0:N_GAINS], grows[0:N_GAINS], ident[0:N_GAINS, 0:N_GAINS]).then_inc(S["full6"], 1)
                elif kind == "mm":
                    u, g = st["unit"], st["group"]
                    for need in st["need"]:
                        wait(pe, need)
                    pe.wait_ge(S["w_lo_ready"], u["c0"] + st["k"] + 1)
                    if st["start"]:
                        for e in ("act", "dve"):
                            if g["free"][e]:
                                pe.wait_ge(S["evac_" + e], g["free"][e])
                    slot, k = u["index"] % PART_SLOTS, st["k"]
                    wh, wl = unit_ap(w_hi, slot, u)[:, k, :], unit_ap(w_lo, slot, u)[:, k, :]
                    kc, first = u["k0"] + k, GEMMS[g["gemm"]][2]
                    ch = h_slot(16 * int(g["gemm"][-1]) + kc) if first is None else first + kc
                    for t in range(TILES):
                        tok = slice(t * P, (t + 1) * P)
                        sums = acc(g, t)[:, 0:u["w"]]
                        pe.matmul(sums, at_hi[:, ch, tok], wh, start=st["start"], stop=False)
                        pe.matmul(sums, at_hi[:, ch, tok], wl, start=False, stop=False)
                        ins = pe.matmul(sums, at_lo[:, ch, tok], wh, start=False, stop=st["stop"])
                    if k == u["kn"] - 1:
                        ins.then_inc(S["unit_used"], 1)
                elif kind == "batch" and st.get("part") != "take":
                    b = st["batch"]
                    wait(pe, b["need"])
                    if b["how"] not in ("probs", "values") and b["src"][0][0] in ("x", "mem"):
                        name, c = b["src"][0]
                        pe.wait_ge(S["x_in" if name == "x" else "mem_low_in" if c < DCH // 2 else "mem_high_in"], 16)
                    if "free" in b:
                        wait(pe, b["free"])
                    tb = t_bank(b)
                    if b["how"] == "probs":
                        for c, _, d, _ in prob_blocks(b["head"]["type"]):
                            ins = pe.transpose(tb[:, d:d + P], scores_buf(b["head"])[:, c:c + P], ident[:])
                    elif b["how"] == "values":
                        for m, hd in enumerate(b["src"]):
                            h, rows, place = hd["h"], slice(DH * m, DH * (m + 1)), 0
                            if hd["type"] == "mem":
                                buf, c0, n = mkv[hd["layer"]], MEM_HEADS * DH + DH * h, DH
                            elif hd["type"] == "swa":
                                buf, c0, n = kvn, KV_HEADS * DH + DH * (h // (SWA_HEADS // KV_HEADS)), DH
                            else:
                                buf, c0, n, rows, place = av, h * P, P, slice(0, P), m * SEQ
                            for t in range(TILES):
                                mine = [blk for blk in prob_blocks(hd["type"]) if blk[3] == t]
                                for i, (_, kt, d, _) in enumerate(mine):
                                    ins = pe.matmul(tb[rows, place + t * P:place + (t + 1) * P], buf[:, kt, c0:c0 + n],
                                                    pt_buf(hd)[:, d:d + P], start=i == 0, stop=i == len(mine) - 1)
                    else:
                        for i in (0, 1):
                            for t in range(TILES):
                                c = i * SEQ + t * P
                                ins = pe.transpose(tb[:, c:c + P], chunk_of(b["src"][i], t), ident[:])
                    ins.then_inc(S["t_full"], 1)
                elif kind == "pool_diff":
                    pe.wait_ge(S["pool_in"], 48)
                    wait(pe, st["need"])
                    take_bank(6, st["use6"])
                    gi = st["gi"]
                    for i, (c0, c1) in enumerate(((0, P), (P, PG))):
                        ch = slice(PG * gi + c0, PG * gi + c1)
                        rows = slice(0, c1 - c0)
                        early, later = (bank[6][rows, i * SEQ + j * P:i * SEQ + (j + 1) * P] for j in (0, 1))
                        pe.matmul(early, nat[:, 0, ch], poolp[:, gi, 0:P], start=True, stop=True)
                        pe.matmul(later, nat[:, 0, ch], poolp[:, gi, P:SEQ], start=True, stop=False)
                        ins = pe.matmul(later, nat[:, 1, ch], poolp[:, gi, SEQ:SEQ + P], start=False, stop=True)
                    ins.then_inc(S["full6"], 1)
                elif kind == "pool_mix":
                    take_bank(7, st["use7"])
                    pe.wait_ge(S["free6"], st["diff"])
                    s, gi = 2 * (st["gi"] % 2), st["gi"]
                    for i, (c0, c1, rows, ch) in enumerate(pool_pieces(gi)):
                        mixed = bank[7][rows, i * SEQ:(i + 1) * SEQ]
                        pe.matmul(mixed, pwa[:, gi, c0:c1], dt[:, s, :], start=True, stop=False)
                        ins = pe.matmul(mixed, pwb[0:PG - P, gi, c0:c1], dt[0:PG - P, s + 1, :], start=False, stop=True)
                    ins.then_inc(S["full7"], 1)
                elif kind == "scores":
                    needs = st["need"]
                    st = st["head"]
                    take_bank(st["bank"], st["use"])
                    h = st["h"]
                    rows = slice(DH * (h % 2), DH * (h % 2) + DH)
                    if st["type"] == "mem":
                        q, k = qt[rows, 6 + h // 2, :], mkt[st["layer"]][rows, h // 2, :]
                    elif st["type"] == "swa":
                        q, k = qt[rows, h // 2, :], kt1[rows, h // (SWA_HEADS // KV_HEADS), :]
                    else:
                        q, k = aq[:, h, :], ak[:, h, :]
                    for need in needs:
                        wait(pe, need)
                    for t, c0, n in segments(st["type"]):
                        ins = pe.matmul(bank[st["bank"]][:, c0:c0 + n], q[:, t * P:(t + 1) * P], k[:, 0:n], start=True, stop=True)
                    ins.then_inc(S[f"full{st['bank']}"], 1)
                elif kind == "bias_rows":
                    take_bank(6, st["use6"])
                    pe.wait_ge(S["block2_in"], 48)
                    pe.matmul(bank[6][0:H2, 0:384], tab[0:BUCKETS + 1, :], hot[0:BUCKETS + 1, :], start=True, stop=True
                              ).then_inc(S["full6"], 1)
                elif kind == "level":
                    l, j, bk = st["l"], st["j"], bank[st["bank"]]
                    take_bank(st["bank"], st["use"])
                    if l == 0:
                        pe.wait_ge(S["t_act"], st["at"]["t_act"])
                        pe.wait_ge(S["forget_ready"], j + 1)
                    else:
                        for k, use in st["scaled"]:
                            pe.wait_ge(S[f"free{k}"], use)
                    if l == 0:
                        for i in range(4):
                            h, tok = 2 * j + i // 2, slice(i % 2 * P, (i % 2 + 1) * P)
                            ins = pe.matmul(bk[:, i * P:(i + 1) * P], k2[:, h, tok], q2[:, h, tok], start=True, stop=True)
                    elif l <= len(LEVELS):
                        for i in range(8):
                            h, tok = 4 * j + i // 2, slice(i % 2 * P, (i % 2 + 1) * P)
                            later = q2[:, h, tok].rearrange("p (b two n) -> p b two n", two=2, n=LEVELS[l - 1])[:, :, 1, :]
                            ins = pe.matmul(bk[:, i * P // 2:(i + 1) * P // 2], k2[:, h, tok], later, start=True, stop=True)
                    else:
                        for i in (0, 1):
                            ins = pe.matmul(bk[:, i * P:(i + 1) * P], k2[:, 2 * j + i, 0:P], q2[:, 2 * j + i, P:SEQ],
                                            start=True, stop=True)
                    ins.then_inc(S[f"full{st['bank']}"], 1)
                elif kind == "hg_out":
                    take_bank(st["bank"], st["use"])
                    pe.wait_ge(S["evac_act"], pl.group_of["w2", 5]["done"])
                    pe.wait_ge(S["free6"], last_level[6])
                    pe.wait_ge(S["free7"], last_level[7])
                    for i in range(4):
                        h = 4 * st["q"] + i
                        sums, vs = bank[st["bank"]][:, i * P:(i + 1) * P], slice(h * P, (h + 1) * P)
                        if st["t"] == 0:
                            ins = pe.matmul(sums, att[:, h, 0, :], v2[:, 0, vs], start=True, stop=True)
                        else:
                            pe.matmul(sums, attx[:, h, :], v2[:, 0, vs], start=True, stop=False)
                            ins = pe.matmul(sums, att[:, h, 1, :], v2[:, 1, vs], start=False, stop=True)
                    ins.then_inc(S[f"full{st['bank']}"], 1)

        @block.vector
        def _(dve):
            chain = [0]

            def tick(ins):
                ins.then_inc(S["dve_chain"], 1)
                chain[0] += 1

            def link(ins):
                tick(ins)
                dve.wait_ge(S["dve_chain"], chain[0])

            for st in steps:
                kind = st["kind"]
                if kind == "gains":
                    dve.wait_ge(S["full6"], 1)
                    dve.tensor_copy(gt[:, 0:N_GAINS], bank[6][:, 0:N_GAINS]).then_inc(S["free6"], 1)
                    dve.wait_ge(S["free6"], 1)
                    c0, c1 = GAIN_ROWS["lb0"][0], GAIN_ROWS["lb1"][0]
                    dve.tensor_tensor(lb[:, 1, :], gt[:, c0:c0 + H2], gt[:, c1:c1 + H2], ALU.subtract
                                      ).then_inc(S["lb_ready"], 1)
                    dve.wait_ge(S["lb_ready"], 2)
                    link(dve.tensor_scalar(lb[:, 1, :], lb[:, 0, :], -1.0, 1.0, ALU.mult, ALU.add))
                elif kind == "split_lo":
                    u = st["unit"]
                    i = u["index"]
                    n = slice(st["k"] * u["w"], (st["k"] + 1) * u["w"])
                    dve.wait_ge(S["w_hi_ready"], u["c0"] + st["k"] + 1)
                    dve.tensor_tensor(w_lo[:, i % PART_SLOTS, n], raw[:, i % RAW_SLOTS, n],
                                      w_hi[:, i % PART_SLOTS, n].bitcast(F32), ALU.subtract
                                      ).then_inc(S["w_lo_ready"], 1)
                elif kind == "batch" and st["batch"]["how"] == "values" and st["part"] == "take":
                    b = st["batch"]
                    chunks = slice(b["dst"], b["dst"] + b["chunks"])
                    dve.wait_ge(S["t_act"], b["act"])
                    dve.tensor_tensor(at_lo[:, chunks, :].rearrange("p c n -> p (c n)"), t_bank(b)[:, 0:b["chunks"] * SEQ],
                                      at_hi[:, chunks, :].rearrange("p c n -> p (c n)").bitcast(F32), ALU.subtract
                                      ).then_inc(S["t_dve"], 1)
                elif kind == "batch" and st["batch"]["how"] == "split":
                    b = st["batch"]
                    dve.wait_ge(S["t_act"], b["act"])
                    for dst, gains in b["splits"]:
                        if gains is None:
                            ins = dve.tensor_tensor(at_lo[:, dst:dst + 2, :].rearrange("p c n -> p (c n)"), t_bank(b)[:],
                                                    at_hi[:, dst:dst + 2, :].rearrange("p c n -> p (c n)").bitcast(F32),
                                                    ALU.subtract)
                            continue
                        for i in (0, 1):
                            hi = at_hi[:, dst + i, :].bitcast(F32)
                            ins = dve.scalar_tensor_tensor(at_lo[:, dst + i, :], t_bank(b)[:, i * SEQ:(i + 1) * SEQ],
                                                           gt[:, gains[i]:gains[i] + 1], hi, ALU.mult, ALU.subtract)
                    ins.then_inc(S["t_dve"], 1)
                elif kind == "batch" and st["batch"]["how"] == "forget":
                    b = st["batch"]
                    dve.wait_ge(S["t_act"], b["act"])
                    for h in (b["dst"][1], b["dst"][1] + 1):
                        dve.tensor_scalar(f2[:, h, :], f2[:, h, :], lb[:, 1, h:h + 1], lb[:, 0, h:h + 1], ALU.mult, ALU.add)
                        ins = dve.tensor_scalar(k2[:, h, :], k2[:, h, :], lb[:, 1, h:h + 1], None, ALU.mult)
                    ins.then_inc(S["forget_ready"], 1)
                elif kind == "evac" and st["group"]["how"] == "res":
                    g = st["group"]
                    dve.wait_ge(S["unit_used"], g["last_unit"])
                    dve.wait_ge(S["squares_summed"], st["at"]["stats"])
                    dve.wait_ge(S["t_full"], st["at"]["t_full"])
                    if st["at"].get("evac_dve"):
                        dve.wait_ge(S["evac_dve"], st["at"]["evac_dve"])
                    for t in range(TILES):
                        xs = x[:, t, g["n0"]:g["n0"] + NCOL]
                        ins = dve.tensor_tensor(xs, xs, acc(g, t)[:], ALU.add)
                    ins.then_inc(S["evac_dve"], 1)
                elif kind == "evac" and st["group"]["how"] == "gate":
                    g = st["group"]
                    branch = 0 if g["gemm"] == "bhg" else 1
                    cols = slice(g["n0"], g["n0"] + NCOL)
                    dve.wait_ge(S["unit_used"], g["last_unit"])
                    dve.wait_ge(S["gates_ready"], 2 * (1 - branch) + g["ng"] + 1)
                    for t in range(TILES):
                        ins = dve.tensor_tensor(gate[:, branch, t, cols], gate[:, branch, t, cols], acc(g, t)[:], ALU.mult)
                    if branch == 0:
                        link(ins)
                        ins = dve.tensor_tensor(gate[:, 0, :, cols], gate[:, 0, :, cols], gate[:, 1, :, cols], ALU.add)
                    ins.then_inc(S["evac_dve"], 1)
                elif kind == "evac" and st["group"]["how"] in ("ffg", "ffu"):
                    g = st["group"]
                    n, w, r = st["n"], g["w"], rstd_col("ffg")
                    buf = hs2[:, (n - 1) % 2]
                    if g["how"] == "ffg":
                        dve.wait_ge(S["sigmoid_ready"], n)
                        if n > 2:
                            dve.wait_ge(S["t_full"], pl.hs_last["g", n - 2])
                        else:
                            settle(dve, st)
                    else:
                        dve.wait_ge(S["unit_used"], g["last_unit"])
                        dve.wait_ge(S["evac_dve"], g["done"] - 1)
                    for t in range(TILES):
                        other = sig2[:, t, 0:w] if g["how"] == "ffg" else buf[:, t, 0:w]
                        ins = dve.scalar_tensor_tensor(buf[:, t, 0:w], acc(g, t)[:, 0:w], col(r + t), other,
                                                       ALU.mult, ALU.mult)
                    ins.then_inc(S["evac_dve"], 1)
                elif kind == "head_squares":
                    src, heads, n, t = natural[st["src"]], st["heads"], st["n"], st["t"]
                    cols = slice(st["off"] * DH, (st["off"] + heads) * DH)
                    if t == 0:
                        wait(dve, st["need"])
                        settle(dve, st)
                        if n > 1:
                            dve.wait_ge(S["head_rstd"], n - 1)
                    link(dve.tensor_tensor(square[:, 0:heads * DH], src[:, t, cols], src[:, t, cols], ALU.mult))
                    ins = dve.tensor_reduce(col(HSS + t * heads, heads),
                                            square[:, 0:heads * DH].rearrange("p (h d) -> p h d", d=DH), AX_X, ALU.add)
                    if t == TILES - 1:
                        ins.then_inc(S["head_squares"], 1)
                    else:
                        link(ins)
                elif kind == "head_scale":
                    src, heads, n = natural[st["src"]], st["heads"], st["n"]
                    cols = slice(st["off"] * DH, (st["off"] + heads) * DH)
                    dve.wait_ge(S["head_rstd"], n)
                    for t in range(TILES):
                        s_ = src[:, t, cols].rearrange("p (h d) -> p h d", d=DH)
                        r_ = col(HR + t * heads, heads).unsqueeze(2).to_broadcast([P, heads, DH])
                        if src is kvn:
                            both = [P, heads, 2, DH]
                            ins = dve.tensor_tensor(kdup[:, t], s_.unsqueeze(2).to_broadcast(both),
                                                    r_.unsqueeze(2).to_broadcast(both), ALU.mult)
                        else:
                            ins = dve.tensor_tensor(s_, s_, r_, ALU.mult)
                    ins.then_inc(S["head_normed"], 1)
                elif kind == "head_scale2":
                    n_h, src = 4, nat2[:, st["slot"]]
                    dve.wait_ge(S["head_rstd"], st["n"])
                    for t in range(TILES):
                        s_ = src[:, t, :].rearrange("p (h d) -> p h d", d=P)
                        r_ = col(HR + t * n_h, n_h).unsqueeze(2).to_broadcast([P, n_h, P])
                        ins = dve.tensor_tensor(s_, s_, r_, ALU.mult)
                    ins.then_inc(S["head_normed"], 1)
                elif kind == "hg_gate":
                    dve.wait_ge(S["hg_silu"], st["n"])
                    dve.wait_ge(S["head_rstd"], st["rstd"])
                    for t in range(TILES):
                        for i in range(4):
                            h = 4 * st["half"] + i
                            o_ = oh[:, t, h * P:(h + 1) * P]
                            ins = dve.scalar_tensor_tensor(o_, o_, col(HR + t * H2 + h), nat2[:, st["slot"], t, i * P:(i + 1) * P],
                                                           ALU.mult, ALU.mult)
                    ins.then_inc(S["hg_gated"], 1)
                elif kind == "pool_diff":
                    s = 2 * (st["gi"] % 2)
                    dve.wait_ge(S["full6"], st["full6"])
                    if st["gi"] > 1:
                        dve.wait_ge(S["full7"], st["gi"] - 1)
                    dve.tensor_copy(dt[:, s, :], bank[6][:, 0:SEQ])
                    dve.tensor_copy(dt[0:PG - P, s + 1, :], bank[6][0:PG - P, SEQ:2 * SEQ]).then_inc(S["free6"], 1)
                elif kind == "pool_mix":
                    dve.wait_ge(S["hi7"], st["hi7"])
                    for i, (c0, c1, rows, ch) in enumerate(pool_pieces(st["gi"])):
                        gc = GAIN_ROWS["pool"][0] + ch
                        ins = dve.scalar_tensor_tensor(at_lo[rows, 8 + ch, :], bank[7][rows, i * SEQ:(i + 1) * SEQ],
                                                       gt[rows, gc:gc + 1], at_hi[rows, 8 + ch, :].bitcast(F32),
                                                       ALU.mult, ALU.subtract)
                    ins.then_inc(S["free7"], 1)
                elif kind == "softmax":
                    st = st["head"]
                    kd, buf, s = st["type"], scores_buf(st), (st["a"] - 1) % SCORE_SLOTS
                    dve.wait_ge(S[f"full{st['bank']}"], st["full"])
                    if st["a"] > SCORE_SLOTS:
                        dve.wait_ge(S["t_full"], pl.prob_batch[st["a"] - SCORE_SLOTS])
                    if kd == "mem":
                        ins = dve.tensor_copy(buf[:, 0:512], bank[st["bank"]][:, 0:512])
                    elif kd == "swa":
                        dve.wait_ge(S["swa_in"], 16)
                        slope = 2.0 ** (-8.0 * (st["h"] + 1) / SWA_HEADS)
                        ins = dve.scalar_tensor_tensor(buf[:, 0:384], dist[:], -slope * DH ** 0.5, bank[st["bank"]][:, 0:384],
                                                       ALU.mult, ALU.add)
                    else:
                        dve.wait_ge(S["bias_in"], 16)
                        for t, c0, m in segments(kd):
                            ins = dve.scalar_tensor_tensor(buf[:, c0:c0 + m], bank[st["bank"]][:, c0:c0 + m], P ** -0.5,
                                                           ebias[:, st["h"], m - 1::-1], ALU.mult, ALU.add)
                    ins.then_inc(S[f"free{st['bank']}"], 1)
                    dve.wait_ge(S[f"free{st['bank']}"], st["use"])
                    for i, (t, c0, m) in enumerate(segments(kd)):
                        ins = dve.tensor_reduce(col(AM + 2 * s + i), buf[:, c0:c0 + m], AX_X, ALU.max)
                    link(ins)
                    scale = 1.0 if kd == "moba" else DH ** -0.5
                    if kd == "swa":
                        dve.wait_ge(S["sink_in"], 16)
                        link(dve.tensor_scalar(col(AM + 2 * s, 2), col(AM + 2 * s, 2), scale, sink[:, st["h"]:st["h"] + 1],
                                               ALU.mult, ALU.max))
                        scale = 1.0
                    dve.tensor_scalar(col(AN + 2 * s, 2), col(AM + 2 * s, 2), -scale, None, ALU.mult
                                      ).then_inc(S["bias_neg"], 1)
                elif kind == "normalise":
                    hd = st["head"]
                    buf, s = scores_buf(hd), (hd["a"] - 1) % SCORE_SLOTS
                    dve.wait_ge(S["probs_raw"], hd["a"])
                    if hd["type"] == "swa":
                        link(dve.tensor_tensor(col(AL + 2 * s, 2), col(AL + 2 * s, 2), col(AE + 2 * s, 2), ALU.add))
                    link(dve.reciprocal(col(AR + 2 * s, 2), col(AL + 2 * s, 2)))
                    for i, (t, c0, m) in enumerate(segments(hd["type"])):
                        ins = dve.tensor_scalar(buf[:, c0:c0 + m], buf[:, c0:c0 + m], col(AR + 2 * s + i), None, ALU.mult)
                    ins.then_inc(S["probs_ready"], 1)
                elif kind == "bias_rows":
                    dve.wait_ge(S["full6"], st["full6"])
                    dve.tensor_copy(rrow[0:H2, :], bank[6][0:H2, 0:384]).then_inc(S["free6"], 1)
                elif kind == "level":
                    l = st["l"]
                    n_heads = 4 if 1 <= l <= len(LEVELS) else 2
                    pair = slice(n_heads * st["j"], n_heads * (st["j"] + 1))
                    dve.wait_ge(S[f"full{st['bank']}"], st["full"])
                    if l == 0:
                        dve.wait_ge(S["block2_in"], 48)
                        attn = att[:, pair].rearrange("p h t n -> p (h t) n")
                        product = bank[st["bank"]][:].rearrange("p (b n) -> p b n", n=P)
                        link(dve.tensor_tensor(attn, product, ident[:].unsqueeze(1).to_broadcast([P, 4, P]), ALU.mult))
                        ins = dve.tensor_tensor(q2[:, pair], q2[:, pair], f2[:, pair], ALU.mult)
                    elif l <= len(LEVELS):
                        half = LEVELS[l - 1]
                        nb = SEQ // half
                        part = [P, 2 * n_heads, P // (2 * half), half]
                        attn = att[:, pair].rearrange("p h t (b two n) -> p (h t) b two n", two=2, n=half)[:, :, :, 1, :]
                        mask = lmask[:, l - 1].bitcast(I32).rearrange("p (b n) -> p b n", n=half).unsqueeze(1)
                        tick(dve.copy_predicated(attn, mask.to_broadcast(part),
                                                 bank[st["bank"]][:].rearrange("p (g b n) -> p g b n", g=part[1], n=half)))
                        cur, nxt = (f2, f2b) if l % 2 else (f2b, f2)
                        f_ = cur[:, pair].rearrange("p h n -> p (h n)")[:, 0:nb * n_heads].rearrange("p (b two) -> p b two", two=2)
                        q_ = q2[:, pair].rearrange("p h (b two n) -> p (h b) two n", two=2, n=half)
                        k_ = k2[:, pair].rearrange("p h (b two n) -> p (h b) two n", two=2, n=half)
                        dve.wait_ge(S["dve_chain"], chain[0])
                        dve.tensor_tensor(q_[:, :, 1, :], q_[:, :, 1, :], f_[:, :, 0:1].to_broadcast([P, nb * n_heads // 2, half]), ALU.mult)
                        dve.tensor_tensor(k_[:, :, 0, :], k_[:, :, 0, :], f_[:, :, 1:2].to_broadcast([P, nb * n_heads // 2, half]), ALU.mult)
                        ins = dve.tensor_tensor(nxt[:, pair].rearrange("p h n -> p (h n)")[:, 0:nb * n_heads // 2], f_[:, :, 0], f_[:, :, 1],
                                                ALU.mult)
                    else:
                        ins = dve.tensor_copy(attx[:, pair].rearrange("p h n -> p (h n)"), bank[st["bank"]][:, 0:2 * P])
                    ins.then_inc(S[f"free{st['bank']}"], 1)
                    dve.wait_ge(S[f"free{st['bank']}"], st["use"])
                elif kind == "hg_out":
                    dve.wait_ge(S[f"full{st['bank']}"], st["full"])
                    dve.tensor_copy(oh[:, st["t"], st["q"] * NCOL:(st["q"] + 1) * NCOL], bank[st["bank"]][:]
                                    ).then_inc(S[f"free{st['bank']}"], 1)


def shape_constants():
    p, c = np.arange(P)[:, None], np.arange(384)[None, :]
    pool = np.zeros((P, len(WINDOWS), 384), np.float32)
    s, t = np.arange(SEQ)[:, None], np.arange(SEQ)[None, :]
    for i, w in enumerate(WINDOWS):
        m = ((t - s >= 0) & (t - s < w)) / np.minimum(t + 1, w) - (t == s)
        pool[:, i, 0:SEQ] = m[0:P]
        pool[:, i, SEQ:] = m[P:, P:]
    d = np.where(c < P, p - c, p + P - (c - P))
    dist = np.where((d >= 0) & (d < P), d, 1.0e30).astype(np.float32)
    n = np.arange(384) - (P - 1)
    nf = np.maximum(n, 1).astype(np.float32)
    large = 16 + (np.log(nf / 16).astype(np.float32) / np.float32(np.log(128 / 16)) * np.float32(16)).astype(np.int32)
    bucket = np.where(n < 16, n, np.minimum(large, BUCKETS - 1))
    hot = np.zeros((BUCKETS + 1, 384), np.float32)
    for j in range(384):
        hot[bucket[j] if n[j] >= 0 else BUCKETS, j] = 1.0
    levels = np.zeros((P, len(LEVELS), P // 2), np.float32)
    q = np.arange(P // 2)[None, :]
    for i, b in enumerate(LEVELS):
        levels[:, i, :] = (p // (2 * b) == q // b) & (p % (2 * b) < b)
    return {"ident": np.eye(P, dtype=np.float32), "poolp": pool, "dist": dist, "hot": hot, "lmask": levels}


def gain_rows(inputs):
    i = {k: np.asarray(v) for k, v in inputs.items()}
    rows = [i["norm_mix"], i["kv_norm"], i["mem_norm"], i["norm_mlp"], i["attn_norm_g_2"], i["ffn_norm_g_2"],
            i["hg_lb_gamma_2"], i["pool_scale"], i["hg_out_norm_g_2"], i["q_norm_g_2"], i["k_norm_g_2"]]
    for v in (i["k_norm"], i["q_norm"], i["mem_q_norm"][0], i["mem_q_norm"][1], i["mem_k_norm"][0], i["mem_k_norm"][1]):
        rows += [v, v]
    return np.concatenate([r.reshape(-1) for r in rows]).reshape(N_GAINS, P)


INPUTS = ["x", "mem", "w_in", "pool_w", "w_kv", "sinks", "w_mem_kv", "w_out", "w_up", "w_down", "w_in_2",
          "rel_bias_table_2", "w_branch_hg_2", "w_branch_attn_2", "w_out_2", "w_ffn_gate_2", "w_ffn_up_2",
          "w_ffn_down_2"]


def kernel(**inputs):
    import concourse.bacc as bacc
    from concourse.bass_utils import run_bass_kernel_spmd

    nc = bacc.Bacc("TRN2", target_bir_lowering=False, num_devices=1)
    arrays, aps = {}, {}
    for name, v in [*((n, inputs[n]) for n in INPUTS), ("gains", gain_rows(inputs)), *shape_constants().items()]:
        v = np.ascontiguousarray(v)
        arrays[f"in_{name}"] = v
        aps[name] = nc.dram_tensor(f"in_{name}", v.shape, mybir.dt.from_np(v.dtype), kind="ExternalInput").ap()
    out = nc.dram_tensor("out_0", (1, SEQ, D), F32, kind="ExternalOutput").ap()
    scratch = nc.dram_tensor("bias_scratch", (H2, 384), F32, kind="Internal").ap()
    two_blocks_kernel(nc, aps, out, scratch)
    return run_bass_kernel_spmd(nc, [arrays], core_ids=[0]).results[0]["out_0"]
```
